# Optimizing a Trainium2 kernel written in Bass

```python
import jax, jax.numpy as jnp
from jax import lax
import numpy as np

D_MODEL = 1024
BATCH = 1
SEQ = 512
DEPTH = 1
DEC_BATCH = 8
DEC_SEQ = 1
PAST_LEN = 1024
PAGE_SIZE = 128

MIX_WIDTH = D_MODEL
CONV_CH = MIX_WIDTH // 2
CONV_K = 31
HEAD_DIM = 64
N_HEADS = (MIX_WIDTH - CONV_CH) // HEAD_DIM
N_KV = 2
GQA_R = N_HEADS // N_KV
ROT_DIM = HEAD_DIM // 4
ROPE_THETA = 500000.0
CMP_LEN = 32
CMP_STRIDE = 16
CMP_HIDDEN = 2 * HEAD_DIM
SEL_BLOCK = 64
N_SEL = 16
WINDOW = 512
Q_BLOCK = 64
D_FF = 4 * D_MODEL
N_IN = 2 * CONV_CH + N_HEADS * HEAD_DIM + 6 * N_KV * HEAD_DIM + 3 * N_HEADS
EPS = 1e-6
NEG = -1e30

kernel_name = 'hymba_conformer_nsa_decode_step'

def rms_norm(x, g):
    xf = x.astype(jnp.float32)
    y = xf * lax.rsqrt(jnp.mean(xf * xf, -1, keepdims=True) + EPS)
    return (y * g.astype(jnp.float32)).astype(x.dtype)

def layer_norm(x, g, b):
    xf = x.astype(jnp.float32)
    xc = xf - jnp.mean(xf, -1, keepdims=True)
    y = xc * lax.rsqrt(jnp.mean(xc * xc, -1, keepdims=True) + EPS)
    return (y * g.astype(jnp.float32) + b.astype(jnp.float32)).astype(x.dtype)

def rope(x, pos):
    half = ROT_DIM // 2
    inv = jnp.power(jnp.float32(ROPE_THETA), -jnp.arange(half, dtype=jnp.float32) * 2.0 / ROT_DIM)
    ang = pos.astype(jnp.float32)[:, None] * inv[None, :]
    cos = jnp.cos(ang)[:, None, :]
    sin = jnp.sin(ang)[:, None, :]
    xf = x[..., :ROT_DIM].astype(jnp.float32)
    x1, x2 = xf[..., :half], xf[..., half:]
    rot = jnp.concatenate([x1 * cos - x2 * sin, x2 * cos + x1 * sin], -1).astype(x.dtype)
    return jnp.concatenate([rot, x[..., ROT_DIM:]], -1)

def masked_softmax(s, mask):
    s = jnp.where(mask, s.astype(jnp.float32), NEG)
    e = jnp.exp(s - jnp.max(s, -1, keepdims=True)) * mask
    return e / jnp.maximum(jnp.sum(e, -1, keepdims=True), 1e-30)

def compress(rows, w1, b1, w2, pe):
    B, T = rows.shape[:2]
    nch = T // CMP_STRIDE
    ch = rows[:, :nch * CMP_STRIDE].reshape(B, nch, CMP_STRIDE, N_KV, HEAD_DIM)
    first = jnp.einsum('bnjgd,jdh->bngh', ch, w1[:CMP_STRIDE])
    second = jnp.einsum('bnjgd,jdh->bngh', ch, w1[CMP_STRIDE:])
    bias = b1 + jnp.einsum('jd,jdh->h', pe, w1)
    h = jax.nn.gelu(first[:, :-1] + second[:, 1:] + bias)
    return jnp.einsum('bngh,hd->bngd', h, w2)

def overlap_matrix(n_cmp, n_blk):
    i = np.arange(n_cmp)[:, None]
    j = np.arange(n_blk)[None, :]
    lo = np.maximum(i * CMP_STRIDE, j * SEL_BLOCK)
    hi = np.minimum(i * CMP_STRIDE + CMP_LEN, (j + 1) * SEL_BLOCK)
    return jnp.asarray((np.maximum(hi - lo, 0) // CMP_STRIDE).astype(np.float32))

def cmp_and_select(q, q_pos, kc, vc, n_blk):
    n_cmp = kc.shape[1]
    s = jnp.einsum('btgrd,bngd->btgrn', q, kc).astype(jnp.float32) * (HEAD_DIM ** -0.5)
    c_end = jnp.arange(n_cmp) * CMP_STRIDE + (CMP_LEN - 1)
    vis = c_end[None, :] <= q_pos[:, None]
    p = masked_softmax(s, vis[None, :, None, None, :])
    o_c = jnp.einsum('btgrn,bngd->btgrd', p, vc.astype(jnp.float32))
    imp = jnp.einsum('btgn,nj->btgj', p.sum(3), overlap_matrix(n_cmp, n_blk))
    blk = jnp.arange(n_blk)[None, :]
    cur = (q_pos // SEL_BLOCK)[:, None]
    future = (blk > cur)[None, :, None, :]
    forced = ((blk == 0) | (blk == cur) | (blk == cur - 1))[None, :, None, :]
    score = jnp.where(future, -jnp.inf, jnp.where(forced, jnp.inf, imp))
    vals, idx = lax.top_k(score, min(N_SEL, n_blk))
    return o_c, idx, vals > -jnp.inf

def sel_branch(q, q_pos, ks, vs, idx, valid):
    B, Tq, G, n = idx.shape
    s = jnp.einsum('btgrd,btgnkd->btgrnk', q, ks).astype(jnp.float32) * (HEAD_DIM ** -0.5)
    kpos = idx[..., None] * SEL_BLOCK + jnp.arange(SEL_BLOCK)
    ok = (kpos <= q_pos[None, :, None, None, None]) & valid[..., None]
    p = masked_softmax(s.reshape(B, Tq, G, GQA_R, n * SEL_BLOCK), ok.reshape(B, Tq, G, 1, n * SEL_BLOCK))
    return jnp.einsum('btgrm,btgmd->btgrd', p, vs.reshape(B, Tq, G, n * SEL_BLOCK, HEAD_DIM).astype(jnp.float32))

def win_branch(q, q_pos, kw, vw, k_pos):
    s = jnp.einsum('btgrd,blgd->btgrl', q, kw).astype(jnp.float32) * (HEAD_DIM ** -0.5)
    kp = k_pos[None, :]
    qp = q_pos[:, None]
    ok = (kp <= qp) & (kp >= qp - WINDOW) & (kp >= 0)
    p = masked_softmax(s, ok[None, :, None, None, :])
    return jnp.einsum('btgrl,blgd->btgrd', p, vw.astype(jnp.float32))

def gate_combine(g, o_c, o_s, o_w):
    return g[:, :, 0, ..., None] * o_c + g[:, :, 1, ..., None] * o_s + g[:, :, 2, ..., None] * o_w

def nsa_prompt(q, k_cmp, v_cmp, k_sel, v_sel, k_win, v_win, gates, cmp_k, cmp_v):
    B, T = q.shape[:2]
    kc = compress(k_cmp, *cmp_k)
    vc = compress(v_cmp, *cmp_v)
    n_blk = T // SEL_BLOCK
    ks_b = k_sel.reshape(B, n_blk, SEL_BLOCK, N_KV, HEAD_DIM)
    vs_b = v_sel.reshape(B, n_blk, SEL_BLOCK, N_KV, HEAD_DIM)
    pad = ((0, 0), (WINDOW, 0), (0, 0), (0, 0))
    kw_pad = jnp.pad(k_win, pad)
    vw_pad = jnp.pad(v_win, pad)
    bidx = jnp.arange(B)[:, None, None, None]
    gidx = jnp.arange(N_KV)[None, None, :, None]

    def one_block(start):
        q_pos = start + jnp.arange(Q_BLOCK)
        q_c = lax.dynamic_slice_in_dim(q, start, Q_BLOCK, 1)
        g_c = lax.dynamic_slice_in_dim(gates, start, Q_BLOCK, 1)
        o_c, idx, valid = cmp_and_select(q_c, q_pos, kc, vc, n_blk)
        o_s = sel_branch(q_c, q_pos, ks_b[bidx, idx, :, gidx], vs_b[bidx, idx, :, gidx], idx, valid)
        kw = lax.dynamic_slice_in_dim(kw_pad, start, WINDOW + Q_BLOCK, 1)
        vw = lax.dynamic_slice_in_dim(vw_pad, start, WINDOW + Q_BLOCK, 1)
        k_pos = start - WINDOW + jnp.arange(WINDOW + Q_BLOCK)
        o_w = win_branch(q_c, q_pos, kw, vw, k_pos)
        return gate_combine(g_c, o_c, o_s, o_w).astype(q.dtype)

    out = lax.map(one_block, jnp.arange(T // Q_BLOCK) * Q_BLOCK)
    return jnp.moveaxis(out, 0, 1).reshape(B, T, N_HEADS * HEAD_DIM)

def nsa_sample(q, q_pos, k_cmp, v_cmp, k_sel, v_sel, k_win, v_win, gates, pool_k_cmp, pool_v_cmp,
               pool_k_sel, pool_v_sel, buf_k_win, buf_v_win, page_table, cmp_k, cmp_v):
    B, Tq = q.shape[:2]
    past = page_table.shape[1] * PAGE_SIZE

    def past_rows(pool):
        return pool[page_table].reshape(B, past, N_KV, HEAD_DIM)

    kc = compress(jnp.concatenate([past_rows(pool_k_cmp), k_cmp], 1), *cmp_k)
    vc = compress(jnp.concatenate([past_rows(pool_v_cmp), v_cmp], 1), *cmp_v)
    n_blk = -(-(past + Tq) // SEL_BLOCK)
    nb_past = past // SEL_BLOCK
    nb_new = n_blk - nb_past
    o_c, idx, valid = cmp_and_select(q, q_pos, kc, vc, n_blk)
    sub = PAGE_SIZE // SEL_BLOCK
    bidx = jnp.arange(B)[:, None, None, None]
    gidx = jnp.arange(N_KV)[None, None, :, None]
    jp = jnp.minimum(idx, nb_past - 1)
    page = page_table[bidx, jp // sub]
    off = jp % sub
    jn = jnp.clip(idx - nb_past, 0, nb_new - 1)
    from_past = (idx < nb_past)[..., None, None]

    def gather(pool, new):
        pool_b = pool.reshape(pool.shape[0], sub, SEL_BLOCK, N_KV, HEAD_DIM)
        new_b = jnp.pad(new, ((0, 0), (0, nb_new * SEL_BLOCK - Tq), (0, 0), (0, 0)))
        new_b = new_b.reshape(B, nb_new, SEL_BLOCK, N_KV, HEAD_DIM)
        return jnp.where(from_past, pool_b[page, off, :, gidx], new_b[bidx, jn, :, gidx])

    o_s = sel_branch(q, q_pos, gather(pool_k_sel, k_sel), gather(pool_v_sel, v_sel), idx, valid)
    wb = buf_k_win.shape[1]
    kw = jnp.concatenate([buf_k_win, k_win], 1)
    vw = jnp.concatenate([buf_v_win, v_win], 1)
    k_pos = past - wb + jnp.arange(wb + Tq)
    o_w = win_branch(q, q_pos, kw, vw, k_pos)
    o = gate_combine(gates, o_c, o_s, o_w).astype(q.dtype).reshape(B, Tq, N_HEADS * HEAD_DIM)
    return o, kw[:, -wb:], vw[:, -wb:]

def mixer_in(x, pos, g_pre, w_in):
    B, T, _ = x.shape
    z = rms_norm(x, g_pre) @ w_in
    c0 = 2 * CONV_CH
    c1 = c0 + N_HEADS * HEAD_DIM
    c2 = c1 + 6 * N_KV * HEAD_DIM
    u = z[..., :CONV_CH] * jax.nn.sigmoid(z[..., CONV_CH:c0])
    q = rope(z[..., c0:c1].reshape(B, T, N_HEADS, HEAD_DIM), pos).reshape(B, T, N_KV, GQA_R, HEAD_DIM)
    kv = z[..., c1:c2].reshape(B, T, 6, N_KV, HEAD_DIM)
    gates = jax.nn.sigmoid(z[..., c2:].astype(jnp.float32)).reshape(B, T, 3, N_KV, GQA_R)
    return (u, q, rope(kv[:, :, 0], pos), kv[:, :, 1], rope(kv[:, :, 2], pos), kv[:, :, 3],
            rope(kv[:, :, 4], pos), kv[:, :, 5], gates)

def dwconv(u_ext, w, b):
    y = lax.conv_general_dilated(u_ext, w[:, None, :].astype(u_ext.dtype), window_strides=(1,), padding='VALID',
                                 dimension_numbers=('NWC', 'WIO', 'NWC'), feature_group_count=CONV_CH)
    return y + b

def conv_tail(y, ln_g, ln_b):
    return jax.nn.silu(layer_norm(y, ln_g, ln_b))

def layer_out(x, conv_y, o_nsa, w_out, g_post, g_pre2, w_up, w_down, g_post2):
    mix = jnp.concatenate([conv_y, o_nsa.astype(conv_y.dtype)], -1) @ w_out
    h = x + rms_norm(mix, g_post)
    f = jnp.square(jax.nn.relu(rms_norm(h, g_pre2) @ w_up)) @ w_down
    return h + rms_norm(f, g_post2)

def setup_inputs(seed: int = 0) -> dict:
    key = jax.random.key(seed)
    ks = jax.random.split(key, 32)
    n_pages = PAST_LEN // PAGE_SIZE
    n_pool = (DEC_BATCH * n_pages * 5) // 4
    wb = min(WINDOW, PAST_LEN)

    def nrm(k, shape, s):
        return jax.random.normal(k, shape, jnp.float32) * s

    def gain(k, n):
        return 1.0 + nrm(k, (DEPTH, n), 0.05)

    pool = (DEPTH, n_pool, PAGE_SIZE, N_KV, HEAD_DIM)
    win = (DEPTH, DEC_BATCH, wb, N_KV, HEAD_DIM)
    page_table = jax.random.permutation(ks[9], n_pool)[:DEC_BATCH * n_pages]
    page_table = page_table.reshape(DEC_BATCH, n_pages).astype(jnp.int32)
    return {
        'x_prompt': nrm(ks[0], (BATCH, SEQ, D_MODEL), 1.0),
        'x_sample': nrm(ks[1], (DEC_BATCH, DEC_SEQ, D_MODEL), 1.0),
        'cache_k_cmp': nrm(ks[2], pool, 1.0),
        'cache_v_cmp': nrm(ks[3], pool, 1.0),
        'cache_k_sel': nrm(ks[4], pool, 1.0),
        'cache_v_sel': nrm(ks[5], pool, 1.0),
        'cache_k_win': nrm(ks[6], win, 1.0),
        'cache_v_win': nrm(ks[7], win, 1.0),
        'cache_conv': nrm(ks[8], (DEPTH, DEC_BATCH, CONV_K - 1, CONV_CH), 0.5),
        'page_table': page_table,
        'g_pre_mix': gain(ks[10], D_MODEL),
        'w_in': nrm(ks[11], (DEPTH, D_MODEL, N_IN), D_MODEL ** -0.5),
        'conv_w': nrm(ks[12], (DEPTH, CONV_K, CONV_CH), CONV_K ** -0.5),
        'conv_b': nrm(ks[13], (DEPTH, CONV_CH), 0.01),
        'conv_ln_g': gain(ks[14], CONV_CH),
        'conv_ln_b': nrm(ks[15], (DEPTH, CONV_CH), 0.01),
        'cmp_k_w1': nrm(ks[16], (DEPTH, CMP_LEN, HEAD_DIM, CMP_HIDDEN), (CMP_LEN * HEAD_DIM) ** -0.5),
        'cmp_k_b1': nrm(ks[17], (DEPTH, CMP_HIDDEN), 0.01),
        'cmp_k_w2': nrm(ks[18], (DEPTH, CMP_HIDDEN, HEAD_DIM), CMP_HIDDEN ** -0.5),
        'cmp_k_pe': nrm(ks[19], (DEPTH, CMP_LEN, HEAD_DIM), 0.1),
        'cmp_v_w1': nrm(ks[20], (DEPTH, CMP_LEN, HEAD_DIM, CMP_HIDDEN), (CMP_LEN * HEAD_DIM) ** -0.5),
        'cmp_v_b1': nrm(ks[21], (DEPTH, CMP_HIDDEN), 0.01),
        'cmp_v_w2': nrm(ks[22], (DEPTH, CMP_HIDDEN, HEAD_DIM), CMP_HIDDEN ** -0.5),
        'cmp_v_pe': nrm(ks[23], (DEPTH, CMP_LEN, HEAD_DIM), 0.1),
        'w_out': nrm(ks[24], (DEPTH, MIX_WIDTH, D_MODEL), MIX_WIDTH ** -0.5),
        'g_post_mix': gain(ks[25], D_MODEL),
        'g_pre_ffn': gain(ks[26], D_MODEL),
        'w_up': nrm(ks[27], (DEPTH, D_MODEL, D_FF), D_MODEL ** -0.5),
        'w_down': nrm(ks[28], (DEPTH, D_FF, D_MODEL), D_FF ** -0.5),
        'g_post_ffn': gain(ks[29], D_MODEL),
    }

def reference(x_prompt, x_sample, cache_k_cmp, cache_v_cmp, cache_k_sel, cache_v_sel, cache_k_win, cache_v_win,
              cache_conv, page_table, g_pre_mix, w_in, conv_w, conv_b, conv_ln_g, conv_ln_b,
              cmp_k_w1, cmp_k_b1, cmp_k_w2, cmp_k_pe, cmp_v_w1, cmp_v_b1, cmp_v_w2, cmp_v_pe,
              w_out, g_post_mix, g_pre_ffn, w_up, w_down, g_post_ffn):
    pos_p = jnp.arange(x_prompt.shape[1])
    pos_s = page_table.shape[1] * PAGE_SIZE + jnp.arange(x_sample.shape[1])
    hp, hs = x_prompt, x_sample
    st = [[] for _ in range(14)]
    for l in range(DEPTH):
        cmp_k = (cmp_k_w1[l], cmp_k_b1[l], cmp_k_w2[l], cmp_k_pe[l])
        cmp_v = (cmp_v_w1[l], cmp_v_b1[l], cmp_v_w2[l], cmp_v_pe[l])
        out_w = (w_out[l], g_post_mix[l], g_pre_ffn[l], w_up[l], w_down[l], g_post_ffn[l])
        u, q, kc, vc, ks, vs, kw, vw, gt = mixer_in(hp, pos_p, g_pre_mix[l], w_in[l])
        cy = conv_tail(dwconv(jnp.pad(u, ((0, 0), (CONV_K - 1, 0), (0, 0))), conv_w[l], conv_b[l]),
                       conv_ln_g[l], conv_ln_b[l])
        o = nsa_prompt(q, kc, vc, ks, vs, kw, vw, gt, cmp_k, cmp_v)
        wb = min(WINDOW, hp.shape[1])
        for i, a in enumerate((kc, vc, ks, vs, kw[:, -wb:], vw[:, -wb:], u[:, -(CONV_K - 1):])):
            st[i].append(a)
        hp = layer_out(hp, cy, o, *out_w)
        u, q, kc, vc, ks, vs, kw, vw, gt = mixer_in(hs, pos_s, g_pre_mix[l], w_in[l])
        u_ext = jnp.concatenate([cache_conv[l], u], 1)
        cy = conv_tail(dwconv(u_ext, conv_w[l], conv_b[l]), conv_ln_g[l], conv_ln_b[l])
        o, kw_buf, vw_buf = nsa_sample(q, pos_s, kc, vc, ks, vs, kw, vw, gt, cache_k_cmp[l], cache_v_cmp[l],
                                       cache_k_sel[l], cache_v_sel[l], cache_k_win[l], cache_v_win[l],
                                       page_table, cmp_k, cmp_v)
        for i, a in enumerate((kc, vc, ks, vs, kw_buf, vw_buf, u_ext[:, -(CONV_K - 1):])):
            st[7 + i].append(a)
        hs = layer_out(hs, cy, o, *out_w)
    s = [jnp.stack(a) for a in st]
    return (hp, hs, s[0], s[1], s[2], s[3], s[4], s[5], s[6], s[7], s[8], s[9], s[10], s[11], s[12], s[13])


_drawn_inputs = setup_inputs


def setup_inputs(seed=0):
    import zlib

    import numpy as np

    out = dict(_drawn_inputs(seed))
    spreads = {}
    factors = {'conv_b': 3.956, 'conv_ln_b': 7.813, 'cmp_k_b1': 64.0, 'cmp_k_pe': 8.0, 'cmp_v_b1': 8.0}
    for name, (base, spread) in spreads.items():
        noise = np.random.default_rng([zlib.crc32(name.encode()), seed]).standard_normal(out[name].shape)
        drawn = base * np.exp(spread * noise) if base else spread * noise
        out[name] = __import__('jax').numpy.asarray(drawn.astype(out[name].dtype))
    for name, factor in factors.items():
        out[name] = (out[name] * factor).astype(out[name].dtype)
    return out
```

```python
from contextlib import ExitStack

import numpy as np

import concourse.bass as bass
from concourse import mybir

F32 = mybir.dt.float32
F32R = mybir.dt.float32r
BF16 = mybir.dt.bfloat16
I32 = mybir.dt.int32
U32 = mybir.dt.uint32
ALU = mybir.AluOpType
ACT = mybir.ActivationFunctionType
AX = mybir.AxisListType

P = 128
D = 1024
KT = D // P
TP = 512
NS = 8
T = TP + NS
HT = T // 2
QT = TP // P
CH = 512
CT = CH // P
TAPS = 31
HD = 64
NH = 8
G = 2
R = NH // G
PAST = 1024
PAGE = 128
NPG = PAST // PAGE
WIN = 512
STRIDE = 16
NCH_S = PAST // STRIDE
NCH_P = TP // STRIDE
NBLK = PAST // 64
EPS = 1e-6
NEG = -1e30

B_KV, B_Q, B_CK, B_CV, B_OUT, B_FFN = 4, 7, 9, 10, 11, 15
N_BLOCKS = B_FFN + 32
N_Z = 18
BW = KT * 2 * P

V_GPRE, V_CB, V_LG, V_LB, V_GPOST, V_GPRE2, V_GPOST2 = 0, 8, 12, 16, 20, 28, 36
V_B1, V_CW, V_PE = 44, 46, 46 + CT * TAPS
N_VEC = V_PE + 32
C_ID, C_PERM, C_COS, C_SIN = 0, 128, 256, 256 + T
C_MASK = C_SIN + T
C_VIS = C_MASK + 128
C_VISB = C_VIS + 128
C_HM = C_VISB + 128
C_BM = C_HM + 24
C_RS = C_BM + 8
C_EB = C_RS + 64
C_OV = C_EB + 64
C_J = C_OV + 16
C_CI = C_J + 14
C_PAR = C_CI + 2
N_C = C_PAR + 2


ROPE = (1, 0, 1, 0, 1, 0, 1, 1, 1, 1)
TOKSLOT = {0: 0, 1: 1, 2: 2, 4: 3}
UNITS = [(r, g, br, i) for r in range(R) for g in range(G) for br in range(2) for i in range(QT)]
N_UNITS = len(UNITS)


def FILL(u):
    return u // 4 * 17 + u % 4 * 4


def W2E(u):
    return u + 1 + (2 if u >= 3 else 0) + (4 if u >= 7 else 0)


DV_CMAX, DV_WMAX, DV_PN, DV_SMAX, DV_P = 1, 8, 12, 23, 33
DP_PN, DP_IM1, DP_IM2, DP_PT, DP_OT = 1, 2, 3, 4, 5
TV_SUM, TV_XC = 3, 4
TV_NRM = TV_XC + CT + 1


def hymba_step(nc, A):
    ctx = ExitStack()
    with ctx:
        def psum(name):
            return ctx.enter_context(nc.psum_tensor(name, [P, 2, 512], F32))

        def sem(name):
            return ctx.enter_context(nc.semaphore(name))

        def region(*groups):
            out, most = {}, 0
            for group in groups:
                size = 0
                with ExitStack() as scope:
                    for name, shape, dt in group:
                        out[name] = scope.enter_context(nc.sbuf_tensor(name, shape, dt))
                        n = int(np.prod(shape[1:])) * (2 if dt == BF16 else 4)
                        size += -(-n // 32) * 32
                most = max(most, size)
            ctx.enter_context(nc.sbuf_tensor("space_of_" + groups[0][0][0], [P, most // 4], F32))
            return out

        def sb(name, shape, dt=F32):
            return ctx.enter_context(nc.sbuf_tensor(name, shape, dt))

        xT = sb("xT", [P, KT, T])
        wraw = [sb(f"wraw{i}", [P, BW]) for i in range(2)]
        wH = [sb(f"wH{i}", [P, BW], F32R) for i in range(2)]
        wL = [sb(f"wL{i}", [P, BW], F32R) for i in range(2)]
        vec = sb("vec", [P, N_VEC])
        ones = sb("ones", [P, 2, P])
        epsc = sb("epsc", [P, 1])
        zero = sb("zero", [P, 1])
        ident = sb("ident", [P, P])
        sq = [sb(f"sq{i}", [P, T]) for i in range(2)]
        rb = sb("rb", [P, T])
        a = region(
            [("actH", [P, KT, T], F32R), ("actL", [P, KT, T], F32R)],
            [("rawc0", [P, 2048], F32), ("rawc1", [P, 2048], F32),
             ("rks_", [P, 2, 1024], F32), ("rkw0", [P, 512], F32), ("rkw1", [P, 512], F32),
             ("kcS", [P, 512], F32), ("vcS", [P, 4, P], F32)],
        )
        actH, actL = a["actH"], a["actL"]
        rawc, rkw = [a["rawc0"], a["rawc1"]], [a["rkw0"], a["rkw1"]]
        rks = [a["rks_"][:, i, :] for i in range(2)]
        pchunk = a["rks_"][0:NCH_P, :, :].rearrange("p a n -> p (a n)")
        kcS, vcS = a["kcS"], a["vcS"]
        base_pre = [
            ("cst", [P, N_C - C_PERM], F32), ("identb", [P, P], BF16), ("maskb", [P, P], BF16),
            ("uP", [P, CT, TAPS - 1 + TP], F32), ("uS", [P, CT, NS, TAPS], F32), ("yC", [P, CT, T], F32),
            ("qT", [P, R, T], F32), ("kz", [P, 2, G, TP], F32), ("knew", [P, 2, NS], F32),
            ("vtok", [P, 2, QT + 1, P], F32), ("gtok", [P, QT + 1, 24], F32), ("w2", [P, 2, HD], F32),
            ("biasc", [P, 2], F32), ("kcBD", [P, HD], F32), ("vcBD", [P, 2, P], F32),
            ("pt_i", [P, 12], I32), ("idx", [P, 12], U32),
        ]
        ffn = [("hH", [P, 16, T], F32R), ("hL", [P, 16, T], F32R), ("fs", [P, KT, T], F32),
               ("rl0", [P, T], F32), ("rl1", [P, T], F32), ("h20", [P, T], F32), ("h21", [P, T], F32)]
        inproj = [("sg", [P, T], F32), ("zr0", [P, T], F32), ("zr1", [P, T], F32), ("zr2", [P, T], F32),
                  ("t1", [P, T], F32), ("t2", [P, T], F32), ("kf0", [P, T], F32), ("kf1", [P, T], F32),
                  ("ktok", [P, 4, QT + 1, P], F32), ("gT", [24, T], F32),
                  ("wg", [P, KT * 24], F32), ("wgH", [P, KT * 24], F32R), ("wgL", [P, KT * 24], F32R)]
        XW = 324
        cmp_ = [("XH0", [P, KT, XW], F32R), ("XH1", [P, KT, XW], F32R),
                ("XL0", [P, KT, XW], F32R), ("XL1", [P, KT, XW], F32R),
                ("hc0", [P, 320], F32), ("hc1", [P, 320], F32)]
        attn = [("KTb0", [P, 1536], F32), ("KTb1", [P, 1536], F32), ("PT", [P, 832], F32), ("PTn", [8, 128], F32),
                ("Ss", [64, PAST + 8], F32), ("Sw", [64, WIN + 8], F32), ("Pd", [64, 2, 64], F32),
                ("Sc0", [64, 64], F32), ("pnT", [64, 64], F32), ("im1", [64, 16], F32), ("im2", [64, 16], F32),
                ("sb0", [64, 16], F32), ("tj", [64, 14], F32), ("tg", [64, 24], F32), ("gB", [64, 4], F32),
                ("nw", [64, 2, 8], F32), ("dsm", [64, 24], F32),
                ("Qc", [P, 64], F32), ("Qpad", [P, 576], F32), ("od", [8, 1024], F32),
                ("Pb0", [P, 512], F32), ("Pb1", [P, 512], F32), ("Pb2", [P, 512], F32),
                ("PTb0", [P, 512], F32), ("PTb1", [P, 512], F32),
                ("Pc0", [P, 256], F32), ("Pc1", [P, 256], F32), ("PcT", [P, 2, TP], F32),
                ("smc", [P, 4, 8], F32), ("smx", [P, 64], F32), ("sms", [P, 64], F32), ("smr", [P, 64], F32)]
        tail = [("ysm", [P, T], F32), ("ac0", [P, T], F32), ("ac1", [P, T], F32),
                ("mixT", [P, KT, T], F32)]
        out = {}
        with ExitStack() as pre:
            for name, shape, dt in base_pre:
                out[name] = pre.enter_context(nc.sbuf_tensor(name, shape, dt))
            for group in (inproj, cmp_, attn, tail):
                with ExitStack() as scope:
                    for name, shape, dt in group:
                        out[name] = scope.enter_context(nc.sbuf_tensor(name, shape, dt))
        for name, shape, dt in ffn:
            out[name] = sb(name, shape, dt)
        (cst, identb, maskb, uP, uS, yC, qT, kz, knew, vtok, gtok, w2, biasc, kcBD, vcBD, pt_i, idx) = (
            out[n] for n, _, _ in base_pre)
        (sg, zr0, zr1, zr2, t1, t2, kf0, kf1, ktok, gT, wg, wgH, wgL) = (out[n] for n, _, _ in inproj)
        zr, kf = [zr0, zr1, zr2], [kf0, kf1]
        XH, XL = [out["XH0"], out["XH1"]], [out["XL0"], out["XL1"]]
        hc = [out["hc0"], out["hc1"]]
        (KTb0, KTb1, PT, PTn, Ss, Sw, Pd, Sc0, pnT, im1, im2, sb0, tj, tg, gB, nw, dsm, Qc, Qpad, od,
         Pb0, Pb1, Pb2, PTb0, PTb1, Pc0, Pc1, PcT, smc, smx, sms, smr) = (out[n] for n, _, _ in attn)
        KTb, Pb, PTb, Pc = [KTb0, KTb1], [Pb0, Pb1, Pb2], [PTb0, PTb1], [Pc0, Pc1]
        ysm, ac0, ac1, mixT = (out[n] for n, _, _ in tail)
        ac = [ac0, ac1]
        hH, hL, fs, rl0, rl1, h20, h21 = (out[n] for n, _, _ in ffn)
        rl, h2 = [rl0, rl1], [h20, h21]

        def C(c0, n, p0=0, p1=P):
            return cst[p0:p1, c0 - C_PERM:c0 - C_PERM + n]

        PA, PB, PR, PS = psum("PA"), psum("PB"), psum("PR"), psum("PS")
        PZ = [PA, PB]

        s_vec, s_cst, s_x, s_misc, s_wg, s_pt, s_us = (sem(n) for n in (
            "vec_loaded", "const_loaded", "x_loaded", "w2_loaded", "wg_loaded", "pt_loaded", "us_loaded"))
        s_raw = [sem(f"block_loaded{i}") for i in range(2)]
        s_whi, s_split, s_wgs = sem("block_hi"), sem("block_split"), sem("wg_split")
        s_init, s_initd, s_idx = sem("pool_init"), sem("dve_init"), sem("idx_ready")
        s_grp = sem("group_done")
        s_gmm = sem("gates_done")
        s_sq, s_st, s_std, s_rinv = sem("squared"), sem("mean_fed"), sem("std_ready"), sem("rinv_ready")
        s_nt, s_nh, s_nl = sem("norm_tmp"), sem("norm_hi"), sem("norm_lo")
        s_sig, s_u, s_z = sem("sigmoid_ready"), sem("glu_ready"), sem("z_ready")
        s_rot, s_rot2, s_t1, s_rope = sem("rot_done"), sem("rot_used"), sem("cos_done"), sem("roped")
        s_tok, s_tokA, s_tokD, s_kzc = sem("tok_done"), sem("tok_evac_act"), sem("tok_evac_dve"), sem("kz_copied")
        s_gt, s_gtt, s_gtk = sem("gates_sig"), sem("gates_turned"), sem("gates_ready")
        s_out = sem("stores_done")
        s_kcd = sem("kcmp_stored")
        s_tap, s_ys = sem("conv_step"), sem("conv_sample")
        s_rc = [sem(f"cmp_raw_loaded{i}") for i in range(2)]
        s_rp = [sem(f"cmp_prompt_loaded{i}") for i in range(2)]
        s_xt, s_xh, s_xl, s_pe, s_cmm = sem("x_turned"), sem("x_hi"), sem("x_lo"), sem("pe_col"), sem("cmp_unit")
        s_bias, s_gelu, s_w2m, s_w2e = sem("cmp_bias"), sem("gelu_done"), sem("cmp_out"), sem("cmp_out_used")
        s_dec = [sem(f"dec_loaded{i}") for i in range(2)]
        s_kt, s_ktA, s_ktD, s_sc = sem("k_turned"), sem("k_evac_act"), sem("k_evac_dve"), sem("scores_done")
        s_q = sem("q_padded")
        s_dA, s_dV, s_dP = sem("dec_act"), sem("dec_dve"), sem("dec_pe")
        s_dpv = sem("dec_pv")
        s_cS, s_cX, s_cP, s_cT, s_cE = (sem(n) for n in ("pc_scores", "pc_exp", "pc_probs", "pc_turned", "pc_evac"))
        s_cV = sem("pc_dve")
        s_pei, s_pel, s_pec = sem("xh_zeroed"), sem("xl_zeroed"), sem("pe_col_lo")
        s_tokst = sem("tokens_stored")
        s_S, s_mx, s_ex, s_pn, s_T, s_ev, s_pv, s_oh, s_ol = (sem(n) for n in (
            "att_scores", "att_max", "att_exp", "att_norm", "att_turned", "att_evac", "att_pv", "att_ohi", "att_olo"))
        s_sm = sem("att_small")
        s_tv, s_ta, s_tp = sem("tail_dve"), sem("tail_act"), sem("tail_pe")
        s_evt = sem("tile_evacuated")
        s_res = sem("residual_step")
        s_h2, s_hh, s_hl = sem("h_squared"), sem("h_hi"), sem("h_lo")
        s_fz = sem("fs_zeroed")
        s_y = sem("y_ready")

        block = ctx.enter_context(nc.Block())
        NORMS = range(4)
        A_wblk = A["wblk"]

        @block.sync
        def _(sp):
            sp.dma_start(vec[:, :], A["vecs"]).then_inc(s_vec, 16)
            sp.dma_start(ident[:, :], A["consts"][:, 0:P]).then_inc(s_vec, 16)
            sp.dma_start(xT[:, :, :], A["x_fm"]).then_inc(s_x, 16)
            for b in range(2):
                sp.dma_start(wraw[b][:, :], A_wblk[b]).then_inc(s_raw[b], 16)
            sp.dma_start(cst[:, :], A["consts"][:, P:N_C]).then_inc(s_cst, 16)
            sp.dma_start(uS[:, :, :, :], A["us0"]).then_inc(s_us, 16)
            sp.dma_start(wg[:, :], A["wgate"]).then_inc(s_wg, 16)
            sp.dma_start(w2[:, :, :], A["w2"]).then_inc(s_misc, 16)
            with sp.Fori(0, (N_BLOCKS - 3) // 2) as i:
                for s in range(2):
                    sp.wait_ge(s_split, 2 * i + 1 + s)
                    sp.dma_start(wraw[s][:, :], A_wblk[bass.ds(2 * i + 2 + s, 1)].rearrange("o p n -> (o p) n"))\
                        .then_inc(s_raw[s], 16)
            sp.wait_ge(s_split, N_BLOCKS - 2)
            sp.dma_start(wraw[0][:, :], A_wblk[N_BLOCKS - 1]).then_inc(s_raw[0], 16)
            for k in range(KT):
                sp.wait_ge(s_y, k + 1)
                sp.dma_start(A["y_fm"][:, k, :], xT[:, k, :]).then_inc(s_out, 16)
            sp.wait_ge(s_out, 16 * (KT + 4))
            sp.wait_ge(s_tokst, 16 * 10)
            sp.wait_ge(s_kcd, 16 * 2)

        @block.gpsimd
        def _(pool):
            n_init = 0
            for t_, v in ((ones[:, 0, :], 1.0 / D), (ones[:, 1, :], 1.0 / CH), (epsc[:, :], EPS), (zero[:, :], 0.0),
                          (uP[:, :, 0:TAPS - 1], 0.0), (kz[:, :, :, :], 0.0), (kcBD[:, :], 0.0),
                          (vcBD[:, :, :], 0.0)):
                pool.memset(t_, v).then_inc(s_init, 1)
                n_init += 1
            assert n_init == 8
            pool.dma_start(pt_i[:, :], A["pt_rep"]).then_inc(s_pt, 16)

            pool.wait_ge(s_init, 8)

            def split(b, s, raw_count, free_sem=None, free_count=0):
                pool.wait_ge(s_raw[s], raw_count)
                if free_sem is not None:
                    pool.wait_ge(free_sem, free_count)
                pool.tensor_tensor(wH[s][:, :], wraw[s][:, :], zero[:, :].broadcast_to([P, BW]), ALU.add)\
                    .then_inc(s_whi, 1)
                pool.wait_ge(s_whi, b + 1)
                pool.tensor_tensor(wL[s][:, :], wraw[s][:, :], wH[s][:, :].bitcast(F32), ALU.subtract)\
                    .then_inc(s_split, 1)

            split(0, 0, 16)
            split(1, 1, 16)
            pool.wait_ge(s_pt, 16)
            pool.wait_ge(s_cst, 16)
            pool.tensor_scalar(idx[:, 0:4], pt_i[:, 0:4], 8.0, C(C_CI, 1), ALU.mult, ALU.add).then_inc(s_idx, 1)
            pool.tensor_scalar(idx[:, 4:12], pt_i[:, 4:12], 16.0, C(C_CI + 1, 1), ALU.mult, ALU.add)\
                .then_inc(s_idx, 1)
            with pool.Fori(1, 4) as i:
                for s in range(2):
                    split(2 * i + s, s, 16 * i + 16, s_grp, 4 * i - 2 + 2 * s)
            pool.wait_ge(s_wg, 16)
            pool.tensor_copy(wgH[:, :], wg[:, :]).then_inc(s_wgs, 1)
            pool.wait_ge(s_wgs, 1)
            pool.tensor_tensor(wgL[:, :], wg[:, :], wgH[:, :].bitcast(F32), ALU.subtract).then_inc(s_wgs, 1)
            split(8, 0, 16 * 5, s_grp, 14)
            split(9, 1, 16 * 5, s_grp, 16)
            pool.wait_ge(s_idx, 2)
            pools_c = [A["pool_kc"], A["pool_vc"]]
            pool.wait_ge(s_gmm, 1)
            for u in range(8):
                kv, pr = divmod(u, 4)
                if u >= 2:
                    pool.wait_ge(s_xt, FILL(u - 2) + 4)
                if u in (0, 4):
                    if u == 0:
                        pool.wait_ge(s_kcd, 32)
                    else:
                        pool.wait_ge(s_xt, FILL(3) + 5)
                    rows_ = A["p_rows"][kv].rearrange("(c j) n -> c j n", j=STRIDE)
                    for g in range(G):
                        pool.dma_start(pchunk[:, g * 1024:(g + 1) * 1024].rearrange("c (j d) -> c j d", j=STRIDE),
                                       rows_[:, :, g * HD:(g + 1) * HD]).then_inc(s_rp[kv], 16)
                pool.indirect_dma_start(rawc[u % 2][:, :], None, pools_c[kv],
                                        bass.IndirectOffsetOnAxis(ap=idx[:, pr:pr + 1], axis=0))\
                    .then_inc(s_rc[u % 2], 16)
                if u == 1:
                    split(10, 0, 16 * 6, s_grp, 18)
            pools_s, wins = [A["pool_ks"], A["pool_vs"]], [A["win_k"], A["win_v"]]

            def dec_load(i):
                kv, b = divmod(i, NS)
                pool.indirect_dma_start(rks[i % 2][:, :], None, pools_s[kv],
                                        bass.IndirectOffsetOnAxis(ap=idx[:, 4 + b:5 + b], axis=0))\
                    .then_inc(s_dec[i % 2], 16)
                pool.dma_start(rkw[i % 2][:, :], wins[kv][b]).then_inc(s_dec[i % 2], 16)

            pool.wait_ge(s_xt, FILL(7) + 5)
            dec_load(0)
            dec_load(1)
            split(11, 1, 16 * 6, s_cmm, 4)
            split(12, 0, 16 * 7, s_cmm, 8)
            for i in range(2, 2 * NS):
                if i < NS + 2:
                    pool.wait_ge(s_kt, 3 * (i - 1))
                else:
                    pool.wait_ge(s_dpv, i - NS - 1)
                dec_load(i)
            with pool.Fori(0, (N_BLOCKS - 13) // 2) as i:
                for s in (1, 0):
                    e = 1 - s
                    split(13 + 2 * i + e, s, 16 * (7 + i + e), s_grp, 20 + 4 * i + 2 * e)

        @block.scalar
        def _(act):
            def squares(norm, src, ready=None, first=0, step=1):
                for k in range(KT):
                    n = norm * KT + k
                    if n >= 2:
                        act.wait_ge(s_st, n - 1)
                    if ready is not None:
                        act.wait_ge(ready, first + step * k)
                    act.activation(sq[k % 2][:, :], src[:, k, :], ACT.Square).then_inc(s_sq, 1)
                act.wait_ge(s_st, KT * (norm + 1))
                act.activation(rb[:, :].rearrange("p (a b) -> p a b", a=2), PS[:, :, 0:HT], ACT.Sqrt,
                               bias=epsc[:, :]).then_inc(s_std, 1)

            def norm_hi(norm_split, ring):
                for k in range(KT):
                    n = norm_split * KT + k
                    act.wait_ge(s_nt, n + 1)
                    act.activation(actH[:, k, :], ring[k % 2][:, :], ACT.Copy).then_inc(s_nh, 1)

            act.wait_ge(s_x, 16)
            act.wait_ge(s_init, 8)
            squares(0, xT)
            norm_hi(0, [t1, t2])
            def tok_evac(c):
                act.wait_ge(s_tok, c + 1)
                dst = vtok[:, (c - 3) // 2] if c in (3, 5) else ktok[:, TOKSLOT[c]]
                act.activation(dst[:, 0:QT, :], PS[:, 0, :].rearrange("p (t d) -> p t d", t=QT), ACT.Copy)\
                    .then_inc(s_tokA, 1)

            def store_tok(c):
                act.wait_ge(s_tokA, c + 1)
                act.wait_ge(s_tokD, c + 1)
                src = vtok[:, (c - 3) // 2] if c in (3, 5) else ktok[:, TOKSLOT[c]]
                act.dma_start(A["p_rows"][c].rearrange("(t p) d -> p t d", p=P), src[:, 0:QT, :])\
                    .then_inc(s_kcd if c < 2 else s_tokst, 16)
                dst = A["s_rows"][c] if c < 4 else A["s_win"][c - 4][:, WIN - 1, :]
                act.dma_start(dst, src[0:NS, QT, :]).then_inc(s_tokst, 16)

            def kz_copies(bi, kfi):
                act.wait_ge(s_rope, kfi + 1)
                for g in range(G):
                    h = slice(g * HD, (g + 1) * HD)
                    act.activation(kz[h, bi, g, :], kf[kfi % 2][h, 0:TP], ACT.Copy).then_inc(s_kzc, 1)
                act.activation(knew[:, bi, :], kf[kfi % 2][:, TP:T], ACT.Copy).then_inc(s_kzc, 1)

            act.wait_ge(s_init, 8)
            for n in range(N_Z):
                if n < 8:
                    if n % 2 == 0:
                        act.wait_ge(s_grp, n + 1)
                        if n >= 2:
                            act.wait_ge(s_u, 3 * (n // 2))
                        act.activation(sg[:, :].rearrange("p (a b) -> p a b", a=2), PZ[0][:, :, 0:HT], ACT.Sigmoid)\
                            .then_inc(s_sig, 1)
                else:
                    z = n - 8
                    act.wait_ge(s_grp, n + 1)
                    if z >= 3:
                        if ROPE[z - 3]:
                            act.wait_ge(s_rot, sum(ROPE[:z - 2]))
                            act.wait_ge(s_t1, sum(ROPE[:z - 2]))
                        if z - 3 < 6 and not ROPE[z - 3]:
                            act.wait_ge(s_tok, z - 2)
                    act.activation(zr[z % 3][:, :].rearrange("p (a b) -> p a b", a=2), PZ[n % 2][:, :, 0:HT],
                                   ACT.Copy, scale=(HD ** -0.5 if z >= 6 else 1.0)).then_inc(s_z, 1)
                    if z == 4:
                        kz_copies(0, 1)
                    if z == 6:
                        kz_copies(1, 2)
                    if 2 <= z < 8:
                        tok_evac(z - 2)
                        store_tok(z - 2)
            act.wait_ge(s_gmm, 1)
            act.activation(gT[:, :].rearrange("p (a b) -> p a b", a=2), PA[0:24, :, 0:HT], ACT.Sigmoid)\
                .then_inc(s_gt, 1)
            act.wait_ge(s_u, 3 * CT)
            act.dma_start(A["pconv"], uP[:, :, TP:TP + TAPS - 1]).then_inc(s_out, 16)
            act.dma_start(A["sconv"], uS[:, :, :, 1:TAPS]).then_inc(s_out, 16)
            for kv in range(2):
                act.dma_start(A["s_win"][kv][:, 0:WIN - 1, :], A["win_rows"][kv][:, 1:WIN, :]).then_inc(s_out, 16)
            def x_evac(f, dst, src):
                act.wait_ge(s_xt, f + 1)
                act.activation(dst, src, ACT.Copy).then_inc(s_xh, 1)

            def gelu(u):
                kv, pr = divmod(u, 4)
                n = 320 if pr == 3 else 256
                act.wait_ge(s_cmm, u + 1)
                act.wait_ge(s_bias, kv + 1)
                if u >= 2:
                    act.wait_ge(s_w2m, u - 1)
                act.activation(hc[u % 2][:, 0:n], PA[:, u % 2, 0:n], ACT.Gelu_apprx_tanh,
                               bias=biasc[:, kv:kv + 1]).then_inc(s_gelu, 1)

            for u in range(8):
                kv, pr = divmod(u, 4)
                if u >= 2:
                    act.wait_ge(s_cmm, u - 1)
                if pr == 0:
                    act.wait_ge(s_pei, 2)
                    act.activation(XH[u % 2][:, :, 256:258], vec[:, V_PE + 16 * kv:V_PE + 16 * kv + 16]
                                   .rearrange("p (a j) -> p j a", a=2), ACT.Copy).then_inc(s_pe, 1)
                for i in range(4):
                    x_evac(FILL(u) + i, XH[u % 2][:, 2 * i:2 * i + 2, 0:256],
                           PR[:, (FILL(u) + i) % 2, :].rearrange("p (j n) -> p j n", j=2))
                if pr == 3:
                    x_evac(FILL(u) + 4, XH[u % 2][:, :, 256:320],
                           PR[:, (FILL(u) + 4) % 2, :].rearrange("p (j n) -> p j n", j=8))
                if u >= 1:
                    gelu(u - 1)
            gelu(7)
            for b in range(NS):
                if b >= 2:
                    act.wait_ge(s_sc, b - 1)
                act.wait_ge(s_kt, 3 * b + 1)
                act.activation(KTb[b % 2][:, 0:512], PR[:, 0, :], ACT.Copy).then_inc(s_ktA, 1)
                act.wait_ge(s_kt, 3 * b + 3)
                act.activation(KTb[b % 2][:, 1024:1536], PS[:, 0, :], ACT.Copy).then_inc(s_ktA, 1)
            act.wait_ge(s_sc, NS + 1)
            act.activation(Ss[:, 0:PAST].rearrange("p (a b) -> p a b", a=2), PA[0:64, :, :], ACT.Copy).then_inc(s_dA, 1)
            act.activation(Sw[:, 0:WIN], PB[0:64, 0, :], ACT.Copy).then_inc(s_dA, 1)
            act.wait_ge(s_dV, DV_CMAX)
            act.activation(Sc0[:, 0:63], PB[0:64, 1, 0:63], ACT.Exp, bias=dsm[:, 0:1], accum_out=dsm[:, 1:2])\
                .then_inc(s_dA, 1)
            act.wait_ge(s_dV, DV_WMAX)
            act.activation(Sw[:, 0:WIN + 1], Sw[:, 0:WIN + 1], ACT.Exp, bias=dsm[:, 4:5], accum_out=dsm[:, 5:6])\
                .then_inc(s_dA, 1)
            act.wait_ge(s_dV, DV_SMAX)
            act.activation(Ss[:, 0:PAST + 1], Ss[:, 0:PAST + 1], ACT.Exp, bias=dsm[:, 8:9], accum_out=dsm[:, 9:10])\
                .then_inc(s_dA, 1)
            act.wait_ge(s_dP, DP_PT)
            act.activation(PT[:, 0:512], PR[:, 0, :], ACT.Copy).then_inc(s_dA, 1)
            act.wait_ge(s_dpv, NS)
            act.activation(od[:, :].rearrange("p (a b) -> p a b", a=2), PA[0:8, :, :], ACT.Copy).then_inc(s_dA, 1)
            act.wait_ge(s_dP, DP_OT)
            for g in range(G):
                h = slice(g * HD, (g + 1) * HD)
                act.activation(actH[h, CT:KT, TP:T],
                               PS[h, 0, 0:64].rearrange("p (b g r) -> p g r b", b=NS, g=G)[:, g], ACT.Copy)\
                    .then_inc(s_dA, 1)
            for i in range(QT):
                act.wait_ge(s_cV, 9 * i + 3)
                act.activation(Pc[i % 2][:, :], Pc[i % 2][:, :], ACT.Exp).then_inc(s_cX, 1)
                act.wait_ge(s_cT, i + 1)
                act.activation(PcT[:, :, i * P:(i + 1) * P],
                               PR[:, i % 2, 0:256].rearrange("p (a q) -> p a q", a=2), ACT.Copy).then_inc(s_cE, 1)
            for s in range(N_UNITS + 2):
                if s < N_UNITS:
                    r, g, br, i = UNITS[s]
                    act.wait_ge(s_mx, s + 1)
                    if s >= 3:
                        act.wait_ge(s_T, s - 2)
                    act.activation(Pb[s % 3][:, 0:(i + 1) * P], PZ[s // 2 % 2][:, s % 2, 0:(i + 1) * P], ACT.Exp,
                                   bias=smx[:, s:s + 1], accum_out=sms[:, s:s + 1]).then_inc(s_ex, 1)
                if s >= 2:
                    u = s - 2
                    r, g, br, i = UNITS[u]
                    act.wait_ge(s_T, u + 1)
                    if u >= 2:
                        act.wait_ge(s_pv, u - 1)
                    act.activation(PTb[u % 2][:, 0:(i + 1) * P], PR[:, u % 2, 0:(i + 1) * P], ACT.Copy)\
                        .then_inc(s_ev, 1)
                if s >= 4 and s - 4 >= 15 and (s - 4) % 16 == 15:
                    rr = (s - 4) // 16
                    act.wait_ge(s_pv, 16 * (rr + 1))
                    act.activation(actH[:, CT + rr, 0:TP], PS[:, rr % 2, :], ACT.Copy).then_inc(s_oh, 1)
            act.wait_ge(s_pv, N_UNITS)
            act.activation(actH[:, KT - 1, 0:TP], PS[:, 1, :], ACT.Copy).then_inc(s_oh, 1)
            for t in range(CT):
                act.wait_ge(s_tv, TV_XC + t)
                if t >= 2:
                    act.wait_ge(s_tp, t)
                act.activation(sq[t % 2][:, :], yC[:, t, :], ACT.Square).then_inc(s_ta, 1)
            act.wait_ge(s_tp, 1 + CT)
            act.activation(rb[:, :].rearrange("p (a b) -> p a b", a=2), PR[:, :, 0:HT], ACT.Sqrt, bias=epsc[:, :])\
                .then_inc(s_ta, 1)
            for t in range(CT):
                act.wait_ge(s_tv, TV_NRM + t)
                if t >= 2:
                    act.wait_ge(s_tv, TV_NRM + CT + t - 2)
                act.activation(ac[t % 2][:, :], yC[:, t, :], ACT.Silu, scale=vec[:, V_LG + t:V_LG + t + 1],
                               bias=vec[:, V_LB + t:V_LB + t + 1]).then_inc(s_ta, 1)
                act.wait_ge(s_ta, CT + 2 + 2 * t)
                act.activation(actH[:, t, :], ac[t % 2][:, :], ACT.Copy).then_inc(s_ta, 1)
            squares(1, mixT, s_evt, 1)
            squares(2, xT, s_res, 2, 2)
            norm_hi(1, [ac0, ac1])
            with act.Fori(0, 2) as fh:
                with act.Fori(0, 4) as j:
                    for c in range(4):
                        f = 16 * fh + 4 * j + c
                        act.wait_ge(s_evt, 8 + 24 * fh + 4 * j + c + 1)
                        act.wait_ge(s_hl, f + 1)
                        act.activation(h2[c % 2][:, :], rl[c % 2][:, :], ACT.Square).then_inc(s_h2, 1)
                        act.wait_ge(s_h2, f + 1)
                        act.activation(hH[:, bass.ds(4 * j + c, 1), :].rearrange("p o t -> p (o t)"),
                                       h2[c % 2][:, :], ACT.Copy).then_inc(s_hh, 1)
            squares(3, fs, s_evt, 8 + 48 - 8 + 1)

        @block.vector
        def _(dve):
            def chain(ins, sm, n):
                ins.then_inc(sm, 1)
                dve.wait_ge(sm, n)

            def rinv(norm):
                dve.wait_ge(s_std, norm + 1)
                dve.reciprocal(rb[:, :], rb[:, :]).then_inc(s_rinv, 1)
                dve.wait_ge(s_rinv, norm + 1)

            def norm_apply(norm_split, g0, ring):
                for k in range(KT + 1):
                    if k < KT:
                        n = norm_split * KT + k
                        if k >= 2:
                            dve.wait_ge(s_nl, n - 1)
                        dve.scalar_tensor_tensor(out=ring[k % 2][:, :], in0=xT[:, k, :],
                                                 scalar=vec[:, g0 + k:g0 + k + 1], in1=rb[:, :],
                                                 op0=ALU.mult, op1=ALU.mult).then_inc(s_nt, 1)
                    if k >= 1:
                        n = norm_split * KT + k - 1
                        dve.wait_ge(s_nh, n + 1)
                        dve.tensor_tensor(actL[:, k - 1, :], ring[(k - 1) % 2][:, :],
                                          actH[:, k - 1, :].bitcast(F32), ALU.subtract).then_inc(s_nl, 1)

            dve.wait_ge(s_vec, 32)
            rinv(0)
            norm_apply(0, V_GPRE, [t1, t2])
            dve.wait_ge(s_cst, 16)
            dve.tensor_copy(identb[:, :], ident[:, :]).then_inc(s_initd, 1)
            dve.tensor_copy(maskb[:, :], C(C_MASK, P)).then_inc(s_initd, 1)
            dve.wait_ge(s_init, 8)
            dve.wait_ge(s_us, 16)

            taps_done = [0] * CT
            steps = [0]
            last = {}

            def conv(t, n):
                for _ in range(n):
                    k = taps_done[t]
                    if k == TAPS:
                        return
                    taps_done[t] += 1
                    w = vec[:, V_CW + t * TAPS + k:V_CW + t * TAPS + k + 1]
                    for hf in range(2):
                        c0 = hf * 256
                        src, dst = uP[:, t, k + c0:k + c0 + 256], yC[:, t, c0:c0 + 256]
                        if k == 0:
                            ins = dve.tensor_scalar(dst, src, w, vec[:, V_CB + t:V_CB + t + 1], ALU.mult, ALU.add)
                        else:
                            dve.wait_ge(s_tap, last[t, hf])
                            ins = dve.scalar_tensor_tensor(out=dst, in0=src, scalar=w, in1=dst, op0=ALU.mult,
                                                           op1=ALU.add)
                        ins.then_inc(s_tap, 1)
                        steps[0] += 1
                        last[t, hf] = steps[0]

            nrope = [0]

            def rope(z):
                j = nrope[0]
                nrope[0] += 1
                dve.wait_ge(s_z, z + 1)
                if j >= 1:
                    dve.wait_ge(s_rope, j)
                dve.tensor_tensor(t1[:, :], zr[z % 3][:, :], C(C_COS, T), ALU.mult).then_inc(s_t1, 1)
                dve.wait_ge(s_rot, j + 1)
                dve.tensor_tensor(t2[:, :].rearrange("p (a b) -> p a b", a=2), PR[:, :, 0:HT],
                                  C(C_SIN, T).rearrange("p (a b) -> p a b", a=2), ALU.mult).then_inc(s_rot2, 1)
                dve.wait_ge(s_t1, j + 1)
                dve.wait_ge(s_rot2, j + 1)
                if j < 3:
                    if j == 2:
                        dve.wait_ge(s_tok, 1)
                    dst = kf[j % 2][:, :]
                else:
                    dst = qT[:, j - 3, :]
                dve.tensor_tensor(dst, t1[:, :], t2[:, :], ALU.add).then_inc(s_rope, 1)

            def tok_evac_s(c):
                dve.wait_ge(s_tok, c + 1)
                dst = vtok[0:NS, (c - 3) // 2] if c in (3, 5) else ktok[0:NS, TOKSLOT[c]]
                dve.tensor_copy(dst[:, QT, :], PS[0:NS, 1, 0:P]).then_inc(s_tokD, 1)

            for n in range(N_Z + 2):
                if n < 8:
                    if n % 2 == 1:
                        t = n // 2
                        dve.wait_ge(s_grp, n + 1)
                        dve.wait_ge(s_sig, t + 1)
                        dve.tensor_tensor(uP[:, t, TAPS - 1:TAPS - 1 + HT], PB[:, 0, 0:HT], sg[:, 0:HT], ALU.mult)\
                            .then_inc(s_u, 1)
                        dve.tensor_tensor(uP[:, t, TAPS - 1 + HT:TAPS - 1 + TP], PB[:, 1, 0:TP - HT], sg[:, HT:TP],
                                          ALU.mult).then_inc(s_u, 1)
                        dve.tensor_tensor(uS[:, t, :, TAPS - 1], PB[:, 1, TP - HT:HT], sg[:, TP:T], ALU.mult)\
                            .then_inc(s_u, 1)
                        dve.wait_ge(s_u, 3 * (t + 1))
                        conv(t, 12)
                else:
                    z = n - 8
                    if 1 <= z <= 10 and ROPE[z - 1]:
                        rope(z - 1)
                    if 2 <= z < 8:
                        tok_evac_s(z - 2)
                    conv(z // 3 if z < 9 else 3, 6)
            dve.wait_ge(s_gtt, 1)
            dve.tensor_copy(gtok[:, 0:QT, :], PS[:, 0, 0:96].rearrange("p (t j) -> p t j", t=QT)).then_inc(s_gtk, 1)
            dve.tensor_copy(gtok[0:NS, QT, :], PS[0:NS, 0, 96:120]).then_inc(s_gtk, 1)

            dve.wait_ge(s_rope, 7)
            dve.wait_ge(s_gtk, 2)
            dve.wait_ge(s_tokst, 16 * 10)
            dve.wait_ge(s_kcd, 32)
            for i, X in enumerate((XH[0], XH[1], XL[0], XL[1])):
                ins = dve.memset(X[:, :, 256:XW].bitcast(U32), 0)
                ins.then_inc(s_pei if i < 2 else s_pel, 1)
            w2c = [0]

            def cmp_out_evac(u):
                kv, pr = divmod(u, 4)
                dve.wait_ge(s_w2m, u + 1)
                if kv == 0:
                    dve.tensor_copy(kcS[:, pr * P:(pr + 1) * P], PS[:, u % 2, 0:P]).then_inc(s_w2e, 1)
                    if pr == 3:
                        for g in range(G):
                            h = slice(g * HD, (g + 1) * HD)
                            dve.tensor_copy(kcBD[h, g * 32:(g + 1) * 32], PS[h, u % 2, P + g * 32:P + (g + 1) * 32])\
                                .then_inc(s_w2e, 1)
                else:
                    dve.tensor_copy(vcS[:, pr, :], PS[:, u % 2, 0:P]).then_inc(s_w2e, 1)
                    if pr == 3:
                        for r2 in range(2):
                            for g in range(G):
                                h = slice(r2 * 64 + g * 32, r2 * 64 + (g + 1) * 32)
                                dve.tensor_copy(vcBD[h, r2, g * HD:(g + 1) * HD], PS[h, u % 2, P:P + HD])\
                                    .then_inc(s_w2e, 1)

            for u in range(8):
                kv, pr = divmod(u, 4)
                if pr == 0:
                    dve.wait_ge(s_pel, 2)
                    dve.wait_ge(s_pe, kv + 1)
                    dve.tensor_tensor(XL[u % 2][:, :, 256:258], vec[:, V_PE + 16 * kv:V_PE + 16 * kv + 16]
                                      .rearrange("p (a j) -> p j a", a=2), XH[u % 2][:, :, 256:258].bitcast(F32),
                                      ALU.subtract).then_inc(s_pec, 1)
                for i in range(5 if pr == 3 else 4):
                    f = FILL(u) + i
                    dve.wait_ge(s_xh, f + 1)
                    if i < 4:
                        c, j, n = slice(2 * i, 2 * i + 2), 2, slice(0, 256)
                    else:
                        c, j, n = slice(0, 8), 8, slice(256, 320)
                    dve.tensor_tensor(XL[u % 2][:, c, n], PR[:, f % 2, :].rearrange("p (j n) -> p j n", j=j),
                                      XH[u % 2][:, c, n].bitcast(F32), ALU.subtract).then_inc(s_xl, 1)
                if pr == 1:
                    dve.wait_ge(s_cmm, u)
                    dve.tensor_tensor(biasc[:, kv:kv + 1], PA[:, (u - 1) % 2, 256:257],
                                      vec[:, V_B1 + kv:V_B1 + kv + 1], ALU.add).then_inc(s_bias, 1)
                if u >= 2:
                    cmp_out_evac(u - 2)
                conv(3, 2)
            dve.wait_ge(s_gelu, 8)
            dve.wait_ge(s_w2m, 7)
            dve.memset(Qc[:, :], 0.0).then_inc(s_q, 1)
            dve.memset(Qpad[:, :], 0.0).then_inc(s_q, 1)
            dve.wait_ge(s_q, 2)
            for g in range(G):
                h = slice(g * HD, (g + 1) * HD)
                src = qT[h, :, TP:T]
                dve.tensor_copy(Qc[h, :].rearrange("p (b g r) -> p g r b", b=NS, g=G)[:, g], src).then_inc(s_q, 1)
                dve.tensor_copy(Qpad[h, :].rearrange("p (b s) -> p s b", b=NS)[:, g * R:(g + 1) * R, :], src)\
                    .then_inc(s_q, 1)
            cmp_out_evac(6)
            cmp_out_evac(7)
            for t in range(CT):
                conv(t, TAPS)
            for b in range(NS):
                if b >= 2:
                    dve.wait_ge(s_sc, b - 1)
                dve.wait_ge(s_kt, 3 * b + 2)
                dve.tensor_copy(KTb[b % 2][:, 512:1024], PR[:, 1, :]).then_inc(s_ktD, 1)
            nv = [0]

            def v(ins):
                ins.then_inc(s_dV, 1)
                nv[0] += 1
                dve.wait_ge(s_dV, nv[0])

            dve.wait_ge(s_sc, NS + 1)
            v(dve.tensor_reduce(dsm[:, 0:1], PB[0:64, 1, 0:63], AX.X, ALU.max, negate=True))
            assert nv[0] == DV_CMAX
            v(dve.tensor_tensor(tg[:, :], PS[0:64, 1, 16:40], C(C_HM, 24, 0, 64), ALU.mult))
            v(dve.tensor_reduce(gB[:, 0:3], tg[:, :].rearrange("p (c h) -> p c h", c=3), AX.X, ALU.add))
            for bi, S_, col in ((0, Ss, PAST), (1, Sw, WIN)):
                v(dve.tensor_tensor(nw[:, bi, :], PS[0:64, 1, bi * 8:bi * 8 + 8], C(C_BM, 8, 0, 64), ALU.mult))
                v(dve.tensor_reduce(S_[:, col:col + 1], nw[:, bi, :], AX.X, ALU.add))
            dve.wait_ge(s_dA, 2)
            v(dve.tensor_reduce(dsm[:, 4:5], Sw[:, 0:WIN + 1], AX.X, ALU.max, negate=True))
            assert nv[0] == DV_WMAX
            dve.wait_ge(s_dA, 3)
            v(dve.tensor_scalar_max(dsm[:, 2:3], dsm[:, 1:2], 1e-30))
            v(dve.reciprocal(dsm[:, 3:4], dsm[:, 2:3]))
            v(dve.memset(Sc0[:, 63:64], 0.0))
            v(dve.tensor_scalar(Sc0[:, 0:63], Sc0[:, 0:63], dsm[:, 3:4], None, ALU.mult))
            assert nv[0] == DV_PN
            dve.wait_ge(s_dP, DP_PN)
            v(dve.tensor_copy(pnT[:, :], PR[0:64, 0, 0:64]))
            dve.wait_ge(s_dP, DP_IM1)
            v(dve.tensor_copy(im1[:, :], PR[0:64, 1, 0:16]))
            dve.wait_ge(s_dP, DP_IM2)
            v(dve.tensor_copy(im2[:, :], PR[0:64, 0, 64:80]))
            v(dve.tensor_reduce(dsm[:, 12:13], im2[:, 1:15], AX.X, ALU.min))
            v(dve.tensor_scalar(tj[:, :], im2[:, 1:15], dsm[:, 12:13], None, ALU.is_le))
            v(dve.tensor_tensor(tj[:, :], tj[:, :], C(C_J, 14, 0, 64), ALU.mult))
            v(dve.tensor_reduce(dsm[:, 13:14], tj[:, :], AX.X, ALU.max))
            v(dve.memset(sb0[:, :], 0.0))
            v(dve.tensor_scalar(sb0[:, 1:15], C(C_J, 14, 0, 64), dsm[:, 13:14], NEG, ALU.is_equal, ALU.mult))
            Ss4 = Ss[:, 0:PAST].rearrange("p (r k c) -> p r k c", r=8, k=NBLK)
            bias4 = sb0[:, :].unsqueeze(1).unsqueeze(3).broadcast_to([64, 8, NBLK, 8])
            v(dve.tensor_tensor(Ss4, Ss4, bias4, ALU.add))
            v(dve.tensor_reduce(dsm[:, 8:9], Ss[:, 0:PAST + 1], AX.X, ALU.max, negate=True))
            assert nv[0] == DV_SMAX
            for a_ in range(2):
                v(dve.tensor_scalar(Pd[:, a_, :], Sc0[:, :], gB[:, 0:1], C(C_PAR + a_, 1, 0, 64), ALU.mult, ALU.mult))
            for bi, S_, n_, o, na in ((1, Sw, WIN, 4, 4), (0, Ss, PAST, 8, 5)):
                dve.wait_ge(s_dA, na)
                v(dve.tensor_scalar_max(dsm[:, o + 2:o + 3], dsm[:, o + 1:o + 2], 1e-30))
                v(dve.reciprocal(dsm[:, o + 3:o + 4], dsm[:, o + 2:o + 3]))
                v(dve.tensor_scalar(S_[:, 0:n_ + 1], S_[:, 0:n_ + 1], dsm[:, o + 3:o + 4], gB[:, 1 + bi:2 + bi],
                                    ALU.mult, ALU.mult))
                v(dve.tensor_scalar(nw[:, bi, :], C(C_BM, 8, 0, 64), S_[:, n_:n_ + 1], None, ALU.mult))
            assert nv[0] == DV_P
            dve.wait_ge(s_dP, DP_PT)
            v(dve.tensor_copy(PT[:, 512:832], PR[:, 1, 0:320]))
            v(dve.tensor_copy(PTn[:, :], PS[0:8, 0, 0:128]))
            for t in range(CT):
                tmp = KTb0[:, t * 248:(t + 1) * 248].rearrange("p (b k) -> p b k", b=NS)
                w = vec[:, V_CW + t * TAPS:V_CW + (t + 1) * TAPS].unsqueeze(1).broadcast_to([P, NS, TAPS])
                chain(dve.tensor_tensor(tmp, uS[:, t, :, :], w, ALU.mult), s_ys, 3 * t + 1)
                chain(dve.tensor_reduce(yC[:, t, TP:T], tmp, AX.X, ALU.add), s_ys, 3 * t + 2)
                chain(dve.tensor_scalar(yC[:, t, TP:T], yC[:, t, TP:T], vec[:, V_CB + t:V_CB + t + 1], None, ALU.add),
                      s_ys, 3 * t + 3)
            dve.wait_ge(s_dA, 9)
            for g in range(G):
                h = slice(g * HD, (g + 1) * HD)
                v(dve.tensor_tensor(actL[h, CT:KT, TP:T],
                                    PS[h, 0, 0:64].rearrange("p (b g r) -> p g r b", b=NS, g=G)[:, g],
                                    actH[h, CT:KT, TP:T].bitcast(F32), ALU.subtract))
            nc_ = [0]

            def cv(ins):
                ins.then_inc(s_cV, 1)
                nc_[0] += 1
                dve.wait_ge(s_cV, nc_[0])

            for i in range(QT):
                p3 = Pc[i % 2][:, :].rearrange("p (h n) -> p h n", h=NH)
                vis = C(C_VIS, 128)[:, i * 32:(i + 1) * 32].unsqueeze(1).broadcast_to([P, NH, 32])
                visb = C(C_VISB, 128)[:, i * 32:(i + 1) * 32].unsqueeze(1).broadcast_to([P, NH, 32])
                sm = smc[:, i, :]
                if i >= 2:
                    dve.wait_ge(s_cT, i - 1)
                dve.wait_ge(s_cS, i + 1)
                cv(dve.tensor_tensor(p3, PZ[i // 2][:, i % 2, 0:256].rearrange("p (h n) -> p h n", h=NH), visb, ALU.add))
                cv(dve.tensor_reduce(sm, p3, AX.X, ALU.max))
                cv(dve.tensor_tensor(p3, p3, sm.unsqueeze(2).broadcast_to([P, NH, 32]), ALU.subtract))
                dve.wait_ge(s_cX, i + 1)
                cv(dve.tensor_tensor(p3, p3, vis, ALU.mult))
                sm2 = smx[:, 8 * i:8 * i + 8]
                sm3 = sms[:, 8 * i:8 * i + 8]
                gate = gtok[:, i, 0:8].rearrange("p (g r) -> p r g", g=G)
                cv(dve.tensor_reduce(sm2, p3, AX.X, ALU.add))
                cv(dve.tensor_scalar_max(sm2, sm2, 1e-30))
                cv(dve.reciprocal(sm3, sm2))
                cv(dve.tensor_tensor(sm3.rearrange("p (r g) -> p r g", r=R), sm3.rearrange("p (r g) -> p r g", r=R),
                                     gate, ALU.mult))
                cv(dve.tensor_tensor(p3, p3, sm3.unsqueeze(2).broadcast_to([P, NH, 32]), ALU.mult))
            for s in range(N_UNITS + 1):
                if s < N_UNITS:
                    r, g, br, i = UNITS[s]
                    dve.wait_ge(s_S, s + 1)
                    dve.tensor_reduce(smx[:, s:s + 1], PZ[s // 2 % 2][:, s % 2, 0:(i + 1) * P], AX.X, ALU.max,
                                      negate=True).then_inc(s_mx, 1)
                if s >= 1:
                    u = s - 1
                    r, g, br, i = UNITS[u]
                    dve.wait_ge(s_ex, u + 1)
                    dve.tensor_scalar_max(sms[:, u:u + 1], sms[:, u:u + 1], 1e-30).then_inc(s_sm, 1)
                    dve.wait_ge(s_sm, 2 * u + 1)
                    dve.reciprocal(smr[:, u:u + 1], sms[:, u:u + 1]).then_inc(s_sm, 1)
                    dve.wait_ge(s_sm, 2 * u + 2)
                    gc = 8 * (1 + br) + g * R + r
                    dve.tensor_scalar(Pb[u % 3][:, 0:(i + 1) * P], Pb[u % 3][:, 0:(i + 1) * P], smr[:, u:u + 1],
                                      gtok[:, i, gc:gc + 1], ALU.mult, ALU.mult).then_inc(s_pn, 1)
                if s >= 4 and s - 4 >= 15 and (s - 4) % 16 == 15:
                    rr = (s - 4) // 16
                    dve.wait_ge(s_oh, rr + 1)
                    dve.tensor_tensor(actL[:, CT + rr, 0:TP], PS[:, rr % 2, :], actH[:, CT + rr, 0:TP].bitcast(F32),
                                      ALU.subtract).then_inc(s_ol, 1)
            dve.wait_ge(s_oh, R)
            dve.tensor_tensor(actL[:, KT - 1, 0:TP], PS[:, 1, :], actH[:, KT - 1, 0:TP].bitcast(F32), ALU.subtract)\
                .then_inc(s_ol, 1)
            tv = [0]

            def tvi(ins, wait=True):
                ins.then_inc(s_tv, 1)
                tv[0] += 1
                if wait:
                    dve.wait_ge(s_tv, tv[0])

            dve.wait_ge(s_tap, 2 * TAPS * CT)
            dve.wait_ge(s_ys, 3 * CT)
            tvi(dve.tensor_tensor(ysm[:, :], yC[:, 0, :], yC[:, 1, :], ALU.add))
            tvi(dve.tensor_tensor(ysm[:, :], ysm[:, :], yC[:, 2, :], ALU.add))
            tvi(dve.tensor_tensor(ysm[:, :], ysm[:, :], yC[:, 3, :], ALU.add))
            assert tv[0] == TV_SUM
            dve.wait_ge(s_tp, 1)
            for t in range(CT):
                y3 = yC[:, t, :].rearrange("p (a b) -> p a b", a=2)
                tvi(dve.tensor_tensor(y3, y3, PS[:, :, 0:HT], ALU.subtract), wait=False)
            assert tv[0] == TV_XC - 1 + CT
            dve.wait_ge(s_ta, CT + 1)
            tvi(dve.reciprocal(rb[:, :], rb[:, :]))
            for t in range(CT):
                tvi(dve.tensor_tensor(yC[:, t, :], yC[:, t, :], rb[:, :], ALU.mult), wait=False)
            assert tv[0] == TV_NRM - 1 + CT
            for t in range(CT):
                dve.wait_ge(s_ta, CT + 1 + 2 * (t + 1))
                tvi(dve.tensor_tensor(actL[:, t, :], ac[t % 2][:, :], actH[:, t, :].bitcast(F32), ALU.subtract),
                    wait=False)
            dve.wait_ge(s_tv, tv[0])
            def evac(k, dst):
                dve.wait_ge(s_grp, N_Z + k + 1)
                dve.tensor_copy(dst.rearrange("p (a b) -> p a b", a=2), PZ[k % 2][:, :, 0:HT]).then_inc(s_evt, 1)

            for k in range(KT):
                evac(k, mixT[:, k, :])

            def residual(i, src, g0):
                for k in range(KT):
                    dve.scalar_tensor_tensor(out=src[:, k, :], in0=src[:, k, :], scalar=vec[:, g0 + k:g0 + k + 1],
                                             in1=rb[:, :], op0=ALU.mult, op1=ALU.mult).then_inc(s_res, 1)
                    dve.wait_ge(s_res, 2 * KT + k + 1 if i else 2 * k + 1)
                    ins = dve.tensor_tensor(xT[:, k, :], xT[:, k, :], src[:, k, :], ALU.add)
                    ins.then_inc(s_y if i else s_res, 1)

            dve.wait_ge(s_evt, KT)
            rinv(1)
            residual(0, mixT, V_GPOST)
            dve.wait_ge(s_res, 2 * KT)
            rinv(2)
            norm_apply(1, V_GPRE2, [ac0, ac1])
            dve.wait_ge(s_nl, 2 * KT)
            dve.wait_ge(s_out, 16 * 4)
            for hf in range(2):
                dve.memset(fs[:, 4 * hf:4 * hf + 4, :], 0.0).then_inc(s_hl, 1)
            dve.wait_ge(s_hl, 2)
            GB = 26
            with dve.Fori(0, 2) as fh:
                with dve.Fori(0, 4) as j:
                    for c in range(4):
                        dve.wait_ge(s_grp, GB + 32 * fh + 4 * j + c + 1)
                        dve.tensor_scalar(rl[c % 2][:, :].rearrange("p (a b) -> p a b", a=2), PZ[c % 2][:, :, 0:HT],
                                          0.0, None, ALU.max).then_inc(s_evt, 1)
                        dve.wait_ge(s_hh, 16 * fh + 4 * j + c + 1)
                        dve.tensor_tensor(hL[:, bass.ds(4 * j + c, 1), :].rearrange("p o t -> p (o t)"),
                                          h2[c % 2][:, :],
                                          hH[:, bass.ds(4 * j + c, 1), :].rearrange("p o t -> p (o t)").bitcast(F32),
                                          ALU.subtract).then_inc(s_hl, 1)
                with dve.Fori(0, 4) as mp:
                    dve.wait_ge(s_evt, 24 * fh + 24)
                    for c in range(2):
                        dve.wait_ge(s_grp, GB + 32 * fh + 16 + 4 * mp + 2 + c + 1)
                        f3 = fs[:, bass.ds(2 * mp + c, 1), :].rearrange("p o (a b) -> p (o a) b", a=2)
                        dve.tensor_tensor(f3, f3, PZ[c % 2][:, :, 0:HT], ALU.add).then_inc(s_evt, 1)
            dve.wait_ge(s_evt, 8 + 48)
            rinv(3)
            residual(1, fs, V_GPOST2)

        @block.tensor
        def _(pe):
            def feed_mean(norm, ready_sem, ready0, o, dst, tiles):
                for k in range(tiles):
                    pe.wait_ge(ready_sem, ready0 + k + 1)
                    for hf in range(2):
                        mm = pe.matmul(dst[:, hf, 0:HT], ones[:, o, :], sq[k % 2][:, hf * HT:(hf + 1) * HT],
                                       start=(k == 0), stop=(k == tiles - 1))
                    mm.then_inc(s_tp if norm is None else s_st, 1)

            def group(s, c, pz, src_h, src_l, k0=0, first=True, last=True, nk=KT):
                for hf in range(2):
                    cols = slice(hf * HT, (hf + 1) * HT)
                    for k in range(nk):
                        w = slice(k * 2 * P + c * P, k * 2 * P + (c + 1) * P)
                        for i, (W_, X_) in enumerate(((wH, src_h), (wH, src_l), (wL, src_h))):
                            mm = pe.matmul(pz[:, hf, 0:HT], W_[s][:, w], X_[:, k0 + k, cols],
                                           start=(first and k == 0 and i == 0),
                                           stop=(last and k == nk - 1 and i == 2))
                mm.then_inc(s_grp, 1)

            pe.wait_ge(s_init, 8)
            feed_mean(0, s_sq, 0, 0, PS, KT)

            def rot(z, j):
                pe.wait_ge(s_z, z + 1)
                if j == 0:
                    pe.wait_ge(s_cst, 16)
                else:
                    pe.wait_ge(s_rot2, j)
                for hf in range(2):
                    mm = pe.matmul(PR[:, hf, 0:HT], C(C_PERM, P), zr[z % 3][:, hf * HT:(hf + 1) * HT],
                                   start=True, stop=True)
                mm.then_inc(s_rot, 1)

            def turn_tok(c):
                if ROPE[c]:
                    j = sum(ROPE[:c])
                    pe.wait_ge(s_rope, j + 1)
                    src = kf[j % 2]
                else:
                    pe.wait_ge(s_z, c + 1)
                    src = zr[c % 3]
                if c >= 1:
                    pe.wait_ge(s_tokA, c)
                    pe.wait_ge(s_tokD, c)
                for t in range(QT):
                    pe.transpose(PS[:, 0, t * P:(t + 1) * P], src[:, t * P:(t + 1) * P], ident[:, :])
                pe.transpose(PS[0:NS, 1, 0:P], src[:, TP:T], ident[:, :]).then_inc(s_tok, 1)

            pe.wait_ge(s_vec, 32)
            pe.wait_ge(s_rinv, 1)
            pe.wait_ge(s_nl, KT)
            for n in range(N_Z):
                b, c = divmod(n, 2)
                pe.wait_ge(s_split, b + 1)
                if 2 <= n < 10:
                    if n % 2 == 0:
                        pe.wait_ge(s_sig, (n - 2) // 2 + 1)
                    else:
                        pe.wait_ge(s_u, 3 * ((n - 2) // 2 + 1))
                elif n >= 10:
                    pe.wait_ge(s_z, n - 2 - 8 + 1)
                group(b % 2, c, PZ[n % 2], actH, actL)
                z = n - 8
                if z >= 1 and ROPE[z - 1]:
                    rot(z - 1, sum(ROPE[:z - 1]))
                if 2 <= z < 8:
                    turn_tok(z - 2)
            pe.wait_ge(s_wgs, 2)
            pe.wait_ge(s_z, 9)
            for hf in range(2):
                for k in range(KT):
                    for i, (W_, X_) in enumerate(((wgH, actH), (wgH, actL), (wgL, actH))):
                        mm = pe.matmul(PA[0:24, hf, 0:HT], W_[:, k * 24:(k + 1) * 24],
                                       X_[:, k, hf * HT:(hf + 1) * HT],
                                       start=(k == 0 and i == 0), stop=(k == KT - 1 and i == 2))
            mm.then_inc(s_gmm, 1)
            rot(9, 6)
            pe.wait_ge(s_gt, 1)
            pe.wait_ge(s_tokA, 6)
            pe.wait_ge(s_tokD, 6)
            for t in range(QT):
                pe.transpose(PS[:, 0, t * 24:(t + 1) * 24], gT[:, t * P:(t + 1) * P], ident[0:24, 0:24])
            pe.transpose(PS[0:NS, 0, 96:120], gT[:, TP:T], ident[0:24, 0:24]).then_inc(s_gtt, 1)

            def turn_unit(u):
                kv, pr = divmod(u, 4)
                pe.wait_ge(s_rc[u % 2], 16 * (u // 2 + 1))
                raw = rawc[u % 2][:, :].rearrange("p (g n) -> p g n", g=G)
                for i in range(5 if pr == 3 else 4):
                    f = FILL(u) + i
                    if f == 0:
                        pe.wait_ge(s_rope, 7)
                    if f >= 2:
                        pe.wait_ge(s_xl, f - 1)
                    if i < 4:
                        for jj in range(2):
                            for g in range(G):
                                jp = 2 * i + jj
                                mm = pe.transpose(PR[:, f % 2, (jj * 2 + g) * P:(jj * 2 + g + 1) * P],
                                                  raw[:, g, jp * P:(jp + 1) * P], ident[:, :])
                    else:
                        pe.wait_ge(s_rp[kv], 32)
                        pw = pchunk.rearrange("p (g n) -> p g n", g=G)
                        for jp in range(8):
                            for g in range(G):
                                mm = pe.transpose(PR[:, f % 2, (jp * 2 + g) * 32:(jp * 2 + g + 1) * 32],
                                                  pw[:, g, jp * P:(jp + 1) * P], ident[0:NCH_P, 0:NCH_P])
                    mm.then_inc(s_xt, 1)

            def cmp_mm(u):
                kv, pr = divmod(u, 4)
                N = (258, 256, 256, 320)[pr]
                s = (B_CK + kv) % 2
                pe.wait_ge(s_split, B_CK + kv + 1)
                pe.wait_ge(s_xl, FILL(u) + (5 if pr == 3 else 4))
                if pr == 0:
                    pe.wait_ge(s_pec, kv + 1)
                if u == 0:
                    pe.wait_ge(s_gt, 1)
                if u >= 2:
                    pe.wait_ge(s_gelu, u - 1)
                for t in range(16):
                    w = slice(t * P, (t + 1) * P)
                    sh = t // 8
                    for i, (W_, X_) in enumerate(((wH, XH), (wH, XL), (wL, XH))):
                        mm = pe.matmul(PA[:, u % 2, 0:N], W_[s][:, w], X_[u % 2][:, t % 8, sh:sh + N],
                                       start=(t == 0 and i == 0), stop=(t == 15 and i == 2))
                mm.then_inc(s_cmm, 1)

            def cmp_out(u):
                kv, pr = divmod(u, 4)
                pe.wait_ge(s_gelu, u + 1)
                if u == 0:
                    pe.wait_ge(s_misc, 16)
                    pe.wait_ge(s_gtk, 2)
                if u >= 2:
                    pe.wait_ge(s_w2e, W2E(u - 2))
                h = hc[u % 2]
                if kv == 0:
                    for g in range(G):
                        mm = pe.matmul(PS[g * HD:(g + 1) * HD, u % 2, 0:P], w2[:, 0, :], h[:, g * P:(g + 1) * P],
                                       start=True, stop=True)
                    if pr == 3:
                        for g in range(G):
                            mm = pe.matmul(PS[g * HD:(g + 1) * HD, u % 2, P + g * 32:P + (g + 1) * 32], w2[:, 0, :],
                                           h[:, 256 + g * 32:256 + (g + 1) * 32], start=True, stop=True)
                else:
                    for g in range(G):
                        mm = pe.matmul(PS[:, u % 2, g * HD:(g + 1) * HD], h[:, g * P:(g + 1) * P], w2[:, 1, :],
                                       start=True, stop=True)
                    if pr == 3:
                        for r2 in range(2):
                            mm = pe.matmul(PS[r2 * 64:(r2 + 1) * 64, u % 2, P:P + HD], h[:, 256:320], w2[:, 1, :],
                                           start=True, stop=True)
                mm.then_inc(s_w2m, 1)

            for u in range(9):
                if u < 8:
                    turn_unit(u)
                if u >= 1:
                    cmp_mm(u - 1)
                if u >= 2:
                    cmp_out(u - 2)
            cmp_out(7)

            def turn_keys(b):
                pe.wait_ge(s_dec[b % 2], 32 * (b // 2 + 1))
                for q in range(2):
                    if b >= 1:
                        pe.wait_ge(s_ktA if q == 0 else s_ktD, 2 * b - 1 if q == 0 else b)
                    for r in range(4):
                        mm = pe.transpose(PR[:, q, r * P:(r + 1) * P], rks[b % 2][:, (4 * q + r) * P:(4 * q + r + 1) * P],
                                          ident[:, :])
                    mm.then_inc(s_kt, 1)
                if b >= 1:
                    pe.wait_ge(s_ktA, 2 * b)
                for r in range(4):
                    mm = pe.transpose(PS[:, 0, r * P:(r + 1) * P], rkw[b % 2][:, r * P:(r + 1) * P], ident[:, :])
                mm.then_inc(s_kt, 1)

            def key_scores(b):
                pe.wait_ge(s_ktA, 2 * b + 2)
                pe.wait_ge(s_ktD, b + 1)
                if b == 0:
                    pe.wait_ge(s_q, 6)
                    pe.wait_ge(s_w2e, W2E(7))
                q = Qpad[:, b * 64:(b + 1) * 64]
                f, l = b == 0, b == NS - 1
                pe.matmul(PA[0:64, 0, :], q, KTb[b % 2][:, 0:512], start=f, stop=l)
                pe.matmul(PA[0:64, 1, :], q, KTb[b % 2][:, 512:1024], start=f, stop=l)
                pe.matmul(PB[0:64, 0, :], q, KTb[b % 2][:, 1024:1536], start=f, stop=l)
                pe.matmul(PB[0:64, 1, 0:64], q, kcS[:, b * 64:(b + 1) * 64], start=f, stop=l).then_inc(s_sc, 1)

            pe.wait_ge(s_w2e, W2E(7))
            for b in range(NS + 1):
                if b < NS:
                    turn_keys(b)
                if b >= 1:
                    key_scores(b - 1)
            pe.wait_ge(s_kzc, 6)
            for bi in range(2):
                pe.matmul(PS[0:64, 1, bi * 8:bi * 8 + 8], Qc[:, :], knew[:, bi, :], start=True, stop=True)
            pe.matmul(PS[0:64, 1, 16:40], C(C_EB, 64, 0, 8), gtok[0:8, QT, :], start=True, stop=True).then_inc(s_sc, 1)
            pe.wait_ge(s_dV, DV_PN)
            pe.transpose(PR[0:64, 0, 0:64], Sc0[:, :], ident[0:64, 0:64]).then_inc(s_dP, 1)
            pe.wait_ge(s_dV, DV_PN + 1)
            pe.matmul(PR[0:64, 1, 0:16], pnT[:, :], C(C_OV, 16, 0, 64), start=True, stop=True).then_inc(s_dP, 1)
            pe.wait_ge(s_dV, DV_PN + 2)
            pe.matmul(PR[0:64, 0, 64:80], C(C_RS, 64, 0, 64), im1[:, :], start=True, stop=True).then_inc(s_dP, 1)
            pe.wait_ge(s_dV, DV_P)
            for r in range(8):
                pe.transpose(PR[:, 0, r * 64:(r + 1) * 64], Ss[:, r * P:(r + 1) * P], ident[0:64, 0:64])
            for r in range(4):
                pe.transpose(PR[:, 1, r * 64:(r + 1) * 64], Sw[:, r * P:(r + 1) * P], ident[0:64, 0:64])
            pe.transpose(PR[:, 1, 256:320], Pd[:, :, :].rearrange("p a n -> p (a n)"), ident[0:64, 0:64])
            for bi in range(2):
                mm = pe.transpose(PS[0:8, 0, bi * 64:(bi + 1) * 64], nw[:, bi, :], ident[0:64, 0:64])
            mm.then_inc(s_dP, 1)
            pe.wait_ge(s_dA, 6)
            pe.wait_ge(s_dV, DV_P + 2)
            for b in range(NS):
                i = NS + b
                pe.wait_ge(s_dec[i % 2], 32 * (i // 2 + 1))
                o = PA[0:8, b // 4, (b % 4) * P:(b % 4 + 1) * P]
                for r in range(8):
                    pe.matmul(o, PT[:, r * 64 + b * 8:r * 64 + b * 8 + 8], rks[i % 2][:, r * P:(r + 1) * P],
                              start=(r == 0), stop=False)
                for r in range(4):
                    pe.matmul(o, PT[:, 512 + r * 64 + b * 8:512 + r * 64 + b * 8 + 8],
                              rkw[i % 2][:, r * P:(r + 1) * P], start=False, stop=False)
                pe.matmul(o, PT[:, 768 + b * 8:768 + b * 8 + 8], vcS[:, b // 2, :], start=False, stop=False)
                for bi in range(2):
                    mm = pe.matmul(o, PTn[0:8, bi * 64 + b * 8:bi * 64 + b * 8 + 8], vtok[0:8, bi, QT, :],
                                   start=False, stop=(bi == 1))
                mm.then_inc(s_dpv, 1)
            pe.wait_ge(s_dA, 7)
            for b in range(NS):
                mm = pe.transpose(PS[:, 0, b * 8:(b + 1) * 8], od[:, b * P:(b + 1) * P], ident[0:8, 0:8])
            mm.then_inc(s_dP, 1)
            def pc_scores(i):
                for r in range(R):
                    mm = pe.matmul(PZ[i // 2][:, i % 2, r * 64:(r + 1) * 64], qT[:, r, i * P:(i + 1) * P], kcBD[:, :],
                                   start=True, stop=True)
                mm.then_inc(s_cS, 1)

            def pc_turn(i):
                pe.wait_ge(s_cV, 9 * i + 9)
                if i >= 2:
                    pe.wait_ge(s_cE, i - 1)
                for rp in range(2):
                    mm = pe.transpose(PR[:, i % 2, rp * P:(rp + 1) * P], Pc[i % 2][:, rp * P:(rp + 1) * P], ident[:, :])
                mm.then_inc(s_cT, 1)

            for i in range(QT):
                pc_scores(i)
            for i in range(QT):
                pc_turn(i)
            pe.wait_ge(s_cE, QT)
            pe.wait_ge(s_initd, 2)
            pe.wait_ge(s_dV, DV_P + 4)
            for s in range(N_UNITS + 3):
                if s < N_UNITS:
                    r, g, br, i = UNITS[s]
                    n = (i + 1) * P
                    if s >= 4:
                        pe.wait_ge(s_ex, s - 3)
                    dst = PZ[s // 2 % 2][:, s % 2, 0:n]
                    pe.matmul(dst, qT[:, r, i * P:(i + 1) * P], kz[:, br, g, 0:n], start=True, stop=True)
                    pe.matmul(dst[:, i * P:n], identb[:, :], maskb[:, :], start=False, stop=True,
                              skip_group_check=True).then_inc(s_S, 1)
                if 2 <= s < N_UNITS + 2:
                    u = s - 2
                    r, g, br, i = UNITS[u]
                    pe.wait_ge(s_pn, u + 1)
                    if u >= 2:
                        pe.wait_ge(s_ev, u - 1)
                    for j in range(i + 1):
                        mm = pe.transpose(PR[:, u % 2, j * P:(j + 1) * P], Pb[u % 3][:, j * P:(j + 1) * P], ident[:, :])
                    mm.then_inc(s_T, 1)
                if s >= 3:
                    u = s - 3
                    r, g, br, i = UNITS[u]
                    if u % 16 == 0:
                        if r >= 2:
                            pe.wait_ge(s_ol, r - 1)
                        pe.matmul(PS[:, r % 2, :], vcBD[:, r % 2, :], PcT[:, r // 2, :], start=True, stop=False,
                                  skip_group_check=True)
                    pe.wait_ge(s_ev, u + 1)
                    for j in range(i + 1):
                        mm = pe.matmul(PS[g * HD:(g + 1) * HD, r % 2, i * P:(i + 1) * P],
                                       vtok[:, br, j, g * HD:(g + 1) * HD], PTb[u % 2][:, j * P:(j + 1) * P],
                                       start=False, stop=(j == i), skip_group_check=True)
                    mm.then_inc(s_pv, 1)
            pe.wait_ge(s_tv, TV_SUM)
            pe.wait_ge(s_ol, R)
            for hf in range(2):
                mm = pe.matmul(PS[:, hf, 0:HT], ones[:, 1, :], ysm[:, hf * HT:(hf + 1) * HT], start=True, stop=True)
            mm.then_inc(s_tp, 1)
            pe.wait_ge(s_ev, N_UNITS)
            feed_mean(None, s_ta, 0, 1, PR, CT)
            pe.wait_ge(s_tv, TV_NRM - 1 + 2 * CT)
            pe.wait_ge(s_ex, N_UNITS)
            for k in range(KT):
                b = B_OUT + k // 2
                pe.wait_ge(s_split, b + 1)
                if k >= 2:
                    pe.wait_ge(s_evt, k - 1)
                group(b % 2, k % 2, PZ[k % 2], actH, actL)
            feed_mean(1, s_sq, KT, 0, PS, KT)
            pe.wait_ge(s_std, 2)
            feed_mean(2, s_sq, 2 * KT, 0, PS, KT)
            pe.wait_ge(s_nl, 2 * KT)
            pe.wait_ge(s_evt, KT)
            with pe.Fori(0, 2) as fh:
                with pe.Fori(0, 4) as j:
                    for q in range(2):
                        s = (B_FFN + q) % 2
                        pe.wait_ge(s_split, B_FFN + 16 * fh + 2 * j + q + 1)
                        for c in range(2):
                            pe.wait_ge(s_evt, 24 * fh + 4 * j + 2 * q + c + 7)
                            group(s, c, PZ[c], actH, actL)
                with pe.Fori(0, 4) as mp:
                    pe.wait_ge(s_hl, 16 * fh + 18)
                    for q in range(2):
                        s = (B_FFN + q) % 2
                        pe.wait_ge(s_split, B_FFN + 16 * fh + 8 + 2 * mp + q + 1)
                        for c in range(2):
                            if q == 0:
                                pe.wait_ge(s_evt, 24 * fh + 16 + 2 * mp + c + 7)
                            group(s, c, PZ[c], hH, hL, q * KT, q == 0, q == 1)
            feed_mean(3, s_sq, 3 * KT, 0, PS, KT)


def kernel(**inputs):
    import concourse.bacc as bacc
    from concourse.bass_utils import run_bass_kernel_spmd

    x = {n: np.asarray(v) for n, v in inputs.items()}
    f32 = np.float32

    def tiles(w):
        return w.reshape(-1, P, w.shape[-1]).transpose(1, 0, 2)

    def fm(v):
        return v.reshape(-1, P).T

    def chunks(n):
        return x[n].reshape(-1, STRIDE, G, HD).transpose(0, 2, 1, 3).reshape(-1, STRIDE * P)

    w_in, w_out, w_up, w_down = (x[n][0] for n in ("w_in", "w_out", "w_up", "w_down"))
    blocks = []
    for t in range(CT):
        blocks.append(np.concatenate([w_in[:, CH + P * t:CH + P * (t + 1)], w_in[:, P * t:P * (t + 1)]], 1))
    c1 = 2 * CH + NH * HD
    for t in range(3):
        blocks.append(w_in[:, c1 + 2 * P * t:c1 + 2 * P * (t + 1)])
    q_w = w_in[:, 2 * CH:c1].reshape(D, G, R, HD).transpose(0, 2, 1, 3).reshape(D, NH * HD)
    blocks += [q_w[:, 0:2 * P], q_w[:, 2 * P:]]
    blocks = [tiles(b).reshape(P, BW) for b in blocks]
    for n in ("cmp_k_w1", "cmp_v_w1"):
        blocks.append(x[n][0].reshape(STRIDE, 2, HD, 2 * HD).transpose(1, 2, 0, 3).reshape(P, BW))
    att = w_out[CH:].reshape(G, R, HD, D).transpose(1, 0, 2, 3).reshape(NH * HD, D)
    w_o = np.concatenate([w_out[:CH], att], 0)
    blocks += [tiles(w_o[:, 2 * P * m:2 * P * (m + 1)]).reshape(P, BW) for m in range(4)]
    for fh in range(2):
        for b in range(8):
            c = fh * 2048 + 2 * P * b
            blocks.append(tiles(w_up[:, c:c + 2 * P]).reshape(P, BW))
        for mp in range(4):
            for q in range(2):
                r = fh * 2048 + q * 1024
                blocks.append(tiles(w_down[r:r + 1024, 2 * P * mp:2 * P * (mp + 1)]).reshape(P, BW))
    wblk = np.stack(blocks)

    pe_ = [x[n][0].reshape(STRIDE, 2, HD).transpose(1, 2, 0).reshape(P, STRIDE) for n in ("cmp_k_pe", "cmp_v_pe")]
    vecs = np.concatenate(
        [fm(x["g_pre_mix"][0]), fm(x["conv_b"][0]), fm(x["conv_ln_g"][0]), fm(x["conv_ln_b"][0]),
         fm(x["g_post_mix"][0]), fm(x["g_pre_ffn"][0]), fm(x["g_post_ffn"][0]),
         x["cmp_k_b1"][0][:, None], x["cmp_v_b1"][0][:, None],
         x["conv_w"][0].reshape(TAPS, CT, P).transpose(2, 1, 0).reshape(P, CT * TAPS)] + pe_, 1)
    wgate = tiles(w_in[:, c1 + 6 * P:]).reshape(P, KT * 24)

    p = np.arange(P)
    pos = np.concatenate([np.arange(TP), np.full(NS, PAST)]).astype(f32)
    inv = np.power(f32(500000.0), -np.arange(8, dtype=f32) * f32(2.0) / f32(16)).astype(f32)
    ang = (pos[None, :] * inv[:, None]).astype(f32)
    cos, sin, perm = np.ones((P, T), f32), np.zeros((P, T), f32), np.zeros((P, P), f32)
    for g in range(G):
        for d in range(16):
            cos[g * HD + d], sin[g * HD + d] = np.cos(ang[d % 8]), np.sin(ang[d % 8])
        for d in range(8):
            perm[g * HD + d + 8, g * HD + d] = -1
            perm[g * HD + d, g * HD + d + 8] = 1
    mask = np.where(p[None, :] <= p[:, None], 0, NEG).astype(f32)
    qpos = (np.arange(QT)[None, :] * P + p[:, None])[:, :, None]
    n32 = np.arange(NCH_P)[None, None, :]
    vis = ((STRIDE * n32 + 31 <= qpos) & (n32 < NCH_P - 1)).reshape(P, QT * NCH_P)
    r64 = np.arange(64)
    i_, j_ = np.arange(NCH_S)[:, None], np.arange(NBLK)[None, :]
    ov = np.maximum(np.minimum(i_ * 16 + 32, (j_ + 1) * 64) - np.maximum(i_ * 16, j_ * 64), 0) // 16 * (i_ < 63)

    def rows(m):
        return np.concatenate([m, np.zeros((P - m.shape[0], m.shape[1]))], 0).astype(f32)

    same = (r64[:, None] // 4 == r64[None, :] // 4)
    consts = np.concatenate(
        [np.eye(P), perm, cos, sin, mask, vis, np.where(vis, 0, NEG),
         rows(r64[:, None] % 8 == np.arange(24)[None, :] % 8), rows(r64[:, None] // 8 == np.arange(8)[None, :]),
         rows(same), rows(np.arange(8)[:, None] == r64[None, :] // 8), rows(ov),
         rows(np.tile(np.arange(1, 15), (64, 1))), np.stack([p % 8, p % 16, p // 8 % 2 == 0, p // 8 % 2 == 1], 1)], 1).astype(f32)
    assert consts.shape == (P, N_C) and vecs.shape == (P, N_VEC)

    xs = np.concatenate([x["x_prompt"][0], x["x_sample"][:, 0]], 0)
    us0 = np.concatenate([x["cache_conv"][0], np.zeros((NS, 1, CH), f32)], 1)
    us0 = us0.reshape(NS, TAPS, CT, P).transpose(3, 2, 0, 1)
    pt = x["page_table"]
    pt_rep = np.stack([pt[2 * pr + p // 64, (p % 64) // 8] for pr in range(4)]
                      + [pt[b, p // STRIDE] for b in range(NS)], 1)
    ins = {"wblk": wblk, "wgate": wgate, "vecs": vecs, "consts": consts, "x_fm": tiles(xs.T), "us0": us0,
           "w2": np.stack([x["cmp_k_w2"][0], x["cmp_v_w2"][0]], 1), "pt_rep": pt_rep,
           "pool_kc": chunks("cache_k_cmp"), "pool_vc": chunks("cache_v_cmp"),
           "pool_ks": x["cache_k_sel"].reshape(-1, 1024), "pool_vs": x["cache_v_sel"].reshape(-1, 1024),
           "cwk": x["cache_k_win"].reshape(NS, WIN, P), "cwv": x["cache_v_win"].reshape(NS, WIN, P)}
    outs = {"y_fm": (P, KT, T), "pconv": (P, CT, TAPS - 1), "sconv": (P, CT, NS, TAPS - 1)}
    for c in range(6):
        outs[f"p_rows{c}"] = (TP, P)
    for c in range(4):
        outs[f"s_rows{c}"] = (NS, P)
    for kv in range(2):
        outs[f"s_win{kv}"] = (NS, WIN, P)

    nc = bacc.Bacc("TRN2", target_bir_lowering=False, num_devices=1)
    arrays, A = {}, {}
    for name, v in ins.items():
        v = np.ascontiguousarray(v)
        arrays[name + "_dram"] = v
        A[name] = nc.dram_tensor(name + "_dram", v.shape, mybir.dt.from_np(v.dtype), kind="ExternalInput").ap()
    for name, shape in outs.items():
        A[name] = nc.dram_tensor(name + "_dram", shape, F32, kind="ExternalOutput").ap()
    for base, n in (("p_rows", 6), ("s_rows", 4), ("s_win", 2)):
        A[base] = [A[f"{base}{i}"] for i in range(n)]
    A["win_rows"] = [A["cwk"], A["cwv"]]
    A["win_k"], A["win_v"] = (A[n].rearrange("b (p r) d -> b p (r d)", r=4) for n in ("cwk", "cwv"))
    hymba_step(nc, A)
    res = run_bass_kernel_spmd(nc, [arrays], core_ids=[0]).results[0]
    res = {name: res[name + "_dram"] for name in outs}

    y = res["y_fm"].transpose(2, 1, 0).reshape(T, D)
    p_new = [res[f"p_rows{c}"].reshape(1, 1, TP, G, HD) for c in range(6)]
    s_new = [res[f"s_rows{c}"].reshape(1, NS, 1, G, HD) for c in range(4)]
    s_win = [res[f"s_win{kv}"].reshape(1, NS, WIN, G, HD) for kv in range(2)]
    pconv = res["pconv"].transpose(2, 1, 0).reshape(1, 1, TAPS - 1, CH)
    sconv = res["sconv"].transpose(2, 3, 1, 0).reshape(1, NS, TAPS - 1, CH)
    return (y[None, :TP], y[TP:, None], *p_new, pconv, *s_new, *s_win, sconv)
```

```python
from contextlib import ExitStack

import numpy as np

import concourse.bass as bass
from concourse import mybir

F32 = mybir.dt.float32
F32R = mybir.dt.float32r
BF16 = mybir.dt.bfloat16
I32 = mybir.dt.int32
U32 = mybir.dt.uint32
ALU = mybir.AluOpType
ACT = mybir.ActivationFunctionType
AX = mybir.AxisListType

P = 128
D = 1024
KT = D // P
TP = 512
NS = 8
T = TP + NS
HT = T // 2
QT = TP // P
CH = 512
CT = CH // P
TAPS = 31
HD = 64
NH = 8
G = 2
R = NH // G
PAST = 1024
PAGE = 128
NPG = PAST // PAGE
WIN = 512
STRIDE = 16
NCH_S = PAST // STRIDE
NCH_P = TP // STRIDE
NBLK = PAST // 64
EPS = 1e-6
NEG = -1e30

B_CK, B_CV, B_IN, B_PK, B_PV, B_OUT, B_FFN = 0, 1, 2, 11, 12, 13, 17
N_BLOCKS = B_FFN + 32
N_Z = 18
BW = KT * 2 * P

V_GPRE, V_CB, V_LG, V_LB, V_GPOST, V_GPRE2, V_GPOST2 = 0, 8, 12, 16, 20, 28, 36
V_B1, V_CW, V_PE = 44, 46, 46 + CT * TAPS
N_VEC = V_PE + 32
C_ID, C_PERM, C_COS, C_SIN = 0, 128, 256, 256 + T
C_MASK = C_SIN + T
C_VIS = C_MASK + 128
C_VISB = C_VIS + 128
C_HM = C_VISB + 128
C_BM = C_HM + 24
C_RS = C_BM + 8
C_EB = C_RS + 64
C_OV = C_EB + 64
C_J = C_OV + 16
C_CI = C_J + 14
C_PAR = C_CI + 2
N_C = C_PAR + 2


ROPE = (1, 0, 1, 0, 1, 0, 1, 1, 1, 1)
TOKSLOT = {0: 0, 1: 1, 2: 2, 4: 3}
UNITS = [(r, g, br, i) for r in range(R) for g in range(G) for br in range(2) for i in range(QT)]
N_UNITS = len(UNITS)
LAG = 3


def SPLITS(b):
    return b + 1 if b < B_PK else b - 1


Y_DVE = [(k, slice(0, T)) for k in range(5)] + [(5, slice(0, HT))]
Y_POOL = [(6, slice(0, T)), (7, slice(0, T)), (5, slice(HT, T))]

DV_CMAX, DV_WMAX, DV_PN, DV_SMAX, DV_P = 1, 8, 12, 23, 33
DP_PN, DP_IM1, DP_IM2, DP_PT, DP_OT = 1, 2, 3, 4, 5
PC_DONE = 10
TV_SUM, TV_XC = 3, 4
TV_NRM = TV_XC + CT + 1


def hymba_step(nc, A):
    ctx = ExitStack()
    with ctx:
        def psum(name):
            return ctx.enter_context(nc.psum_tensor(name, [P, 2, 512], F32))

        def sem(name):
            return ctx.enter_context(nc.semaphore(name))

        def region(*groups):
            out, most = {}, 0
            for group in groups:
                size = 0
                with ExitStack() as scope:
                    for name, shape, dt in group:
                        out[name] = scope.enter_context(nc.sbuf_tensor(name, shape, dt))
                        n = int(np.prod(shape[1:])) * (2 if dt == BF16 else 4)
                        size += -(-n // 32) * 32
                most = max(most, size)
            ctx.enter_context(nc.sbuf_tensor("space_of_" + groups[0][0][0], [P, most // 4], F32))
            return out

        def sb(name, shape, dt=F32):
            return ctx.enter_context(nc.sbuf_tensor(name, shape, dt))

        xT = sb("xT", [P, KT, T])
        wraw = [sb(f"wraw{i}", [P, BW]) for i in range(2)]
        wH = [sb(f"wH{i}", [P, BW], F32R) for i in range(2)]
        wL = [sb(f"wL{i}", [P, BW], F32R) for i in range(2)]
        vec = sb("vec", [P, N_VEC])
        ones = sb("ones", [P, 2, P])
        epsc = sb("epsc", [P, 1])
        zero = sb("zero", [P, 1])
        ident = sb("ident", [P, P])
        swap = sb("swap", [P, P])
        sq = [sb(f"sq{i}", [P, T]) for i in range(2)]
        rb = sb("rb", [P, T])
        a = region(
            [("cH", [P, CT, T], F32R), ("cL", [P, CT, T], F32R)],
            [("hcp", [P, 2, P], F32), ("ysm", [P, T], F32), ("ctmp", [P, CT, NS, TAPS], F32)],
        )
        b = region(
            [("oH", [P, CT, T], F32R), ("oL", [P, CT, T], F32R)],
            [("rks", [P, 2, 1024], F32), ("rkw", [P, 2, 512], F32), ("od", [NH, 1024], F32)],
        )
        cH, cL, hcp, ysm, ctmp = (a[n] for n in ("cH", "cL", "hcp", "ysm", "ctmp"))
        oH, oL, od = b["oH"], b["oL"], b["od"]
        rks, rkw = ([b[n][:, i, :] for i in range(2)] for n in ("rks", "rkw"))
        actH = [(cH if k < CT else oH)[:, k % CT, :] for k in range(KT)]
        actL = [(cL if k < CT else oL)[:, k % CT, :] for k in range(KT)]
        base = [
            ("cst", [P, N_C - C_PERM], F32), ("identb", [P, P], BF16), ("maskb", [P, P], BF16),
            ("uS", [P, CT, NS, TAPS], F32), ("w2", [P, 2, HD], F32),
            ("biasc", [P, 2], F32), ("kcBD", [P, HD], F32), ("vcBD", [P, 2, P], F32),
            ("kcS", [P, 512], F32), ("vcS", [P, 4, P], F32), ("pt_i", [P, 12], I32), ("idx", [P, 12], U32),
        ]
        mixer = [
            ("uP", [P, CT, TAPS - 1 + TP], F32), ("yC", [P, CT, T], F32),
            ("qT", [P, R, T], F32), ("kz", [P, 2, G, TP], F32), ("knew", [P, 2, NS], F32),
            ("vtok", [P, 2, QT + 1, P], F32), ("gtok", [P, QT + 1, 24], F32),
        ]
        ffn = [("hH", [P, 16, T], F32R), ("hL", [P, 16, T], F32R), ("fs", [P, KT, T], F32),
               ("r2", [P, T], F32), ("r4", [P, T], F32),
               ("rl0", [P, T], F32), ("rl1", [P, T], F32), ("h20", [P, T], F32), ("h21", [P, T], F32)]
        inproj = [("sg", [P, T], F32), ("zr0", [P, T], F32), ("zr1", [P, T], F32), ("zr2", [P, T], F32),
                  ("t1", [P, T], F32), ("t2", [P, T], F32), ("kf0", [P, T], F32), ("kf1", [P, T], F32),
                  ("ktok", [P, 4, QT + 1, P], F32), ("gT", [24, T], F32),
                  ("wg", [P, KT * 24], F32), ("wgH", [P, KT * 24], F32R), ("wgL", [P, KT * 24], F32R),
                  ("XP", [P, 2, 8, 130], F32)]
        XW = 260
        cmp_ = [("XH0", [P, KT, XW], F32R), ("XH1", [P, KT, XW], F32R),
                ("XL0", [P, KT, XW], F32R), ("XL1", [P, KT, XW], F32R),
                ("hc0", [P, XW], F32), ("hc1", [P, XW], F32),
                ("rawc0", [P, 2048], F32), ("rawc1", [P, 2048], F32), ("rawc2", [P, 2048], F32),
                ("rawc3", [P, 2048], F32)]
        attn = [("KTb0", [P, 1536], F32), ("KTb1", [P, 1536], F32), ("PT", [P, 832], F32), ("PTn", [8, 128], F32),
                ("Ss", [64, PAST + 8], F32), ("Sw", [64, WIN + 8], F32), ("Pd", [64, 2, 64], F32),
                ("Sc0", [64, 64], F32), ("pnT", [64, 64], F32), ("im1", [64, 16], F32), ("im2", [64, 16], F32),
                ("sb0", [64, 16], F32), ("tj", [64, 14], F32), ("tg", [64, 24], F32), ("gB", [64, 4], F32),
                ("nw", [64, 2, 8], F32), ("dsm", [64, 24], F32),
                ("Qc", [P, 64], F32), ("Qpad", [P, 576], F32),
                ("Pb0", [P, 512], F32), ("Pb1", [P, 512], F32), ("Pb2", [P, 512], F32),
                ("PTb0", [P, 512], F32), ("PTb1", [P, 512], F32),
                ("PcT", [P, 2, TP], F32),
                ("smc", [P, 4, 8], F32), ("smx", [P, 64], F32), ("sms", [P, 64], F32), ("smr", [P, 64], F32)]
        tail = [("mixT", [P, KT, T], F32)]
        out = {}
        with ExitStack() as pre:
            for name, shape, dt in base:
                out[name] = pre.enter_context(nc.sbuf_tensor(name, shape, dt))
            with ExitStack() as scope:
                for name, shape, dt in cmp_:
                    out[name] = scope.enter_context(nc.sbuf_tensor(name, shape, dt))
            for name, shape, dt in mixer:
                out[name] = pre.enter_context(nc.sbuf_tensor(name, shape, dt))
            for group in (inproj, attn, tail):
                with ExitStack() as scope:
                    for name, shape, dt in group:
                        out[name] = scope.enter_context(nc.sbuf_tensor(name, shape, dt))
        for name, shape, dt in ffn:
            out[name] = sb(name, shape, dt)
        (cst, identb, maskb, uS, w2, biasc, kcBD, vcBD, kcS, vcS, pt_i, idx) = (out[n] for n, _, _ in base)
        (uP, yC, qT, kz, knew, vtok, gtok) = (out[n] for n, _, _ in mixer)
        (sg, zr0, zr1, zr2, t1, t2, kf0, kf1, ktok, gT, wg, wgH, wgL, XP) = (out[n] for n, _, _ in inproj)
        zr, kf = [zr0, zr1, zr2], [kf0, kf1]
        XH, XL = [out["XH0"], out["XH1"]], [out["XL0"], out["XL1"]]
        rawc = [out[f"rawc{i}"] for i in range(4)]
        hc = [out["hc0"], out["hc1"]]
        (KTb0, KTb1, PT, PTn, Ss, Sw, Pd, Sc0, pnT, im1, im2, sb0, tj, tg, gB, nw, dsm, Qc, Qpad,
         Pb0, Pb1, Pb2, PTb0, PTb1, PcT, smc, smx, sms, smr) = (out[n] for n, _, _ in attn)
        KTb, Pb, PTb, Pc = [KTb0, KTb1], [Pb0, Pb1, Pb2, KTb0[:, 0:TP]], [PTb0, PTb1], KTb1[:, 0:1024]
        mixT = out["mixT"]
        hH, hL, fs, r2, r4, rl0, rl1, h20, h21 = (out[n] for n, _, _ in ffn)
        rl, h2 = [rl0, rl1], [h20, h21]

        def C(c0, n, p0=0, p1=P):
            return cst[p0:p1, c0 - C_PERM:c0 - C_PERM + n]

        PA, PB, PR, PS = psum("PA"), psum("PB"), psum("PR"), psum("PS")
        PZ = [PA, PB]

        s_vec, s_cst, s_x, s_misc, s_wg, s_pt, s_us = (sem(n) for n in (
            "vec_loaded", "const_loaded", "x_loaded", "w2_loaded", "wg_loaded", "pt_loaded", "us_loaded"))
        s_raw = [sem(f"block_loaded{i}") for i in range(2)]
        s_whi, s_split, s_wgs = sem("block_hi"), sem("block_split"), sem("wg_split")
        s_init, s_initd, s_idx = sem("pool_init"), sem("dve_init"), sem("idx_ready")
        s_grp = sem("group_done")
        s_gmm = sem("gates_done")
        s_sq, s_st, s_std, s_rinv = sem("squared"), sem("mean_fed"), sem("std_ready"), sem("rinv_ready")
        s_nt, s_nh, s_nl = sem("norm_tmp"), sem("norm_hi"), sem("norm_lo")
        s_sig, s_u, s_z = sem("sigmoid_ready"), sem("glu_ready"), sem("z_ready")
        s_rot, s_rot2, s_t1, s_rope = sem("rot_done"), sem("rot_used"), sem("cos_done"), sem("roped")
        s_tok, s_tokA, s_tokD, s_kzc = sem("tok_done"), sem("tok_evac_act"), sem("tok_evac_dve"), sem("kz_copied")
        s_gt, s_gtt, s_gtk = sem("gates_sig"), sem("gates_turned"), sem("gates_ready")
        s_out = sem("stores_done")
        s_kcd = sem("kcmp_stored")
        s_tap, s_ys = sem("conv_step"), sem("conv_sample")
        s_rc = [sem(f"cmp_raw_loaded{i}") for i in range(4)]
        s_xt, s_xh, s_xl, s_pe, s_cmm = sem("x_turned"), sem("x_hi"), sem("x_lo"), sem("pe_col"), sem("cmp_unit")
        s_bias, s_gelu, s_w2m, s_w2e = sem("cmp_bias"), sem("gelu_done"), sem("cmp_out"), sem("cmp_out_used")
        s_dec = [sem(f"dec_loaded{i}") for i in range(2)]
        s_win = [sem(f"window_loaded{i}") for i in range(2)]
        s_kt, s_ktA, s_ktD, s_sc = sem("k_turned"), sem("k_evac_act"), sem("k_evac_dve"), sem("scores_done")
        s_q = sem("q_padded")
        s_dA, s_dV, s_dP = sem("dec_act"), sem("dec_dve"), sem("dec_pe")
        s_dpv = sem("dec_pv")
        s_cS, s_cX, s_cP, s_cT, s_cE = (sem(n) for n in ("pc_scores", "pc_exp", "pc_probs", "pc_turned", "pc_evac"))
        s_cV = sem("pc_dve")
        s_pei, s_pel, s_pec = sem("xh_zeroed"), sem("xl_zeroed"), sem("pe_col_lo")
        s_tokst = sem("tokens_stored")
        s_init2 = sem("mixer_zeroed")
        s_swp, s_xp, s_pcm = sem("prompt_swapped"), sem("prompt_x"), sem("prompt_cmp")
        s_S, s_mx, s_ex, s_pn, s_T, s_ev, s_pv, s_oh, s_ol = (sem(n) for n in (
            "att_scores", "att_max", "att_exp", "att_norm", "att_turned", "att_evac", "att_pv", "att_ohi", "att_olo"))
        s_sm = sem("att_small")
        s_tv, s_ta, s_tp = sem("tail_dve"), sem("tail_act"), sem("tail_pe")
        s_evt = sem("tile_evacuated")
        s_scaled, s_res = sem("branch_scaled"), sem("residual_added")
        s_r = sem("mlp_scale_step")
        s_fsq, s_acc, s_fg = sem("f_squared"), sem("f_squares_summed"), sem("f_gained")
        s_ym, s_yd, s_ypm, s_yp = sem("y_scaled_dve"), sem("y_dve"), sem("y_scaled_pool"), sem("y_pool")
        s_h2, s_hh, s_hl = sem("h_squared"), sem("h_hi"), sem("h_lo")
        s_fz = sem("fs_zeroed")

        block = ctx.enter_context(nc.Block())
        NORMS = range(4)
        A_wblk = A["wblk"]

        @block.sync
        def _(sp):
            sp.dma_start(vec[:, :], A["vecs"]).then_inc(s_vec, 16)
            sp.dma_start(ident[:, :], A["consts"][:, 0:P]).then_inc(s_vec, 16)
            sp.dma_start(wraw[0][:, :], A_wblk[0]).then_inc(s_raw[0], 16)
            sp.dma_start(w2[:, :, :], A["w2"]).then_inc(s_misc, 16)
            sp.dma_start(swap[:, 0:64], A["consts"][:, 64:P]).then_inc(s_misc, 16)
            sp.dma_start(swap[:, 64:P], A["consts"][:, 0:64]).then_inc(s_misc, 16)
            sp.wait_ge(s_rc[0], 16)
            sp.dma_start(xT[:, :, :], A["x_fm"]).then_inc(s_x, 16)
            sp.dma_start(wraw[1][:, :], A_wblk[1]).then_inc(s_raw[1], 16)
            sp.dma_start(cst[:, 0:C_CI - C_PERM], A["consts"][:, P:C_CI]).then_inc(s_cst, 16)
            sp.dma_start(C(C_PAR, 2), A["consts"][:, C_PAR:C_PAR + 2]).then_inc(s_cst, 16)
            sp.dma_start(uS[:, :, :, :], A["us0"]).then_inc(s_us, 16)

            def load(slot, b):
                sp.dma_start(wraw[slot][:, :], A_wblk[bass.ds(b, 1)].rearrange("o p n -> (o p) n"))\
                    .then_inc(s_raw[slot], 16)

            with sp.Fori(1, 6) as i:
                for s in range(2):
                    sp.wait_ge(s_split, 2 * i + s - 1)
                    load(s, 2 * i + s)
            sp.wait_ge(s_split, SPLITS(10))
            sp.dma_start(wraw[0][:, :], A_wblk[12]).then_inc(s_raw[0], 16)
            for b in (13, 14):
                sp.wait_ge(s_pcm, b - 12)
                sp.dma_start(wraw[b % 2][:, :], A_wblk[b]).then_inc(s_raw[b % 2], 16)
            with sp.Fori(0, (N_BLOCKS - 15) // 2) as i:
                for e in range(2):
                    sp.wait_ge(s_split, 12 + 2 * i + e)
                    load(1 - e, 15 + 2 * i + e)
            for k, sm, n in ((0, s_yd, 1), (1, s_yd, 2), (6, s_yp, 1), (2, s_yd, 3), (3, s_yd, 4), (7, s_yp, 2),
                             (4, s_yd, 5), (5, s_yd, 6)):
                sp.wait_ge(sm, n)
                if k == 5:
                    sp.wait_ge(s_yp, 3)
                sp.dma_start(A["y_fm"][:, k, :], xT[:, k, :]).then_inc(s_out, 16)
            sp.wait_ge(s_out, 16 * (KT + 4))
            sp.wait_ge(s_tokst, 16 * 10)
            sp.wait_ge(s_kcd, 16 * 2)

        @block.gpsimd
        def _(pool):
            for t_, v in ((ones[:, 0, :], 1.0 / D), (ones[:, 1, :], 1.0 / CH), (epsc[:, :], EPS),
                          (zero[:, :], 0.0), (kcBD[:, :], 0.0), (vcBD[:, :, :], 0.0)):
                pool.memset(t_, v).then_inc(s_init, 1)
            pool.wait_ge(s_pt, 32)
            pool.tensor_scalar(idx[:, 0:4], pt_i[:, 0:4], 8.0, C(C_CI, 1), ALU.mult, ALU.add).then_inc(s_idx, 1)
            pool.tensor_scalar(idx[:, 4:12], pt_i[:, 4:12], 16.0, C(C_CI + 1, 1), ALU.mult, ALU.add)\
                .then_inc(s_idx, 1)
            pool.wait_ge(s_init, 6)

            def split(b, s, raw_count, n_split, free_sem=None, free_count=0):
                pool.wait_ge(s_raw[s], raw_count)
                if free_sem is not None:
                    pool.wait_ge(free_sem, free_count)
                pool.tensor_tensor(wH[s][:, :], wraw[s][:, :], zero[:, :].broadcast_to([P, BW]), ALU.add)\
                    .then_inc(s_whi, 1)
                pool.wait_ge(s_whi, n_split)
                pool.tensor_tensor(wL[s][:, :], wraw[s][:, :], wH[s][:, :].bitcast(F32), ALU.subtract)\
                    .then_inc(s_split, 1)

            pools_c = [A["pool_kc"], A["pool_vc"]]

            def gather(u):
                kv, pr = divmod(u, 4)
                if u >= 4:
                    pool.wait_ge(s_xt, 4 * (u - 3))
                pool.indirect_dma_start(rawc[u % 4][:, :], None, pools_c[kv],
                                        bass.IndirectOffsetOnAxis(ap=idx[:, pr:pr + 1], axis=0))\
                    .then_inc(s_rc[u % 4], 16)

            pool.wait_ge(s_idx, 2)
            for u in range(4):
                gather(u)
            gather(4)
            split(1, 1, 16, 2)
            gather(5)
            gather(6)
            gather(7)
            split(2, 0, 32, 3, s_cmm, 4)
            pool.wait_ge(s_cmm, 8)
            pool.memset(uP[:, :, 0:TAPS - 1], 0.0).then_inc(s_init2, 1)
            split(3, 1, 32, 4, s_cmm, 8)
            pool.memset(XP[:, :, :, 64:130], 0.0).then_inc(s_init2, 1)
            pool.wait_ge(s_w2m, 8)
            pool.memset(kz[:, :, :, :], 0.0).then_inc(s_init2, 1)
            with pool.Fori(2, 4) as i:
                for s in range(2):
                    split(2 * i + s, s, 16 * i + 16, 2 * i + s + 1, s_grp, 4 * i + 2 * s - 6)
            pool.wait_ge(s_wg, 16)
            pool.tensor_copy(wgH[:, :], wg[:, :]).then_inc(s_wgs, 1)
            pool.wait_ge(s_wgs, 1)
            pool.tensor_tensor(wgL[:, :], wg[:, :], wgH[:, :].bitcast(F32), ALU.subtract).then_inc(s_wgs, 1)
            split(8, 0, 16 * 5, 9, s_grp, 10)
            split(9, 1, 16 * 5, 10, s_grp, 12)
            split(10, 0, 16 * 6, 11, s_grp, 14)

            pool.wait_ge(s_gmm, 1)
            pools_s = [A["pool_ks"], A["pool_vs"]]

            def dec_load(i):
                kv, b = divmod(i, NS)
                pool.indirect_dma_start(rks[i % 2][:, :], None, pools_s[kv],
                                        bass.IndirectOffsetOnAxis(ap=idx[:, 4 + b:5 + b], axis=0))\
                    .then_inc(s_dec[i % 2], 16)

            dec_load(0)
            dec_load(1)
            for i in range(2, 2 * NS):
                if i < NS + 2:
                    pool.wait_ge(s_kt, 3 * (i - 1))
                else:
                    pool.wait_ge(s_dpv, i - NS - 1)
                dec_load(i)
            split(13, 1, 16 * 7, 12, s_grp, 16)
            split(14, 0, 16 * 8, 13, s_grp, 18)
            split(15, 1, 16 * 8, 14, s_grp, 20)
            split(16, 0, 16 * 9, 15, s_grp, 22)
            split(17, 1, 16 * 9, 16, s_grp, 24)
            for k in range(KT):
                pool.wait_ge(s_scaled, k + 1)
                pool.tensor_tensor(xT[:, k, :], xT[:, k, :], mixT[:, k, :], ALU.add).then_inc(s_res, 1)
            split(18, 0, 16 * 10, 17, s_grp, 26)
            with pool.Fori(0, (N_BLOCKS - 19) // 2) as i:
                for e in range(2):
                    split(19, 1 - e, 16 * (10 + i + e), 18 + 2 * i + e, s_grp, 28 + 4 * i + 2 * e)
            for k in range(1, 6):
                pool.wait_ge(s_fsq, k + 1)
                if k >= 2:
                    pool.wait_ge(s_acc, k - 1)
                pool.tensor_tensor(rl0[:, :], rl0[:, :], (h20, h21)[k % 2][:, :], ALU.add).then_inc(s_acc, 1)
            pool.wait_ge(s_r, 4)
            pool.wait_ge(s_fg, KT)
            for j, (k, c) in enumerate(Y_POOL):
                pool.tensor_tensor(fs[:, k, c], fs[:, k, c], rb[:, c], ALU.mult).then_inc(s_ypm, 1)
                pool.wait_ge(s_ypm, j + 1)
                pool.tensor_tensor(xT[:, k, c], xT[:, k, c], fs[:, k, c], ALU.add).then_inc(s_yp, 1)

        @block.scalar
        def _(act):
            def squares(norm, src, ready=None, first=0, step=1):
                for k in range(KT):
                    n = norm * KT + k
                    if n >= 2:
                        act.wait_ge(s_st, n - 1)
                    if ready is not None:
                        act.wait_ge(ready, first + step * k)
                    act.activation(sq[k % 2][:, :], src[:, k, :], ACT.Square).then_inc(s_sq, 1)
                root(norm)

            def root(norm):
                act.wait_ge(s_st, KT * (norm + 1))
                act.activation(rb[:, :].rearrange("p (a b) -> p a b", a=2), PS[:, :, 0:HT], ACT.Sqrt,
                               bias=epsc[:, :]).then_inc(s_std, 1)

            def x_evac(u, i):
                act.wait_ge(s_xt, 4 * u + i + 1)
                act.activation(XH[u % 2][:, 2 * i:2 * i + 2, 0:256],
                               PR[:, i % 2, :].rearrange("p (j n) -> p j n", j=2), ACT.Copy).then_inc(s_xh, 1)

            def norm_hi(k0, k1):
                for k in range(k0, k1):
                    act.wait_ge(s_nt, k + 1)
                    act.activation(actH[k], sq[k % 2][:, :], ACT.Copy).then_inc(s_nh, 1)

            def gelu(u):
                kv = u // 4
                act.wait_ge(s_cmm, u + 1)
                act.wait_ge(s_bias, kv + 1)
                if u >= 2:
                    act.wait_ge(s_w2m, u - 1)
                act.activation(hc[u % 2][:, 0:256], PA[:, u % 2, 0:256], ACT.Gelu_apprx_tanh,
                               bias=biasc[:, kv:kv + 1]).then_inc(s_gelu, 1)

            act.dma_start(pt_i[:, :], A["pt_rep"]).then_inc(s_pt, 16)
            act.dma_start(C(C_CI, 2), A["consts"][:, C_CI:C_CI + 2]).then_inc(s_pt, 16)
            act.wait_ge(s_raw[0], 16)
            act.activation(wH[0][:, :], wraw[0][:, :], ACT.Copy).then_inc(s_whi, 1)
            act.wait_ge(s_vec, 32)
            for u in range(8):
                kv, pr = divmod(u, 4)
                if u >= 2:
                    act.wait_ge(s_cmm, u - 1)
                if pr == 0:
                    act.wait_ge(s_pei, 2)
                    act.activation(XH[u % 2][:, :, 256:258], vec[:, V_PE + 16 * kv:V_PE + 16 * kv + 16]
                                   .rearrange("p (a j) -> p j a", a=2), ACT.Copy).then_inc(s_pe, 1)
                for i in range(4):
                    x_evac(u, i)
                if 2 <= u < 6:
                    act.wait_ge(s_x, 16)
                    for k in (2 * u - 4, 2 * u - 3):
                        if k >= 2:
                            act.wait_ge(s_st, k - 1)
                        act.activation(sq[k % 2][:, :], xT[:, k, :], ACT.Square).then_inc(s_sq, 1)
                if u == 5:
                    act.wait_ge(s_init, 6)
                    act.wait_ge(s_st, KT)
                    act.activation(rb[:, :].rearrange("p (a b) -> p a b", a=2), PB[:, :, 0:HT], ACT.Sqrt,
                                   bias=epsc[:, :]).then_inc(s_std, 1)
                if u >= 6:
                    norm_hi(3 * (u - 6), 3 * (u - 5))
                if u >= 1:
                    gelu(u - 1)
            norm_hi(6, KT)
            gelu(7)
            def tok_evac(c):
                act.wait_ge(s_tok, c + 1)
                dst = vtok[:, (c - 3) // 2] if c in (3, 5) else ktok[:, TOKSLOT[c]]
                act.activation(dst[:, 0:QT, :], PS[:, 0, :].rearrange("p (t d) -> p t d", t=QT), ACT.Copy)\
                    .then_inc(s_tokA, 1)

            def store_tok(c):
                act.wait_ge(s_tokA, c + 1)
                act.wait_ge(s_tokD, c + 1)
                src = vtok[:, (c - 3) // 2] if c in (3, 5) else ktok[:, TOKSLOT[c]]
                act.dma_start(A["p_rows"][c].rearrange("(t p) d -> p t d", p=P), src[:, 0:QT, :])\
                    .then_inc(s_kcd if c < 2 else s_tokst, 16)
                dst = A["s_rows"][c] if c < 4 else A["s_win"][c - 4][:, WIN - 1, :]
                act.dma_start(dst, src[0:NS, QT, :]).then_inc(s_tokst, 16)

            def kz_copies(bi, kfi):
                act.wait_ge(s_rope, kfi + 1)
                for g in range(G):
                    h = slice(g * HD, (g + 1) * HD)
                    act.activation(kz[h, bi, g, :], kf[kfi % 2][h, 0:TP], ACT.Copy).then_inc(s_kzc, 1)
                act.activation(knew[:, bi, :], kf[kfi % 2][:, TP:T], ACT.Copy).then_inc(s_kzc, 1)

            def prompt_chunks():
                act.wait_ge(s_rope, 1)
                act.wait_ge(s_z, 2)
                act.wait_ge(s_swp, 1)
                for kv, own in enumerate((kf[0], zr[1])):
                    for jj in range(2):
                        h = slice(jj * HD, (jj + 1) * HD)
                        for g, src in ((jj, own[h, 0:TP]), (1 - jj, PR[h, kv, :])):
                            act.activation(XP[h, kv, :, g * 32:(g + 1) * 32],
                                           src.rearrange("p (c t j) -> p t c j", t=8, j=2)[:, :, :, jj], ACT.Copy)\
                                .then_inc(s_xp, 1)

            act.dma_start(wg[:, :], A["wgate"]).then_inc(s_wg, 16)
            for kv in range(2):
                act.dma_start(A["s_win"][kv][:, 0:WIN - 1, :], A["win_rows"][kv][:, 1:WIN, :]).then_inc(s_out, 16)
            act.wait_ge(s_init2, 3)
            for n in range(N_Z):
                if n < 8:
                    if n % 2 == 0:
                        act.wait_ge(s_grp, n + 1)
                        if n >= 2:
                            act.wait_ge(s_u, 3 * (n // 2))
                        act.activation(sg[:, :].rearrange("p (a b) -> p a b", a=2), PZ[0][:, :, 0:HT], ACT.Sigmoid)\
                            .then_inc(s_sig, 1)
                else:
                    z = n - 8
                    act.wait_ge(s_grp, n + 1)
                    if z >= 3:
                        if ROPE[z - 3]:
                            act.wait_ge(s_rot, sum(ROPE[:z - 2]))
                            act.wait_ge(s_t1, sum(ROPE[:z - 2]))
                        if z == 4:
                            act.wait_ge(s_xp, 8)
                        if z - 3 < 6 and not ROPE[z - 3]:
                            act.wait_ge(s_tok, z - 2)
                    act.activation(zr[z % 3][:, :].rearrange("p (a b) -> p a b", a=2), PZ[n % 2][:, :, 0:HT],
                                   ACT.Copy, scale=(HD ** -0.5 if z >= 6 else 1.0)).then_inc(s_z, 1)
                    if z == 2:
                        prompt_chunks()
                    if z == 4:
                        kz_copies(0, 1)
                    if z == 6:
                        kz_copies(1, 2)
                    if 2 <= z < 8:
                        tok_evac(z - 2)
                        store_tok(z - 2)
            act.wait_ge(s_gmm, 1)
            act.activation(gT[:, :].rearrange("p (a b) -> p a b", a=2), PA[0:24, :, 0:HT], ACT.Sigmoid)\
                .then_inc(s_gt, 1)
            for i in range(2):
                act.dma_start(rkw[i][:, :], A["win_k"][i]).then_inc(s_win[i], 16)
            act.wait_ge(s_u, 3 * CT)
            act.dma_start(A["pconv"], uP[:, :, TP:TP + TAPS - 1]).then_inc(s_out, 16)
            act.dma_start(A["sconv"], uS[:, :, :, 1:TAPS]).then_inc(s_out, 16)
            for kv in range(2):
                act.wait_ge(s_pcm, kv + 1)
                act.activation(hcp[:, kv, 0:64], PA[:, kv, 0:64], ACT.Gelu_apprx_tanh, bias=biasc[:, kv:kv + 1])\
                    .then_inc(s_gelu, 1)
            act.wait_ge(s_tokst, 16 * 10)
            act.wait_ge(s_kcd, 32)

            def window_load(i):
                kv, b = divmod(i, NS)
                if 2 <= i < NS + 2:
                    act.wait_ge(s_kt, 3 * (i - 1))
                elif i >= 2:
                    act.wait_ge(s_dpv, i - NS - 1)
                act.dma_start(rkw[i % 2][:, :], (A["win_k"], A["win_v"])[kv][b]).then_inc(s_win[i % 2], 16)

            def keys_evac(b):
                if b >= 2:
                    act.wait_ge(s_sc, b - 1)
                act.wait_ge(s_kt, 3 * b + 1)
                act.activation(KTb[b % 2][:, 0:512], PR[:, 0, :], ACT.Copy).then_inc(s_ktA, 1)
                act.wait_ge(s_kt, 3 * b + 3)
                act.activation(KTb[b % 2][:, 1024:1536], PS[:, 0, :], ACT.Copy).then_inc(s_ktA, 1)
                window_load(b + 2)

            for b in range(NS):
                keys_evac(b)
            act.wait_ge(s_sc, NS + 1)
            act.activation(Ss[:, 0:PAST].rearrange("p (a b) -> p a b", a=2), PA[0:64, :, :], ACT.Copy).then_inc(s_dA, 1)
            act.activation(Sw[:, 0:WIN], PB[0:64, 0, :], ACT.Copy).then_inc(s_dA, 1)
            act.wait_ge(s_dV, DV_CMAX)
            act.activation(Sc0[:, 0:63], PB[0:64, 1, 0:63], ACT.Exp, bias=dsm[:, 0:1], accum_out=dsm[:, 1:2])\
                .then_inc(s_dA, 1)
            act.wait_ge(s_dV, DV_WMAX)
            act.activation(Sw[:, 0:WIN + 1], Sw[:, 0:WIN + 1], ACT.Exp, bias=dsm[:, 4:5], accum_out=dsm[:, 5:6])\
                .then_inc(s_dA, 1)
            act.wait_ge(s_dV, DV_SMAX)
            act.activation(Ss[:, 0:PAST + 1], Ss[:, 0:PAST + 1], ACT.Exp, bias=dsm[:, 8:9], accum_out=dsm[:, 9:10])\
                .then_inc(s_dA, 1)
            act.wait_ge(s_dP, DP_PT)
            act.activation(PT[:, 0:512], PR[:, 0, :], ACT.Copy).then_inc(s_dA, 1)
            act.wait_ge(s_cV, 3)
            act.activation(Pc, Pc, ACT.Exp).then_inc(s_cX, 1)
            for i in range(NS + 2, NS + 5):
                window_load(i)
            for t in range(CT):
                act.wait_ge(s_tv, TV_XC + t)
                if t == 2:
                    window_load(NS + 5)
                if t >= 2:
                    act.wait_ge(s_tp, t)
                act.activation(sq[t % 2][:, :], yC[:, t, :], ACT.Square).then_inc(s_ta, 1)
            act.wait_ge(s_tp, 1 + CT)
            act.activation(rb[:, :].rearrange("p (a b) -> p a b", a=2), PB[:, :, 0:HT], ACT.Sqrt, bias=epsc[:, :])\
                .then_inc(s_ta, 1)
            window_load(NS + 6)
            act.wait_ge(s_cT, 1)
            act.activation(PcT[:, :, :].rearrange("p c (i q) -> p i c q", i=QT),
                           PR[:, :, :].rearrange("p a (i c q) -> p (a i) c q", i=2, c=2), ACT.Copy).then_inc(s_cE, 1)
            window_load(NS + 7)
            for t in range(CT):
                act.wait_ge(s_tv, TV_NRM + t)
                if t >= 2:
                    act.wait_ge(s_tv, TV_NRM + CT + t - 2)
                act.activation(sq[t % 2][:, :], yC[:, t, :], ACT.Silu, scale=vec[:, V_LG + t:V_LG + t + 1],
                               bias=vec[:, V_LB + t:V_LB + t + 1]).then_inc(s_ta, 1)
                act.wait_ge(s_ta, CT + 2 + 2 * t)
                act.activation(actH[t], sq[t % 2][:, :], ACT.Copy).then_inc(s_ta, 1)
            act.wait_ge(s_dpv, NS)
            act.activation(od[:, :].rearrange("p (a b) -> p a b", a=2), PA[0:8, :, :], ACT.Copy).then_inc(s_dA, 1)
            act.wait_ge(s_dP, DP_OT)
            for g in range(G):
                h = slice(g * HD, (g + 1) * HD)
                act.activation(oH[h, :, TP:T],
                               PS[h, 0, 0:64].rearrange("p (b g r) -> p g r b", b=NS, g=G)[:, g], ACT.Copy)\
                    .then_inc(s_dA, 1)
            for s in range(N_UNITS + LAG):
                if s < N_UNITS:
                    r, g, br, i = UNITS[s]
                    act.wait_ge(s_mx, s + 1)
                    if s >= 4:
                        act.wait_ge(s_T, s - 3)
                    act.activation(Pb[s % 4][:, 0:(i + 1) * P], PZ[s // 2 % 2][:, s % 2, 0:(i + 1) * P], ACT.Exp,
                                   bias=smx[:, s:s + 1], accum_out=sms[:, s:s + 1]).then_inc(s_ex, 1)
                if s >= LAG:
                    u = s - LAG
                    r, g, br, i = UNITS[u]
                    act.wait_ge(s_T, u + 1)
                    if u >= 2:
                        act.wait_ge(s_pv, u - 1)
                    act.activation(PTb[u % 2][:, 0:(i + 1) * P], PR[:, u % 2, 0:(i + 1) * P], ACT.Copy)\
                        .then_inc(s_ev, 1)
                if s >= 20 and s % 16 == 4 and s < N_UNITS:
                    rr = s // 16 - 1
                    act.wait_ge(s_pv, 16 * (rr + 1))
                    act.activation(actH[CT + rr][:, 0:TP], PS[:, rr % 2, :], ACT.Copy).then_inc(s_oh, 1)
            act.wait_ge(s_pv, N_UNITS)
            act.activation(actH[KT - 1][:, 0:TP], PS[:, 1, :], ACT.Copy).then_inc(s_oh, 1)
            for k in range(KT):
                act.wait_ge(s_grp, N_Z + k + 1)
                act.wait_ge(s_st, KT + k - 1)
                act.activation(sq[k % 2][:, :].rearrange("p (a b) -> p a b", a=2), PZ[k % 2][:, :, 0:HT], ACT.Square)\
                    .then_inc(s_sq, 1)
            root(1)
            for k in range(KT):
                act.wait_ge(s_res, k + 1)
                act.activation(actH[k], xT[:, k, :], ACT.Copy, scale=vec[:, V_GPRE2 + k:V_GPRE2 + k + 1])\
                    .then_inc(s_nh, 1)
            squares(2, xT)
            with act.Fori(0, 2) as fh:
                with act.Fori(0, 4) as j:
                    for c in range(4):
                        f = 16 * fh + 4 * j + c
                        act.wait_ge(s_evt, 8 + 24 * fh + 4 * j + c + 1)
                        act.wait_ge(s_hl, f + 1)
                        act.activation(h2[c % 2][:, :], rl[c % 2][:, :], ACT.Square).then_inc(s_h2, 1)
                        act.wait_ge(s_h2, f + 1)
                        act.activation(hH[:, bass.ds(4 * j + c, 1), :].rearrange("p o t -> p (o t)"),
                                       h2[c % 2][:, :], ACT.Copy).then_inc(s_hh, 1)
            act.wait_ge(s_hl, 34)
            fsq = [rl0, h21, h20, h21, h20, h21, sq[0], sq[1]]
            for k in range(KT):
                act.wait_ge(s_evt, 8 + 48 - 8 + k + 1)
                if 3 <= k < 6:
                    act.wait_ge(s_acc, k - 2)
                act.activation(fsq[k][:, :], fs[:, k, :], ACT.Square).then_inc(s_fsq, 1)
                act.activation(fs[:, k, :], fs[:, k, :], ACT.Copy, scale=vec[:, V_GPOST2 + k:V_GPOST2 + k + 1])\
                    .then_inc(s_fg, 1)
            act.wait_ge(s_r, 3)
            act.activation(rb[:, :], rb[:, :], ACT.Sqrt, bias=epsc[:, :]).then_inc(s_std, 1)

        @block.vector
        def _(dve):
            def chain(ins, sm, n):
                ins.then_inc(sm, 1)
                dve.wait_ge(sm, n)

            def rinv(norm):
                dve.wait_ge(s_std, norm + 1)
                dve.reciprocal(rb[:, :], rb[:, :]).then_inc(s_rinv, 1)
                dve.wait_ge(s_rinv, norm + 1)

            def norm_lo(k):
                dve.wait_ge(s_nh, k + 1)
                dve.tensor_tensor(actL[k], sq[k % 2][:, :], actH[k].bitcast(F32), ALU.subtract).then_inc(s_nl, 1)

            dve.wait_ge(s_vec, 32)
            for i, X in enumerate((XH[0], XH[1], XL[0], XL[1])):
                ins = dve.memset(X[:, :, 256:XW].bitcast(U32), 0)
                ins.then_inc(s_pei if i < 2 else s_pel, 1)

            dve.wait_ge(s_whi, 1)
            dve.tensor_tensor(wL[0][:, :], wraw[0][:, :], wH[0][:, :].bitcast(F32), ALU.subtract).then_inc(s_split, 1)

            def cmp_out_evac(u):
                kv, pr = divmod(u, 4)
                dve.wait_ge(s_w2m, u + 1)
                dst = vcS[:, pr, :] if kv else kcS[:, pr * P:(pr + 1) * P]
                dve.tensor_copy(dst, PS[:, u % 2, 0:P]).then_inc(s_w2e, 1)

            for u in range(8):
                kv, pr = divmod(u, 4)
                if pr == 0:
                    dve.wait_ge(s_pel, 2)
                    dve.wait_ge(s_pe, kv + 1)
                    dve.tensor_tensor(XL[u % 2][:, :, 256:258], vec[:, V_PE + 16 * kv:V_PE + 16 * kv + 16]
                                      .rearrange("p (a j) -> p j a", a=2), XH[u % 2][:, :, 256:258].bitcast(F32),
                                      ALU.subtract).then_inc(s_pec, 1)
                for i in range(4):
                    c = slice(2 * i, 2 * i + 2)
                    dve.wait_ge(s_xh, 4 * u + i + 1)
                    dve.tensor_tensor(XL[u % 2][:, c, 0:256], PR[:, i % 2, :].rearrange("p (j n) -> p j n", j=2),
                                      XH[u % 2][:, c, 0:256].bitcast(F32), ALU.subtract).then_inc(s_xl, 1)
                if pr == 1:
                    dve.wait_ge(s_cmm, u)
                    dve.tensor_tensor(biasc[:, kv:kv + 1], PA[:, (u - 1) % 2, 256:257],
                                      vec[:, V_B1 + kv:V_B1 + kv + 1], ALU.add).then_inc(s_bias, 1)
                if u == 5:
                    rinv(0)
                if u >= 6:
                    for k in range(3 * (u - 6), 3 * (u - 5)):
                        if k >= 2:
                            dve.wait_ge(s_nl, k - 1)
                        dve.scalar_tensor_tensor(out=sq[k % 2][:, :], in0=xT[:, k, :],
                                                 scalar=vec[:, V_GPRE + k:V_GPRE + k + 1], in1=rb[:, :],
                                                 op0=ALU.mult, op1=ALU.mult).then_inc(s_nt, 1)
                        if k >= 1:
                            norm_lo(k - 1)
                if u >= 2:
                    cmp_out_evac(u - 2)
            cmp_out_evac(6)
            for k in (6, 7):
                dve.wait_ge(s_nl, k - 1)
                dve.scalar_tensor_tensor(out=sq[k % 2][:, :], in0=xT[:, k, :], scalar=vec[:, V_GPRE + k:V_GPRE + k + 1],
                                         in1=rb[:, :], op0=ALU.mult, op1=ALU.mult).then_inc(s_nt, 1)
                norm_lo(k - 1)
            norm_lo(KT - 1)
            cmp_out_evac(7)
            dve.wait_ge(s_cst, 32)
            dve.tensor_copy(identb[:, :], ident[:, :]).then_inc(s_initd, 1)
            dve.tensor_copy(maskb[:, :], C(C_MASK, P)).then_inc(s_initd, 1)
            dve.wait_ge(s_init2, 3)
            dve.wait_ge(s_us, 16)

            taps_done = [0] * CT
            steps = [0]
            last = {}

            def conv(t, n):
                for _ in range(n):
                    k = taps_done[t]
                    if k == TAPS:
                        return
                    taps_done[t] += 1
                    w = vec[:, V_CW + t * TAPS + k:V_CW + t * TAPS + k + 1]
                    for hf in range(2):
                        c0 = hf * 256
                        src, dst = uP[:, t, k + c0:k + c0 + 256], yC[:, t, c0:c0 + 256]
                        if k == 0:
                            ins = dve.tensor_scalar(dst, src, w, vec[:, V_CB + t:V_CB + t + 1], ALU.mult, ALU.add)
                        else:
                            dve.wait_ge(s_tap, last[t, hf])
                            ins = dve.scalar_tensor_tensor(out=dst, in0=src, scalar=w, in1=dst, op0=ALU.mult,
                                                           op1=ALU.add)
                        ins.then_inc(s_tap, 1)
                        steps[0] += 1
                        last[t, hf] = steps[0]

            def conv_some(n):
                for _ in range(n):
                    left = [t for t in range(CT) if taps_done[t] < TAPS]
                    if left:
                        conv(left[0], 1)

            nrope = [0]

            def rope(z):
                j = nrope[0]
                nrope[0] += 1
                dve.wait_ge(s_z, z + 1)
                if j >= 1:
                    dve.wait_ge(s_rope, j)
                dve.tensor_tensor(t1[:, :], zr[z % 3][:, :], C(C_COS, T), ALU.mult).then_inc(s_t1, 1)
                dve.wait_ge(s_rot, j + 1)
                dve.tensor_tensor(t2[:, :].rearrange("p (a b) -> p a b", a=2), PR[:, :, 0:HT],
                                  C(C_SIN, T).rearrange("p (a b) -> p a b", a=2), ALU.mult).then_inc(s_rot2, 1)
                dve.wait_ge(s_t1, j + 1)
                dve.wait_ge(s_rot2, j + 1)
                if j < 3:
                    if j == 2:
                        dve.wait_ge(s_tok, 1)
                        dve.wait_ge(s_xp, 8)
                    dst = kf[j % 2][:, :]
                else:
                    dst = qT[:, j - 3, :]
                dve.tensor_tensor(dst, t1[:, :], t2[:, :], ALU.add).then_inc(s_rope, 1)

            def tok_evac_s(c):
                dve.wait_ge(s_tok, c + 1)
                dst = vtok[0:NS, (c - 3) // 2] if c in (3, 5) else ktok[0:NS, TOKSLOT[c]]
                dve.tensor_copy(dst[:, QT, :], PS[0:NS, 1, 0:P]).then_inc(s_tokD, 1)

            for n in range(N_Z + 2):
                if n < 8:
                    if n % 2 == 1:
                        t = n // 2
                        dve.wait_ge(s_grp, n + 1)
                        dve.wait_ge(s_sig, t + 1)
                        dve.tensor_tensor(uP[:, t, TAPS - 1:TAPS - 1 + HT], PB[:, 0, 0:HT], sg[:, 0:HT], ALU.mult)\
                            .then_inc(s_u, 1)
                        dve.tensor_tensor(uP[:, t, TAPS - 1 + HT:TAPS - 1 + TP], PB[:, 1, 0:TP - HT], sg[:, HT:TP],
                                          ALU.mult).then_inc(s_u, 1)
                        dve.tensor_tensor(uS[:, t, :, TAPS - 1], PB[:, 1, TP - HT:HT], sg[:, TP:T], ALU.mult)\
                            .then_inc(s_u, 1)
                        dve.wait_ge(s_u, 3 * (t + 1))
                        conv(t, 12)
                else:
                    z = n - 8
                    if 1 <= z <= 10 and ROPE[z - 1]:
                        rope(z - 1)
                    if 2 <= z < 8:
                        tok_evac_s(z - 2)
                    if z < 9:
                        conv(z // 3, 5)
            dve.wait_ge(s_gtt, 1)
            dve.tensor_copy(gtok[:, 0:QT, :], PS[:, 0, 0:96].rearrange("p (t j) -> p t j", t=QT)).then_inc(s_gtk, 1)
            dve.tensor_copy(gtok[0:NS, QT, :], PS[0:NS, 0, 96:120]).then_inc(s_gtk, 1)

            dve.wait_ge(s_rope, 7)
            dve.wait_ge(s_w2m, 9)
            for g in range(G):
                h = slice(g * HD, (g + 1) * HD)
                dve.tensor_copy(kcBD[h, g * 32:(g + 1) * 32], PS[h, 0, g * 32:(g + 1) * 32]).then_inc(s_w2e, 1)
            dve.wait_ge(s_w2m, 10)
            for rr in range(2):
                for g in range(G):
                    h = slice(rr * 64 + g * 32, rr * 64 + (g + 1) * 32)
                    dve.tensor_copy(vcBD[h, rr, g * HD:(g + 1) * HD], PS[h, 1, 0:HD]).then_inc(s_w2e, 1)
            dve.wait_ge(s_tokst, 16 * 10)
            dve.wait_ge(s_kcd, 32)

            def keys_evac(b):
                if b >= 2:
                    dve.wait_ge(s_sc, b - 1)
                dve.wait_ge(s_kt, 3 * b + 2)
                dve.tensor_copy(KTb[b % 2][:, 512:1024], PR[:, 1, :]).then_inc(s_ktD, 1)

            keys_evac(0)
            dve.memset(Qc[:, :], 0.0).then_inc(s_q, 1)
            dve.memset(Qpad[:, :], 0.0).then_inc(s_q, 1)
            dve.wait_ge(s_q, 2)
            for g in range(G):
                h = slice(g * HD, (g + 1) * HD)
                src = qT[h, :, TP:T]
                dve.tensor_copy(Qc[h, :].rearrange("p (b g r) -> p g r b", b=NS, g=G)[:, g], src).then_inc(s_q, 1)
                dve.tensor_copy(Qpad[h, :].rearrange("p (b s) -> p s b", b=NS)[:, g * R:(g + 1) * R, :], src)\
                    .then_inc(s_q, 1)
            for b in range(1, NS):
                keys_evac(b)
                conv_some(4)
            nv = [0]

            def v(ins):
                ins.then_inc(s_dV, 1)
                nv[0] += 1
                dve.wait_ge(s_dV, nv[0])

            dve.wait_ge(s_sc, NS + 1)
            v(dve.tensor_reduce(dsm[:, 0:1], PB[0:64, 1, 0:63], AX.X, ALU.max, negate=True))
            assert nv[0] == DV_CMAX
            v(dve.tensor_tensor(tg[:, :], PS[0:64, 1, 16:40], C(C_HM, 24, 0, 64), ALU.mult))
            v(dve.tensor_reduce(gB[:, 0:3], tg[:, :].rearrange("p (c h) -> p c h", c=3), AX.X, ALU.add))
            for bi, S_, col in ((0, Ss, PAST), (1, Sw, WIN)):
                v(dve.tensor_tensor(nw[:, bi, :], PS[0:64, 1, bi * 8:bi * 8 + 8], C(C_BM, 8, 0, 64), ALU.mult))
                v(dve.tensor_reduce(S_[:, col:col + 1], nw[:, bi, :], AX.X, ALU.add))
            dve.wait_ge(s_dA, 2)
            v(dve.tensor_reduce(dsm[:, 4:5], Sw[:, 0:WIN + 1], AX.X, ALU.max, negate=True))
            assert nv[0] == DV_WMAX
            dve.wait_ge(s_dA, 3)
            v(dve.tensor_scalar_max(dsm[:, 2:3], dsm[:, 1:2], 1e-30))
            v(dve.reciprocal(dsm[:, 3:4], dsm[:, 2:3]))
            v(dve.memset(Sc0[:, 63:64], 0.0))
            v(dve.tensor_scalar(Sc0[:, 0:63], Sc0[:, 0:63], dsm[:, 3:4], None, ALU.mult))
            assert nv[0] == DV_PN
            dve.wait_ge(s_dP, DP_PN)
            v(dve.tensor_copy(pnT[:, :], PR[0:64, 0, 0:64]))
            dve.wait_ge(s_dP, DP_IM1)
            v(dve.tensor_copy(im1[:, :], PR[0:64, 1, 0:16]))
            dve.wait_ge(s_dP, DP_IM2)
            v(dve.tensor_copy(im2[:, :], PR[0:64, 0, 64:80]))
            v(dve.tensor_reduce(dsm[:, 12:13], im2[:, 1:15], AX.X, ALU.min))
            v(dve.tensor_scalar(tj[:, :], im2[:, 1:15], dsm[:, 12:13], None, ALU.is_le))
            v(dve.tensor_tensor(tj[:, :], tj[:, :], C(C_J, 14, 0, 64), ALU.mult))
            v(dve.tensor_reduce(dsm[:, 13:14], tj[:, :], AX.X, ALU.max))
            v(dve.memset(sb0[:, :], 0.0))
            v(dve.tensor_scalar(sb0[:, 1:15], C(C_J, 14, 0, 64), dsm[:, 13:14], NEG, ALU.is_equal, ALU.mult))
            Ss4 = Ss[:, 0:PAST].rearrange("p (r k c) -> p r k c", r=8, k=NBLK)
            bias4 = sb0[:, :].unsqueeze(1).unsqueeze(3).broadcast_to([64, 8, NBLK, 8])
            v(dve.tensor_tensor(Ss4, Ss4, bias4, ALU.add))
            v(dve.tensor_reduce(dsm[:, 8:9], Ss[:, 0:PAST + 1], AX.X, ALU.max, negate=True))
            assert nv[0] == DV_SMAX
            for a_ in range(2):
                v(dve.tensor_scalar(Pd[:, a_, :], Sc0[:, :], gB[:, 0:1], C(C_PAR + a_, 1, 0, 64), ALU.mult, ALU.mult))
            for bi, S_, n_, o, na in ((1, Sw, WIN, 4, 4), (0, Ss, PAST, 8, 5)):
                dve.wait_ge(s_dA, na)
                v(dve.tensor_scalar_max(dsm[:, o + 2:o + 3], dsm[:, o + 1:o + 2], 1e-30))
                v(dve.reciprocal(dsm[:, o + 3:o + 4], dsm[:, o + 2:o + 3]))
                v(dve.tensor_scalar(S_[:, 0:n_ + 1], S_[:, 0:n_ + 1], dsm[:, o + 3:o + 4], gB[:, 1 + bi:2 + bi],
                                    ALU.mult, ALU.mult))
                v(dve.tensor_scalar(nw[:, bi, :], C(C_BM, 8, 0, 64), S_[:, n_:n_ + 1], None, ALU.mult))
            assert nv[0] == DV_P
            dve.wait_ge(s_dP, DP_PT)
            v(dve.tensor_copy(PT[:, 512:832], PR[:, 1, 0:320]))
            v(dve.tensor_copy(PTn[:, :], PS[0:8, 0, 0:128]))
            conv_some(TAPS * CT)
            for t in range(CT):
                w = vec[:, V_CW + t * TAPS:V_CW + (t + 1) * TAPS].unsqueeze(1).broadcast_to([P, NS, TAPS])
                dve.tensor_tensor(ctmp[:, t], uS[:, t, :, :], w, ALU.mult).then_inc(s_ys, 1)
            dve.wait_ge(s_ys, CT)
            dve.tensor_reduce(yC[:, :, TP:T], ctmp[:, :, :, :], AX.X, ALU.add).then_inc(s_ys, 1)
            dve.wait_ge(s_ys, CT + 1)
            dve.tensor_tensor(yC[:, :, TP:T], yC[:, :, TP:T],
                              vec[:, V_CB:V_CB + CT].unsqueeze(2).broadcast_to([P, CT, NS]), ALU.add).then_inc(s_ys, 1)
            tv = [0]

            def tvi(ins, wait=True):
                ins.then_inc(s_tv, 1)
                tv[0] += 1
                if wait:
                    dve.wait_ge(s_tv, tv[0])

            dve.wait_ge(s_tap, 2 * TAPS * CT)
            dve.wait_ge(s_ys, CT + 2)
            tvi(dve.tensor_tensor(ysm[:, :], yC[:, 0, :], yC[:, 1, :], ALU.add))
            tvi(dve.tensor_tensor(ysm[:, :], ysm[:, :], yC[:, 2, :], ALU.add))
            tvi(dve.tensor_tensor(ysm[:, :], ysm[:, :], yC[:, 3, :], ALU.add))
            assert tv[0] == TV_SUM
            nc_ = [0]

            def cv(ins):
                ins.then_inc(s_cV, 1)
                nc_[0] += 1
                dve.wait_ge(s_cV, nc_[0])

            p4 = Pc.rearrange("p (i h n) -> p i h n", i=QT, h=NH)
            p3 = Pc.rearrange("p (h n) -> p h n", n=32)
            vis, visb = (C(c, 128).rearrange("p (i n) -> p i n", i=QT).unsqueeze(2).broadcast_to([P, QT, NH, 32])
                         for c in (C_VIS, C_VISB))
            cmx = smc[:, :, :].rearrange("p i h -> p (i h)")
            csum, cinv = smx[:, 0:32], sms[:, 0:32]
            dve.wait_ge(s_cS, 1)
            cv(dve.tensor_tensor(p4, PR[:, :, :].rearrange("p a (i h n) -> p (a i) h n", i=2, h=NH), visb, ALU.add))
            cv(dve.tensor_reduce(cmx, p3, AX.X, ALU.max))
            cv(dve.tensor_tensor(p3, p3, cmx.unsqueeze(2).broadcast_to([P, 32, 32]), ALU.subtract))
            dve.wait_ge(s_tp, 1)
            for t in range(CT):
                y3 = yC[:, t, :].rearrange("p (a b) -> p a b", a=2)
                tvi(dve.tensor_tensor(y3, y3, PB[:, :, 0:HT], ALU.subtract), wait=False)
            assert tv[0] == TV_XC - 1 + CT
            dve.wait_ge(s_cX, 1)
            cv(dve.tensor_tensor(p4, p4, vis, ALU.mult))
            cv(dve.tensor_reduce(csum, p3, AX.X, ALU.add))
            cv(dve.tensor_scalar_max(csum, csum, 1e-30))
            cv(dve.reciprocal(cinv, csum))
            for g in range(G):
                cinv_g = cinv.rearrange("p (i r g) -> p i r g", i=QT, r=R)[:, :, :, g]
                cv(dve.tensor_tensor(cinv_g, cinv_g, gtok[:, 0:QT, g * R:(g + 1) * R], ALU.mult))
            cv(dve.tensor_tensor(p3, p3, cinv.unsqueeze(2).broadcast_to([P, 32, 32]), ALU.mult))
            assert nc_[0] == PC_DONE
            dve.wait_ge(s_ta, CT + 1)
            tvi(dve.reciprocal(rb[:, :], rb[:, :]))
            for t in range(CT):
                tvi(dve.tensor_tensor(yC[:, t, :], yC[:, t, :], rb[:, :], ALU.mult), wait=False)
            assert tv[0] == TV_NRM - 1 + CT
            for t in range(CT):
                dve.wait_ge(s_ta, CT + 1 + 2 * (t + 1))
                tvi(dve.tensor_tensor(actL[t], sq[t % 2][:, :], actH[t].bitcast(F32), ALU.subtract), wait=False)
            dve.wait_ge(s_dA, 9)
            for g in range(G):
                h = slice(g * HD, (g + 1) * HD)
                v(dve.tensor_tensor(oL[h, :, TP:T],
                                    PS[h, 0, 0:64].rearrange("p (b g r) -> p g r b", b=NS, g=G)[:, g],
                                    oH[h, :, TP:T].bitcast(F32), ALU.subtract))
            for s in range(N_UNITS + 1):
                if s < N_UNITS:
                    r, g, br, i = UNITS[s]
                    dve.wait_ge(s_S, s + 1)
                    dve.tensor_reduce(smx[:, s:s + 1], PZ[s // 2 % 2][:, s % 2, 0:(i + 1) * P], AX.X, ALU.max,
                                      negate=True).then_inc(s_mx, 1)
                if s >= 1:
                    u = s - 1
                    r, g, br, i = UNITS[u]
                    dve.wait_ge(s_ex, u + 1)
                    dve.tensor_scalar_max(sms[:, u:u + 1], sms[:, u:u + 1], 1e-30).then_inc(s_sm, 1)
                    dve.wait_ge(s_sm, 2 * u + 1)
                    dve.reciprocal(smr[:, u:u + 1], sms[:, u:u + 1]).then_inc(s_sm, 1)
                    dve.wait_ge(s_sm, 2 * u + 2)
                    gc = 8 * (1 + br) + g * R + r
                    dve.tensor_scalar(Pb[u % 4][:, 0:(i + 1) * P], Pb[u % 4][:, 0:(i + 1) * P], smr[:, u:u + 1],
                                      gtok[:, i, gc:gc + 1], ALU.mult, ALU.mult).then_inc(s_pn, 1)
                if s >= 20 and s % 16 == 4 and s < N_UNITS:
                    rr = s // 16 - 1
                    dve.wait_ge(s_oh, rr + 1)
                    dve.tensor_tensor(actL[CT + rr][:, 0:TP], PS[:, rr % 2, :], actH[CT + rr][:, 0:TP].bitcast(F32),
                                      ALU.subtract).then_inc(s_ol, 1)
            dve.wait_ge(s_oh, R)
            dve.tensor_tensor(actL[KT - 1][:, 0:TP], PS[:, 1, :], actH[KT - 1][:, 0:TP].bitcast(F32), ALU.subtract)\
                .then_inc(s_ol, 1)
            for k in range(KT):
                dve.wait_ge(s_grp, N_Z + k + 1)
                dve.wait_ge(s_sq, KT + k + 1)
                dve.tensor_scalar(mixT[:, k, :].rearrange("p (a b) -> p a b", a=2), PZ[k % 2][:, :, 0:HT],
                                  vec[:, V_GPOST + k:V_GPOST + k + 1], None, ALU.mult).then_inc(s_evt, 1)
            dve.wait_ge(s_evt, KT)
            rinv(1)
            for k in range(KT + 1):
                if k < KT:
                    dve.tensor_tensor(mixT[:, k, :], mixT[:, k, :], rb[:, :], ALU.mult).then_inc(s_scaled, 1)
                if k >= 1:
                    dve.wait_ge(s_nh, KT + k)
                    dve.scalar_tensor_tensor(out=actL[k - 1], in0=xT[:, k - 1, :],
                                             scalar=vec[:, V_GPRE2 + k - 1:V_GPRE2 + k],
                                             in1=actH[k - 1].bitcast(F32), op0=ALU.mult, op1=ALU.subtract)\
                        .then_inc(s_nl, 1)
            dve.wait_ge(s_out, 16 * 4)
            dve.wait_ge(s_nl, 2 * KT)
            for hf in range(2):
                dve.memset(fs[:, 4 * hf:4 * hf + 4, :], 0.0).then_inc(s_hl, 1)
            dve.wait_ge(s_hl, 2)
            GB = 26
            for fh in range(2):
                with dve.Fori(0, 4) as j:
                    for c in range(4):
                        dve.wait_ge(s_grp, GB + 32 * fh + 4 * j + c + 1)
                        dve.tensor_scalar(rl[c % 2][:, :].rearrange("p (a b) -> p a b", a=2), PZ[c % 2][:, :, 0:HT],
                                          0.0, None, ALU.max).then_inc(s_evt, 1)
                        dve.wait_ge(s_hh, 16 * fh + 4 * j + c + 1)
                        dve.tensor_tensor(hL[:, bass.ds(4 * j + c, 1), :].rearrange("p o t -> p (o t)"),
                                          h2[c % 2][:, :],
                                          hH[:, bass.ds(4 * j + c, 1), :].rearrange("p o t -> p (o t)").bitcast(F32),
                                          ALU.subtract).then_inc(s_hl, 1)
                if fh == 0:
                    dve.wait_ge(s_std, 3)
                    dve.tensor_tensor(r4[:, :], rb[:, :], rb[:, :], ALU.mult).then_inc(s_r, 1)
                    dve.wait_ge(s_r, 1)
                    dve.reciprocal(r2[:, :], r4[:, :]).then_inc(s_r, 1)
                    dve.wait_ge(s_r, 2)
                    dve.tensor_tensor(r4[:, :], r2[:, :], r2[:, :], ALU.mult).then_inc(s_rinv, 1)
                    dve.wait_ge(s_rinv, 3)
                with dve.Fori(0, 4) as mp:
                    dve.wait_ge(s_evt, 24 * fh + 24)
                    for c in range(2):
                        dve.wait_ge(s_grp, GB + 32 * fh + 16 + 4 * mp + 2 + c + 1)
                        f3 = fs[:, bass.ds(2 * mp + c, 1), :].rearrange("p o (a b) -> p (o a) b", a=2)
                        dve.tensor_tensor(f3, f3, PZ[c % 2][:, :, 0:HT], ALU.add).then_inc(s_evt, 1)
            dve.wait_ge(s_evt, 8 + 48)
            dve.wait_ge(s_st, 3 * KT + 1)
            dve.tensor_tensor(rb[:, :].rearrange("p (a b) -> p a b", a=2), PS[:, :, 0:HT],
                              r4[:, :].rearrange("p (a b) -> p a b", a=2), ALU.mult).then_inc(s_r, 1)
            rinv(3)
            dve.tensor_tensor(rb[:, :], rb[:, :], r2[:, :], ALU.mult).then_inc(s_r, 1)
            dve.wait_ge(s_r, 4)
            dve.wait_ge(s_fg, KT)
            for j in range(len(Y_DVE) + 1):
                if j < len(Y_DVE):
                    k, c = Y_DVE[j]
                    dve.tensor_tensor(fs[:, k, c], fs[:, k, c], rb[:, c], ALU.mult).then_inc(s_ym, 1)
                if j >= 1:
                    k, c = Y_DVE[j - 1]
                    dve.wait_ge(s_ym, j)
                    dve.tensor_tensor(xT[:, k, c], xT[:, k, c], fs[:, k, c], ALU.add).then_inc(s_yd, 1)

        @block.tensor
        def _(pe):
            def feed_tile(n, dst=PS):
                pe.wait_ge(s_sq, n + 1)
                for hf in range(2):
                    mm = pe.matmul(dst[:, hf, 0:HT], ones[:, 0, :], sq[n % 2][:, hf * HT:(hf + 1) * HT],
                                   start=(n % KT == 0), stop=(n % KT == KT - 1))
                mm.then_inc(s_st, 1)

            def group(s, c, pz, src_h, src_l, k0=0, first=True, last=True, nk=KT):
                for hf in range(2):
                    cols = slice(hf * HT, (hf + 1) * HT)
                    for k in range(nk):
                        w = slice(k * 2 * P + c * P, k * 2 * P + (c + 1) * P)
                        for i, (W_, X_) in enumerate(((wH, src_h), (wH, src_l), (wL, src_h))):
                            mm = pe.matmul(pz[:, hf, 0:HT], W_[s][:, w], X_[k0 + k][:, cols],
                                           start=(first and k == 0 and i == 0),
                                           stop=(last and k == nk - 1 and i == 2))
                mm.then_inc(s_grp, 1)

            def first_group(s, pz):
                for k in range(KT):
                    pe.wait_ge(s_nl, KT + k + 1)
                    for i, (W_, X_) in enumerate(((wH, actH), (wH, actL), (wL, actH))):
                        for hf in range(2):
                            mm = pe.matmul(pz[:, hf, 0:HT], W_[s][:, k * 2 * P:k * 2 * P + P],
                                           X_[k][:, hf * HT:(hf + 1) * HT],
                                           start=(k == 0 and i == 0), stop=(k == KT - 1 and i == 2))
                mm.then_inc(s_grp, 1)

            def turn_unit(u):
                pe.wait_ge(s_rc[u % 4], 16 * (u // 4 + 1))
                raw = rawc[u % 4][:, :].rearrange("p (g n) -> p g n", g=G)
                for i in range(4):
                    f = 4 * u + i
                    if f >= 2:
                        pe.wait_ge(s_xl, f - 1)
                    for jj in range(2):
                        for g in range(G):
                            jp = 2 * i + jj
                            mm = pe.transpose(PR[:, f % 2, (jj * 2 + g) * P:(jj * 2 + g + 1) * P],
                                              raw[:, g, jp * P:(jp + 1) * P], ident[:, :])
                    mm.then_inc(s_xt, 1)

            def cmp_mm(u, between=None):
                kv, pr = divmod(u, 4)
                N = 258 if pr == 0 else 256
                s = B_CK + kv
                pe.wait_ge(s_split, s + 1)
                pe.wait_ge(s_xl, 4 * u + 4)
                if pr == 0:
                    pe.wait_ge(s_pec, kv + 1)
                if u >= 2:
                    pe.wait_ge(s_gelu, u - 1)
                for t in range(16):
                    if t == 8 and between is not None:
                        between()
                    w = slice(t * P, (t + 1) * P)
                    sh = t // 8
                    for i, (W_, X_) in enumerate(((wH, XH), (wH, XL), (wL, XH))):
                        mm = pe.matmul(PA[:, u % 2, 0:N], W_[s][:, w], X_[u % 2][:, t % 8, sh:sh + N],
                                       start=(t == 0 and i == 0), stop=(t == 15 and i == 2))
                mm.then_inc(s_cmm, 1)

            def cmp_out(u):
                pe.wait_ge(s_gelu, u + 1)
                if u == 0:
                    pe.wait_ge(s_misc, 48)
                if u >= 2:
                    pe.wait_ge(s_w2e, u - 1)
                h = hc[u % 2]
                for g in range(G):
                    if u < 4:
                        mm = pe.matmul(PS[g * HD:(g + 1) * HD, u % 2, 0:P], w2[:, 0, :], h[:, g * P:(g + 1) * P],
                                       start=True, stop=True)
                    else:
                        mm = pe.matmul(PS[:, u % 2, g * HD:(g + 1) * HD], h[:, g * P:(g + 1) * P], w2[:, 1, :],
                                       start=True, stop=True)
                mm.then_inc(s_w2m, 1)

            pe.wait_ge(s_vec, 32)
            for u in range(9):
                if u < 8:
                    turn_unit(u)
                def feed_two():
                    if u == 2:
                        pe.wait_ge(s_init, 6)
                    feed_tile(2 * u - 4, PB)
                    feed_tile(2 * u - 3, PB)

                if u >= 1:
                    cmp_mm(u - 1, feed_two if 2 <= u < 6 else None)
                if u >= 2:
                    cmp_out(u - 2)

            def rot(z, j):
                pe.wait_ge(s_z, z + 1)
                if j == 0:
                    pe.wait_ge(s_cst, 32)
                else:
                    pe.wait_ge(s_rot2, j)
                if j == 1:
                    pe.wait_ge(s_xp, 8)
                for hf in range(2):
                    mm = pe.matmul(PR[:, hf, 0:HT], C(C_PERM, P), zr[z % 3][:, hf * HT:(hf + 1) * HT],
                                   start=True, stop=True)
                mm.then_inc(s_rot, 1)

            def turn_tok(c):
                if ROPE[c]:
                    j = sum(ROPE[:c])
                    pe.wait_ge(s_rope, j + 1)
                    src = kf[j % 2]
                else:
                    pe.wait_ge(s_z, c + 1)
                    src = zr[c % 3]
                if c >= 1:
                    pe.wait_ge(s_tokA, c)
                    pe.wait_ge(s_tokD, c)
                for t in range(QT):
                    pe.transpose(PS[:, 0, t * P:(t + 1) * P], src[:, t * P:(t + 1) * P], ident[:, :])
                pe.transpose(PS[0:NS, 1, 0:P], src[:, TP:T], ident[:, :]).then_inc(s_tok, 1)

            pe.wait_ge(s_nl, KT)
            for n in range(N_Z):
                b, c = B_IN + n // 2, n % 2
                pe.wait_ge(s_split, SPLITS(b))
                if n == 0:
                    pe.wait_ge(s_gelu, 8)
                if 2 <= n < 10:
                    if n % 2 == 0:
                        pe.wait_ge(s_sig, (n - 2) // 2 + 1)
                    else:
                        pe.wait_ge(s_u, 3 * ((n - 2) // 2 + 1))
                elif n >= 10:
                    pe.wait_ge(s_z, n - 2 - 8 + 1)
                group(b % 2, c, PZ[n % 2], actH, actL)
                if n == 0:
                    cmp_out(7)
                z = n - 8
                if z >= 1 and ROPE[z - 1]:
                    rot(z - 1, sum(ROPE[:z - 1]))
                if z == 2:
                    pe.wait_ge(s_rope, 1)
                    pe.wait_ge(s_z, 2)
                    for kv, src in enumerate((kf[0], zr[1])):
                        mm = pe.matmul(PR[:, kv, :], swap[:, :], src[:, 0:TP], start=True, stop=True)
                    mm.then_inc(s_swp, 1)
                if 2 <= z < 8:
                    turn_tok(z - 2)
            pe.wait_ge(s_wgs, 2)
            pe.wait_ge(s_z, 9)
            for hf in range(2):
                for k in range(KT):
                    for i, (W_, X_) in enumerate(((wgH, actH), (wgH, actL), (wgL, actH))):
                        mm = pe.matmul(PA[0:24, hf, 0:HT], W_[:, k * 24:(k + 1) * 24],
                                       X_[k][:, hf * HT:(hf + 1) * HT],
                                       start=(k == 0 and i == 0), stop=(k == KT - 1 and i == 2))
            mm.then_inc(s_gmm, 1)
            rot(9, 6)
            pe.wait_ge(s_gt, 1)
            pe.wait_ge(s_tokA, 6)
            pe.wait_ge(s_tokD, 6)
            for t in range(QT):
                pe.transpose(PS[:, 0, t * 24:(t + 1) * 24], gT[:, t * P:(t + 1) * P], ident[0:24, 0:24])
            pe.transpose(PS[0:NS, 0, 96:120], gT[:, TP:T], ident[0:24, 0:24]).then_inc(s_gtt, 1)

            pe.wait_ge(s_rope, 7)
            for kv in range(2):
                s = (B_PK + kv) % 2
                pe.wait_ge(s_raw[s], 16 * ((B_PK + kv) // 2 + 1))
                pe.wait_ge(s_xp, 8)
                for t in range(16):
                    sh = t // 8
                    mm = pe.matmul(PA[:, kv, 0:P], wraw[s][:, t * P:(t + 1) * P], XP[:, kv, t % 8, sh:sh + P],
                                   start=(t == 0), stop=(t == 15))
                mm.then_inc(s_pcm, 1)
            pe.wait_ge(s_gtk, 2)
            pe.wait_ge(s_gelu, 9)
            for g in range(G):
                mm = pe.matmul(PS[g * HD:(g + 1) * HD, 0, g * 32:(g + 1) * 32], w2[:, 0, :],
                               hcp[:, 0, g * 32:(g + 1) * 32], start=True, stop=True)
            mm.then_inc(s_w2m, 1)
            pe.wait_ge(s_gelu, 10)
            for rr in range(2):
                mm = pe.matmul(PS[rr * 64:(rr + 1) * 64, 1, 0:HD], hcp[:, 1, 0:64], w2[:, 1, :],
                               start=True, stop=True)
            mm.then_inc(s_w2m, 1)
            def turn_keys(b):
                pe.wait_ge(s_dec[b % 2], 16 * (b // 2 + 1))
                pe.wait_ge(s_win[b % 2], 16 * (b // 2 + 1))
                for q in range(2):
                    if b >= 1:
                        pe.wait_ge(s_ktA if q == 0 else s_ktD, 2 * b - 1 if q == 0 else b)
                    for r in range(4):
                        mm = pe.transpose(PR[:, q, r * P:(r + 1) * P], rks[b % 2][:, (4 * q + r) * P:(4 * q + r + 1) * P],
                                          ident[:, :])
                    mm.then_inc(s_kt, 1)
                if b >= 1:
                    pe.wait_ge(s_ktA, 2 * b)
                for r in range(4):
                    mm = pe.transpose(PS[:, 0, r * P:(r + 1) * P], rkw[b % 2][:, r * P:(r + 1) * P], ident[:, :])
                mm.then_inc(s_kt, 1)

            def key_scores(b):
                pe.wait_ge(s_ktA, 2 * b + 2)
                pe.wait_ge(s_ktD, b + 1)
                if b == 0:
                    pe.wait_ge(s_q, 6)
                q = Qpad[:, b * 64:(b + 1) * 64]
                f, l = b == 0, b == NS - 1
                pe.matmul(PA[0:64, 0, :], q, KTb[b % 2][:, 0:512], start=f, stop=l)
                pe.matmul(PA[0:64, 1, :], q, KTb[b % 2][:, 512:1024], start=f, stop=l)
                pe.matmul(PB[0:64, 0, :], q, KTb[b % 2][:, 1024:1536], start=f, stop=l)
                pe.matmul(PB[0:64, 1, 0:64], q, kcS[:, b * 64:(b + 1) * 64], start=f, stop=l).then_inc(s_sc, 1)

            pe.wait_ge(s_w2e, 14)
            for b in range(NS + 1):
                if b < NS:
                    turn_keys(b)
                if b >= 1:
                    key_scores(b - 1)
            pe.wait_ge(s_kzc, 6)
            for bi in range(2):
                pe.matmul(PS[0:64, 1, bi * 8:bi * 8 + 8], Qc[:, :], knew[:, bi, :], start=True, stop=True)
            pe.matmul(PS[0:64, 1, 16:40], C(C_EB, 64, 0, 8), gtok[0:8, QT, :], start=True, stop=True).then_inc(s_sc, 1)
            pe.wait_ge(s_dV, DV_PN)
            pe.transpose(PR[0:64, 0, 0:64], Sc0[:, :], ident[0:64, 0:64]).then_inc(s_dP, 1)
            pe.wait_ge(s_dV, DV_PN + 1)
            pe.matmul(PR[0:64, 1, 0:16], pnT[:, :], C(C_OV, 16, 0, 64), start=True, stop=True).then_inc(s_dP, 1)
            pe.wait_ge(s_dV, DV_PN + 2)
            pe.matmul(PR[0:64, 0, 64:80], C(C_RS, 64, 0, 64), im1[:, :], start=True, stop=True).then_inc(s_dP, 1)
            pe.wait_ge(s_dV, DV_P)
            for r in range(8):
                pe.transpose(PR[:, 0, r * 64:(r + 1) * 64], Ss[:, r * P:(r + 1) * P], ident[0:64, 0:64])
            for r in range(4):
                pe.transpose(PR[:, 1, r * 64:(r + 1) * 64], Sw[:, r * P:(r + 1) * P], ident[0:64, 0:64])
            pe.transpose(PR[:, 1, 256:320], Pd[:, :, :].rearrange("p a n -> p (a n)"), ident[0:64, 0:64])
            for bi in range(2):
                mm = pe.transpose(PS[0:8, 0, bi * 64:(bi + 1) * 64], nw[:, bi, :], ident[0:64, 0:64])
            mm.then_inc(s_dP, 1)
            pe.wait_ge(s_dA, 6)
            pe.wait_ge(s_dV, DV_P + 2)
            for i in range(QT):
                for r in range(R):
                    mm = pe.matmul(PR[:, i // 2, (i % 2) * 256 + r * 64:(i % 2) * 256 + (r + 1) * 64],
                                   qT[:, r, i * P:(i + 1) * P], kcBD[:, :], start=True, stop=True)
            mm.then_inc(s_cS, 1)
            for b in range(NS):
                i = NS + b
                pe.wait_ge(s_dec[i % 2], 16 * (i // 2 + 1))
                pe.wait_ge(s_win[i % 2], 16 * (i // 2 + 1))
                o = PA[0:8, b // 4, (b % 4) * P:(b % 4 + 1) * P]
                for r in range(8):
                    pe.matmul(o, PT[:, r * 64 + b * 8:r * 64 + b * 8 + 8], rks[i % 2][:, r * P:(r + 1) * P],
                              start=(r == 0), stop=False)
                for r in range(4):
                    pe.matmul(o, PT[:, 512 + r * 64 + b * 8:512 + r * 64 + b * 8 + 8],
                              rkw[i % 2][:, r * P:(r + 1) * P], start=False, stop=False)
                pe.matmul(o, PT[:, 768 + b * 8:768 + b * 8 + 8], vcS[:, b // 2, :], start=False, stop=False)
                for bi in range(2):
                    mm = pe.matmul(o, PTn[0:8, bi * 64 + b * 8:bi * 64 + b * 8 + 8], vtok[0:8, bi, QT, :],
                                   start=False, stop=(bi == 1))
                mm.then_inc(s_dpv, 1)
                if b == 2:
                    pe.wait_ge(s_tv, TV_SUM)
                    for hf in range(2):
                        mm = pe.matmul(PB[:, hf, 0:HT], ones[:, 1, :], ysm[:, hf * HT:(hf + 1) * HT],
                                       start=True, stop=True)
                    mm.then_inc(s_tp, 1)
                if b == 4:
                    pe.wait_ge(s_tv, TV_XC - 1 + CT)
                    for t in range(CT):
                        pe.wait_ge(s_ta, t + 1)
                        for hf in range(2):
                            mm = pe.matmul(PB[:, hf, 0:HT], ones[:, 1, :], sq[t % 2][:, hf * HT:(hf + 1) * HT],
                                           start=(t == 0), stop=(t == CT - 1))
                        mm.then_inc(s_tp, 1)
                if b == 5:
                    pe.wait_ge(s_cV, PC_DONE)
                    for i in range(QT):
                        for rp in range(2):
                            c = (i % 2) * 256 + rp * P
                            mm = pe.transpose(PR[:, i // 2, c:c + P], Pc[:, i * 256 + rp * P:i * 256 + (rp + 1) * P],
                                              ident[:, :])
                    mm.then_inc(s_cT, 1)
            pe.wait_ge(s_dA, 7)
            for b in range(NS):
                mm = pe.transpose(PS[:, 0, b * 8:(b + 1) * 8], od[:, b * P:(b + 1) * P], ident[0:8, 0:8])
            mm.then_inc(s_dP, 1)
            pe.wait_ge(s_cE, 1)
            pe.wait_ge(s_ta, CT + 1)
            pe.wait_ge(s_initd, 2)
            pe.wait_ge(s_dV, DV_P + 4)
            for s in range(N_UNITS + LAG + 1):
                if s < N_UNITS:
                    r, g, br, i = UNITS[s]
                    n = (i + 1) * P
                    if s >= 4:
                        pe.wait_ge(s_ex, s - 3)
                    dst = PZ[s // 2 % 2][:, s % 2, 0:n]
                    pe.matmul(dst, qT[:, r, i * P:(i + 1) * P], kz[:, br, g, 0:n], start=True, stop=True)
                    pe.matmul(dst[:, i * P:n], identb[:, :], maskb[:, :], start=False, stop=True,
                              skip_group_check=True).then_inc(s_S, 1)
                if LAG <= s < N_UNITS + LAG:
                    u = s - LAG
                    r, g, br, i = UNITS[u]
                    pe.wait_ge(s_pn, u + 1)
                    if u >= 2:
                        pe.wait_ge(s_ev, u - 1)
                    for j in range(i + 1):
                        mm = pe.transpose(PR[:, u % 2, j * P:(j + 1) * P], Pb[u % 4][:, j * P:(j + 1) * P], ident[:, :])
                    mm.then_inc(s_T, 1)
                if s > LAG:
                    u = s - LAG - 1
                    r, g, br, i = UNITS[u]
                    if u % 16 == 0:
                        if r >= 2:
                            pe.wait_ge(s_ol, r - 1)
                        pe.matmul(PS[:, r % 2, :], vcBD[:, r % 2, :], PcT[:, r // 2, :], start=True, stop=False,
                                  skip_group_check=True)
                    pe.wait_ge(s_ev, u + 1)
                    for j in range(i + 1):
                        mm = pe.matmul(PS[g * HD:(g + 1) * HD, r % 2, i * P:(i + 1) * P],
                                       vtok[:, br, j, g * HD:(g + 1) * HD], PTb[u % 2][:, j * P:(j + 1) * P],
                                       start=False, stop=(j == i), skip_group_check=True)
                    mm.then_inc(s_pv, 1)
            pe.wait_ge(s_tv, TV_NRM - 1 + 2 * CT)
            pe.wait_ge(s_ol, R)
            pe.wait_ge(s_ex, N_UNITS)
            for k in range(KT):
                b = B_OUT + k // 2
                pe.wait_ge(s_split, SPLITS(b))
                if k >= 2:
                    pe.wait_ge(s_evt, k - 1)
                group(b % 2, k % 2, PZ[k % 2], actH, actL)
                if k >= 1:
                    feed_tile(KT + k - 1)
            feed_tile(2 * KT - 1)
            pe.wait_ge(s_evt, KT)
            hHk, hLk = ([h_[:, k, :] for k in range(16)] for h_ in (hH, hL))
            for fh in range(2):
                for q in range(2):
                    pe.wait_ge(s_split, SPLITS(B_FFN) - 1 + 16 * fh + q + 1)
                    for c in range(2):
                        pe.wait_ge(s_evt, 24 * fh + 2 * q + c + 7)
                        if fh == 0 and q == 0 and c == 0:
                            first_group(B_FFN % 2, PZ[0])
                        else:
                            group((B_FFN + q) % 2, c, PZ[c], actH, actL)
                    if fh == 0 and q == 0:
                        for k in range(KT):
                            feed_tile(2 * KT + k)
                with pe.Fori(1, 4) as j:
                    for q in range(2):
                        pe.wait_ge(s_split, SPLITS(B_FFN) - 1 + 16 * fh + 2 * j + q + 1)
                        for c in range(2):
                            pe.wait_ge(s_evt, 24 * fh + 4 * j + 2 * q + c + 7)
                            group((B_FFN + q) % 2, c, PZ[c], actH, actL)
                with pe.Fori(0, 4) as mp:
                    for q in range(2):
                        s = (B_FFN + q) % 2
                        pe.wait_ge(s_split, SPLITS(B_FFN) - 1 + 16 * fh + 8 + 2 * mp + q + 1)
                        pe.wait_ge(s_hl, 16 * fh + 8 * q + 10)
                        for c in range(2):
                            if q == 0:
                                pe.wait_ge(s_evt, 24 * fh + 16 + 2 * mp + c + 7)
                            group(s, c, PZ[c], hHk, hLk, q * KT, q == 0, q == 1)
            pe.wait_ge(s_std, 3)
            for i, (sm, n, src) in enumerate(((s_acc, 5, rl0), (s_fsq, 7, sq[0]), (s_fsq, 8, sq[1]))):
                pe.wait_ge(sm, n)
                for hf in range(2):
                    mm = pe.matmul(PS[:, hf, 0:HT], ones[:, 0, :], src[:, hf * HT:(hf + 1) * HT],
                                   start=(i == 0), stop=(i == 2))
            mm.then_inc(s_st, 1)


def kernel(**inputs):
    import concourse.bacc as bacc
    from concourse.bass_utils import run_bass_kernel_spmd

    x = {n: np.asarray(v) for n, v in inputs.items()}
    f32 = np.float32

    def tiles(w):
        return w.reshape(-1, P, w.shape[-1]).transpose(1, 0, 2)

    def fm(v):
        return v.reshape(-1, P).T

    def chunks(n):
        return x[n].reshape(-1, STRIDE, G, HD).transpose(0, 2, 1, 3).reshape(-1, STRIDE * P)

    w_in, w_out, w_up, w_down = (x[n][0] for n in ("w_in", "w_out", "w_up", "w_down"))
    blocks = []
    w1s = [x[n][0].reshape(STRIDE, 2, HD, 2 * HD).transpose(1, 2, 0, 3).reshape(P, BW)
           for n in ("cmp_k_w1", "cmp_v_w1")]
    for t in range(CT):
        blocks.append(np.concatenate([w_in[:, CH + P * t:CH + P * (t + 1)], w_in[:, P * t:P * (t + 1)]], 1))
    c1 = 2 * CH + NH * HD
    for t in range(3):
        blocks.append(w_in[:, c1 + 2 * P * t:c1 + 2 * P * (t + 1)])
    q_w = w_in[:, 2 * CH:c1].reshape(D, G, R, HD).transpose(0, 2, 1, 3).reshape(D, NH * HD)
    blocks += [q_w[:, 0:2 * P], q_w[:, 2 * P:]]
    blocks = w1s + [tiles(b).reshape(P, BW) for b in blocks] + w1s
    att = w_out[CH:].reshape(G, R, HD, D).transpose(1, 0, 2, 3).reshape(NH * HD, D)
    w_o = np.concatenate([w_out[:CH], att], 0)
    blocks += [tiles(w_o[:, 2 * P * m:2 * P * (m + 1)]).reshape(P, BW) for m in range(4)]
    for fh in range(2):
        for b in range(8):
            c = fh * 2048 + 2 * P * b
            blocks.append(tiles(w_up[:, c:c + 2 * P]).reshape(P, BW))
        for mp in range(4):
            for q in range(2):
                r = fh * 2048 + q * 1024
                blocks.append(tiles(w_down[r:r + 1024, 2 * P * mp:2 * P * (mp + 1)]).reshape(P, BW))
    wblk = np.stack(blocks)

    pe_ = [x[n][0].reshape(STRIDE, 2, HD).transpose(1, 2, 0).reshape(P, STRIDE) for n in ("cmp_k_pe", "cmp_v_pe")]
    vecs = np.concatenate(
        [fm(x["g_pre_mix"][0]), fm(x["conv_b"][0]), fm(x["conv_ln_g"][0]), fm(x["conv_ln_b"][0]),
         fm(x["g_post_mix"][0]), fm(x["g_pre_ffn"][0]), fm(x["g_post_ffn"][0]),
         x["cmp_k_b1"][0][:, None], x["cmp_v_b1"][0][:, None],
         x["conv_w"][0].reshape(TAPS, CT, P).transpose(2, 1, 0).reshape(P, CT * TAPS)] + pe_, 1)
    wgate = tiles(w_in[:, c1 + 6 * P:]).reshape(P, KT * 24)

    p = np.arange(P)
    pos = np.concatenate([np.arange(TP), np.full(NS, PAST)]).astype(f32)
    inv = np.power(f32(500000.0), -np.arange(8, dtype=f32) * f32(2.0) / f32(16)).astype(f32)
    ang = (pos[None, :] * inv[:, None]).astype(f32)
    cos, sin, perm = np.ones((P, T), f32), np.zeros((P, T), f32), np.zeros((P, P), f32)
    for g in range(G):
        for d in range(16):
            cos[g * HD + d], sin[g * HD + d] = np.cos(ang[d % 8]), np.sin(ang[d % 8])
        for d in range(8):
            perm[g * HD + d + 8, g * HD + d] = -1
            perm[g * HD + d, g * HD + d + 8] = 1
    mask = np.where(p[None, :] <= p[:, None], 0, NEG).astype(f32)
    qpos = (np.arange(QT)[None, :] * P + p[:, None])[:, :, None]
    n32 = np.arange(NCH_P)[None, None, :]
    vis = ((STRIDE * n32 + 31 <= qpos) & (n32 < NCH_P - 1)).reshape(P, QT * NCH_P)
    r64 = np.arange(64)
    i_, j_ = np.arange(NCH_S)[:, None], np.arange(NBLK)[None, :]
    ov = np.maximum(np.minimum(i_ * 16 + 32, (j_ + 1) * 64) - np.maximum(i_ * 16, j_ * 64), 0) // 16 * (i_ < 63)

    def rows(m):
        return np.concatenate([m, np.zeros((P - m.shape[0], m.shape[1]))], 0).astype(f32)

    same = (r64[:, None] // 4 == r64[None, :] // 4)
    consts = np.concatenate(
        [np.eye(P), perm, cos, sin, mask, vis, np.where(vis, 0, NEG),
         rows(r64[:, None] % 8 == np.arange(24)[None, :] % 8), rows(r64[:, None] // 8 == np.arange(8)[None, :]),
         rows(same), rows(np.arange(8)[:, None] == r64[None, :] // 8), rows(ov),
         rows(np.tile(np.arange(1, 15), (64, 1))), np.stack([p % 8, p % 16, p // 8 % 2 == 0, p // 8 % 2 == 1], 1)], 1).astype(f32)
    assert consts.shape == (P, N_C) and vecs.shape == (P, N_VEC)

    xs = np.concatenate([x["x_prompt"][0], x["x_sample"][:, 0]], 0)
    us0 = np.concatenate([x["cache_conv"][0], np.zeros((NS, 1, CH), f32)], 1)
    us0 = us0.reshape(NS, TAPS, CT, P).transpose(3, 2, 0, 1)
    pt = x["page_table"]
    pt_rep = np.stack([pt[2 * pr + p // 64, (p % 64) // 8] for pr in range(4)]
                      + [pt[b, p // STRIDE] for b in range(NS)], 1)
    ins = {"wblk": wblk, "wgate": wgate, "vecs": vecs, "consts": consts, "x_fm": tiles(xs.T), "us0": us0,
           "w2": np.stack([x["cmp_k_w2"][0], x["cmp_v_w2"][0]], 1), "pt_rep": pt_rep,
           "pool_kc": chunks("cache_k_cmp"), "pool_vc": chunks("cache_v_cmp"),
           "pool_ks": x["cache_k_sel"].reshape(-1, 1024), "pool_vs": x["cache_v_sel"].reshape(-1, 1024),
           "cwk": x["cache_k_win"].reshape(NS, WIN, P), "cwv": x["cache_v_win"].reshape(NS, WIN, P)}
    outs = {"y_fm": (P, KT, T), "pconv": (P, CT, TAPS - 1), "sconv": (P, CT, NS, TAPS - 1)}
    for c in range(6):
        outs[f"p_rows{c}"] = (TP, P)
    for c in range(4):
        outs[f"s_rows{c}"] = (NS, P)
    for kv in range(2):
        outs[f"s_win{kv}"] = (NS, WIN, P)

    nc = bacc.Bacc("TRN2", target_bir_lowering=False, num_devices=1)
    arrays, A = {}, {}
    for name, v in ins.items():
        v = np.ascontiguousarray(v)
        arrays[name + "_dram"] = v
        A[name] = nc.dram_tensor(name + "_dram", v.shape, mybir.dt.from_np(v.dtype), kind="ExternalInput").ap()
    for name, shape in outs.items():
        A[name] = nc.dram_tensor(name + "_dram", shape, F32, kind="ExternalOutput").ap()
    for base, n in (("p_rows", 6), ("s_rows", 4), ("s_win", 2)):
        A[base] = [A[f"{base}{i}"] for i in range(n)]
    A["win_rows"] = [A["cwk"], A["cwv"]]
    A["win_k"], A["win_v"] = (A[n].rearrange("b (p r) d -> b p (r d)", r=4) for n in ("cwk", "cwv"))
    hymba_step(nc, A)
    res = run_bass_kernel_spmd(nc, [arrays], core_ids=[0]).results[0]
    res = {name: res[name + "_dram"] for name in outs}

    y = res["y_fm"].transpose(2, 1, 0).reshape(T, D)
    p_new = [res[f"p_rows{c}"].reshape(1, 1, TP, G, HD) for c in range(6)]
    s_new = [res[f"s_rows{c}"].reshape(1, NS, 1, G, HD) for c in range(4)]
    s_win = [res[f"s_win{kv}"].reshape(1, NS, WIN, G, HD) for kv in range(2)]
    pconv = res["pconv"].transpose(2, 1, 0).reshape(1, 1, TAPS - 1, CH)
    sconv = res["sconv"].transpose(2, 3, 1, 0).reshape(1, NS, TAPS - 1, CH)
    return (y[None, :TP], y[TP:, None], *p_new, pconv, *s_new, *s_win, sconv)
```

```python
from contextlib import ExitStack

import numpy as np

import concourse.bass as bass
from concourse import mybir

F32 = mybir.dt.float32
F32R = mybir.dt.float32r
BF16 = mybir.dt.bfloat16
I32 = mybir.dt.int32
U32 = mybir.dt.uint32
ALU = mybir.AluOpType
ACT = mybir.ActivationFunctionType
AX = mybir.AxisListType

P = 128
D = 1024
KT = D // P
TP = 512
NS = 8
T = TP + NS
HT = T // 2
QT = TP // P
CH = 512
CT = CH // P
TAPS = 31
HD = 64
NH = 8
G = 2
R = NH // G
PAST = 1024
PAGE = 128
NPG = PAST // PAGE
WIN = 512
STRIDE = 16
NCH_S = PAST // STRIDE
NCH_P = TP // STRIDE
NBLK = PAST // 64
EPS = 1e-6
NEG = -1e30

B_CK, B_CV, B_IN, B_PK, B_PV, B_OUT, B_FFN = 0, 1, 2, 11, 12, 13, 17
N_BLOCKS = B_FFN + 32
N_Z = 18
BW = KT * 2 * P

V_GPRE, V_CB, V_LG, V_LB, V_GPOST, V_GPRE2, V_GPOST2 = 0, 8, 12, 16, 20, 28, 36
V_B1, V_CW, V_PE = 44, 46, 46 + CT * TAPS
N_VEC = V_PE + 32
C_ID, C_PERM, C_COS, C_SIN = 0, 128, 256, 256 + T
C_MASK = C_SIN + T
C_VIS = C_MASK + 128
C_VISB = C_VIS + 128
C_HM = C_VISB + 128
C_BM = C_HM + 24
C_RS = C_BM + 8
C_EB = C_RS + 64
C_OV = C_EB + 64
C_J = C_OV + 16
C_CI = C_J + 14
C_PAR = C_CI + 2
N_C = C_PAR + 2


ROPE = (1, 0, 1, 0, 1, 0, 1, 1, 1, 1)
TOKSLOT = {0: 0, 1: 1, 2: 2, 4: 3}
UNITS = [(r, g, br, i) for r in range(R) for g in range(G) for br in range(2) for i in range(QT)]
N_UNITS = len(UNITS)
NORM_AT = {5: (0, 1), 6: (2, 3, 4), 7: (5, 6, 7)}
LAG = 3


def SPLITS(b):
    return b + 1 if b < B_PK else b - 1


Y_DVE = [(k, slice(0, T)) for k in range(5)] + [(5, slice(0, HT))]
Y_POOL = [(6, slice(0, T)), (7, slice(0, T)), (5, slice(HT, T))]

DV_CMAX, DV_PN, DV_DROP, DV_SMAX, DV_WMAX, DV_PS, DV_P = 1, 11, 20, 22, 23, 29, 33
DP_PN, DP_IM1, DP_IM2, DP_PTS, DP_PT, DP_OT = 1, 2, 3, 4, 5, 6
PC_DONE = 10
TV_SUM, TV_XC = 3, 4
TV_NRM = TV_XC + CT + 1


def hymba_step(nc, A):
    ctx = ExitStack()
    with ctx:
        def psum(name):
            return ctx.enter_context(nc.psum_tensor(name, [P, 2, 512], F32))

        def sem(name):
            return ctx.enter_context(nc.semaphore(name))

        def region(*groups):
            out, most = {}, 0
            for group in groups:
                size = 0
                with ExitStack() as scope:
                    for name, shape, dt in group:
                        out[name] = scope.enter_context(nc.sbuf_tensor(name, shape, dt))
                        n = int(np.prod(shape[1:])) * (2 if dt == BF16 else 4)
                        size += -(-n // 32) * 32
                most = max(most, size)
            ctx.enter_context(nc.sbuf_tensor("space_of_" + groups[0][0][0], [P, most // 4], F32))
            return out

        def sb(name, shape, dt=F32):
            return ctx.enter_context(nc.sbuf_tensor(name, shape, dt))

        xT = sb("xT", [P, KT, T])
        wraw = [sb(f"wraw{i}", [P, BW]) for i in range(2)]
        wH = [sb(f"wH{i}", [P, BW], F32R) for i in range(2)]
        wL = [sb(f"wL{i}", [P, BW], F32R) for i in range(2)]
        vec = sb("vec", [P, N_VEC])
        ones = sb("ones", [P, 2, P])
        epsc = sb("epsc", [P, 1])
        zero = sb("zero", [P, 1])
        warm = sb("warm", [P, 1])
        ident = sb("ident", [P, P])
        swap = sb("swap", [P, P])
        sq = [sb(f"sq{i}", [P, T]) for i in range(2)]
        rb = sb("rb", [P, T])
        a = region(
            [("cH", [P, CT, T], F32R), ("cL", [P, CT, T], F32R)],
            [("hcp", [P, 2, P], F32), ("ysm", [P, T], F32), ("ctmp", [P, CT, NS, TAPS], F32)],
        )
        b = region(
            [("oH", [P, CT, T], F32R), ("oL", [P, CT, T], F32R)],
            [("rks", [P, 2, 1024], F32), ("rkw", [P, 2, 512], F32), ("od", [NH, 1024], F32)],
        )
        cH, cL, hcp, ysm, ctmp = (a[n] for n in ("cH", "cL", "hcp", "ysm", "ctmp"))
        oH, oL, od = b["oH"], b["oL"], b["od"]
        rks, rkw = ([b[n][:, i, :] for i in range(2)] for n in ("rks", "rkw"))
        actH = [(cH if k < CT else oH)[:, k % CT, :] for k in range(KT)]
        actL = [(cL if k < CT else oL)[:, k % CT, :] for k in range(KT)]
        base = [
            ("cst", [P, N_C - C_PERM], F32), ("identb", [P, P], BF16), ("maskb", [P, P], BF16),
            ("uS", [P, CT, NS, TAPS], F32), ("w2", [P, 2, HD], F32),
            ("biasc", [P, 2], F32), ("kcBD", [P, HD], F32), ("vcBD", [P, 2, P], F32),
            ("kcS", [P, 512], F32), ("vcS", [P, 4, P], F32), ("pt_i", [P, 12], I32), ("idx", [P, 12], U32),
        ]
        mixer = [
            ("uP", [P, CT, TAPS - 1 + TP], F32), ("yC", [P, CT, T], F32),
            ("qT", [P, R, T], F32), ("kz", [P, 2, G, TP], F32), ("knew", [P, 2, NS], F32),
            ("vtok", [P, 2, QT + 1, P], F32), ("gtok", [P, QT + 1, 24], F32),
        ]
        ffn = [("hH", [P, 16, T], F32R), ("hL", [P, 16, T], F32R), ("fs", [P, KT, T], F32),
               ("r2", [P, T], F32),
               ("rl0", [P, T], F32), ("rl1", [P, T], F32), ("h20", [P, T], F32), ("h21", [P, T], F32)]
        inproj = [("sg", [P, T], F32), ("zr0", [P, T], F32), ("zr1", [P, T], F32), ("zr2", [P, T], F32),
                  ("t1", [P, T], F32), ("t2", [P, T], F32), ("kf0", [P, T], F32), ("kf1", [P, T], F32),
                  ("ktok", [P, 4, QT + 1, P], F32), ("gT", [24, T], F32),
                  ("wg", [P, KT * 24], F32), ("wgH", [P, KT * 24], F32R), ("wgL", [P, KT * 24], F32R),
                  ("XP", [P, 2, 8, 130], F32)]
        XW = 260
        cmp_ = [("XH0", [P, KT, XW], F32R), ("XH1", [P, KT, XW], F32R),
                ("XL0", [P, KT, XW], F32R), ("XL1", [P, KT, XW], F32R),
                ("hc0", [P, XW], F32), ("hc1", [P, XW], F32),
                ("rawc0", [P, 2048], F32), ("rawc1", [P, 2048], F32), ("rawc2", [P, 2048], F32),
                ("rawc3", [P, 2048], F32)]
        attn = [("KTb0", [P, 1536], F32), ("KTb1", [P, 1536], F32), ("PT", [P, 832], F32), ("PTn", [8, 128], F32),
                ("Ss", [64, PAST + 8], F32), ("Sw", [64, WIN + 8], F32), ("Pd", [64, 2, 64], F32),
                ("Sc0", [64, 64], F32), ("pnT", [64, 64], F32), ("im1", [64, 16], F32), ("im2", [64, 16], F32),
                ("sb0", [64, 16], F32), ("tj", [64, 14], F32), ("tg", [64, 24], F32), ("gB", [64, 4], F32),
                ("nw", [64, 2, 8], F32), ("dsm", [64, 24], F32),
                ("Qc", [P, 64], F32), ("Qpad", [P, 576], F32),
                ("Pb0", [P, 512], F32), ("Pb1", [P, 512], F32), ("Pb2", [P, 512], F32),
                ("PTb0", [P, 512], F32), ("PTb1", [P, 512], F32),
                ("PcT", [P, 2, TP], F32),
                ("smc", [P, 4, 8], F32), ("smx", [P, 64], F32), ("sms", [P, 64], F32), ("smr", [P, 64], F32)]
        tail = [("mixT", [P, KT, T], F32)]
        out = {}
        with ExitStack() as pre:
            for name, shape, dt in base:
                out[name] = pre.enter_context(nc.sbuf_tensor(name, shape, dt))
            with ExitStack() as scope:
                for name, shape, dt in cmp_:
                    out[name] = scope.enter_context(nc.sbuf_tensor(name, shape, dt))
            for name, shape, dt in mixer:
                out[name] = pre.enter_context(nc.sbuf_tensor(name, shape, dt))
            for group in (inproj, attn, tail):
                with ExitStack() as scope:
                    for name, shape, dt in group:
                        out[name] = scope.enter_context(nc.sbuf_tensor(name, shape, dt))
        for name, shape, dt in ffn:
            out[name] = sb(name, shape, dt)
        (cst, identb, maskb, uS, w2, biasc, kcBD, vcBD, kcS, vcS, pt_i, idx) = (out[n] for n, _, _ in base)
        (uP, yC, qT, kz, knew, vtok, gtok) = (out[n] for n, _, _ in mixer)
        (sg, zr0, zr1, zr2, t1, t2, kf0, kf1, ktok, gT, wg, wgH, wgL, XP) = (out[n] for n, _, _ in inproj)
        zr, kf = [zr0, zr1, zr2], [kf0, kf1]
        XH, XL = [out["XH0"], out["XH1"]], [out["XL0"], out["XL1"]]
        rawc = [out[f"rawc{i}"] for i in range(4)]
        hc = [out["hc0"], out["hc1"]]
        (KTb0, KTb1, PT, PTn, Ss, Sw, Pd, Sc0, pnT, im1, im2, sb0, tj, tg, gB, nw, dsm, Qc, Qpad,
         Pb0, Pb1, Pb2, PTb0, PTb1, PcT, smc, smx, sms, smr) = (out[n] for n, _, _ in attn)
        KTb, Pb, PTb, Pc = [KTb0, KTb1], [Pb0, Pb1, Pb2, KTb0[:, 0:TP]], [PTb0, PTb1], KTb1[:, 0:1024]
        mixT = out["mixT"]
        sqb = [sq[0]] + [sq[1] if k % 2 else rb for k in range(1, KT)]
        hH, hL, fs, r2, rl0, rl1, h20, h21 = (out[n] for n, _, _ in ffn)
        rl, h2 = [rl0, rl1], [h20, h21]

        def C(c0, n, p0=0, p1=P):
            return cst[p0:p1, c0 - C_PERM:c0 - C_PERM + n]

        PA, PB, PR, PS = psum("PA"), psum("PB"), psum("PR"), psum("PS")
        PZ = [PA, PB]

        s_vec, s_cst, s_x, s_misc, s_wg, s_pt, s_us = (sem(n) for n in (
            "vec_loaded", "const_loaded", "x_loaded", "w2_loaded", "wg_loaded", "pt_loaded", "us_loaded"))
        s_raw = [sem(f"block_loaded{i}") for i in range(2)]
        s_whi, s_split, s_wgs = sem("block_hi"), sem("block_split"), sem("wg_split")
        s_init, s_initd, s_idx = sem("pool_init"), sem("dve_init"), sem("idx_ready")
        s_grp = sem("group_done")
        s_gmm = sem("gates_done")
        s_ahi = sem("block_hi_by_scalar")
        s_add, s_rh = sem("square_added"), sem("rinv_half")
        s_sq, s_st, s_std, s_rinv = sem("squared"), sem("mean_fed"), sem("std_ready"), sem("rinv_ready")
        s_nt, s_nh, s_nl = sem("norm_tmp"), sem("norm_hi"), sem("norm_lo")
        s_sig, s_u, s_z = sem("sigmoid_ready"), sem("glu_ready"), sem("z_ready")
        s_rot, s_rot2, s_t1, s_rope = sem("rot_done"), sem("rot_used"), sem("cos_done"), sem("roped")
        s_tok, s_tokA, s_tokD, s_kzc = sem("tok_done"), sem("tok_evac_act"), sem("tok_evac_dve"), sem("kz_copied")
        s_gt, s_gtt, s_gtk = sem("gates_sig"), sem("gates_turned"), sem("gates_ready")
        s_out = sem("stores_done")
        s_kcd = sem("kcmp_stored")
        s_tap, s_ys = sem("conv_step"), sem("conv_sample")
        s_rc = [sem(f"cmp_raw_loaded{i}") for i in range(4)]
        s_xt, s_xh, s_xl, s_pe, s_cmm = sem("x_turned"), sem("x_hi"), sem("x_lo"), sem("pe_col"), sem("cmp_unit")
        s_bias, s_gelu, s_w2m, s_w2e = sem("cmp_bias"), sem("gelu_done"), sem("cmp_out"), sem("cmp_out_used")
        s_dec = [sem(f"dec_loaded{i}") for i in range(2)]
        s_win = [sem(f"window_loaded{i}") for i in range(2)]
        s_kt, s_ktA, s_ktD, s_sc = sem("k_turned"), sem("k_evac_act"), sem("k_evac_dve"), sem("scores_done")
        s_q, s_scc = sem("q_padded"), sem("cmp_scores_done")
        s_dA, s_dV, s_dP = sem("dec_act"), sem("dec_dve"), sem("dec_pe")
        s_dpv = sem("dec_pv")
        s_cS, s_cX, s_cT, s_cE = (sem(n) for n in ("pc_scores", "pc_exp", "pc_turned", "pc_evac"))
        s_cV = sem("pc_dve")
        s_pei, s_pel, s_pec = sem("xh_zeroed"), sem("xl_zeroed"), sem("pe_col_lo")
        s_tokst = sem("tokens_stored")
        s_init2 = sem("mixer_zeroed")
        s_swp, s_xp, s_pcm = sem("prompt_swapped"), sem("prompt_x"), sem("prompt_cmp")
        s_S, s_mx, s_ex, s_pn, s_T, s_ev, s_pv, s_oh, s_ol = (sem(n) for n in (
            "att_scores", "att_max", "att_exp", "att_norm", "att_turned", "att_evac", "att_pv", "att_ohi", "att_olo"))
        s_sm = sem("att_small")
        s_tv, s_ta, s_tp = sem("tail_dve"), sem("tail_act"), sem("tail_pe")
        s_evt = sem("tile_evacuated")
        s_scaled, s_res = sem("branch_scaled"), sem("residual_added")
        s_r = sem("mlp_scale_step")
        s_fsq, s_acc, s_fg = sem("f_squared"), sem("f_squares_summed"), sem("f_gained")
        s_ym, s_yd, s_ypm, s_yp = sem("y_scaled_dve"), sem("y_dve"), sem("y_scaled_pool"), sem("y_pool")
        s_h2, s_hh, s_hl = sem("h_squared"), sem("h_hi"), sem("h_lo")
        s_warm = sem("table_loaded")

        block = ctx.enter_context(nc.Block())
        A_wblk = A["wblk"]

        @block.sync
        def _(sp):
            sp.dma_start(vec[:, :], A["vecs"]).then_inc(s_vec, 16)
            sp.dma_start(ident[:, :], A["consts"][:, 0:P]).then_inc(s_vec, 16)
            sp.dma_start(wraw[0][:, :], A_wblk[0]).then_inc(s_raw[0], 16)
            sp.dma_start(w2[:, :, :], A["w2"]).then_inc(s_misc, 16)
            sp.dma_start(swap[:, 0:64], A["consts"][:, 64:P]).then_inc(s_misc, 16)
            sp.dma_start(swap[:, 64:P], A["consts"][:, 0:64]).then_inc(s_misc, 16)
            sp.wait_ge(s_rc[0], 16)
            sp.dma_start(xT[:, :, :], A["x_fm"]).then_inc(s_x, 16)
            sp.dma_start(wraw[1][:, :], A_wblk[1]).then_inc(s_raw[1], 16)
            sp.dma_start(cst[:, 0:C_CI - C_PERM], A["consts"][:, P:C_CI]).then_inc(s_cst, 16)
            sp.dma_start(C(C_PAR, 2), A["consts"][:, C_PAR:C_PAR + 2]).then_inc(s_cst, 16)
            sp.dma_start(uS[:, :, :, :], A["us0"]).then_inc(s_us, 16)

            def load(slot, b):
                sp.dma_start(wraw[slot][:, :], A_wblk[bass.ds(b, 1)].rearrange("o p n -> (o p) n"))\
                    .then_inc(s_raw[slot], 16)

            with sp.Fori(1, 6) as i:
                for s in range(2):
                    sp.wait_ge(s_split, 2 * i + s - 1)
                    load(s, 2 * i + s)
            sp.wait_ge(s_split, SPLITS(10))
            sp.dma_start(wraw[0][:, :], A_wblk[12]).then_inc(s_raw[0], 16)
            for b in (13, 14):
                sp.wait_ge(s_pcm, b - 12)
                sp.dma_start(wraw[b % 2][:, :], A_wblk[b]).then_inc(s_raw[b % 2], 16)
            with sp.Fori(0, (N_BLOCKS - 15) // 2) as i:
                for e in range(2):
                    sp.wait_ge(s_split, 12 + 2 * i + e)
                    load(1 - e, 15 + 2 * i + e)
            for k, sm, n in ((0, s_yd, 1), (1, s_yd, 2), (6, s_yp, 1), (2, s_yd, 3), (3, s_yd, 4), (7, s_yp, 2),
                             (4, s_yd, 5), (5, s_yd, 6)):
                sp.wait_ge(sm, n)
                if k == 5:
                    sp.wait_ge(s_yp, 3)
                sp.dma_start(A["y_fm"][:, k, :], xT[:, k, :]).then_inc(s_out, 16)
            sp.wait_ge(s_out, 16 * (KT + 4))
            sp.wait_ge(s_tokst, 16 * 10)
            sp.wait_ge(s_kcd, 16 * 2)

        @block.gpsimd
        def _(pool):
            for t_, v in ((ones[:, 0, :], 1.0 / D), (ones[:, 1, :], 1.0 / CH), (epsc[:, :], EPS),
                          (zero[:, :], 0.0), (kcBD[:, :], 0.0), (vcBD[:, :, :], 0.0)):
                pool.memset(t_, v).then_inc(s_init, 1)
            pool.wait_ge(s_pt, 32)
            pool.tensor_scalar(idx[:, 0:4], pt_i[:, 0:4], 8.0, C(C_CI, 1), ALU.mult, ALU.add).then_inc(s_idx, 1)
            pool.tensor_scalar(idx[:, 4:12], pt_i[:, 4:12], 16.0, C(C_CI + 1, 1), ALU.mult, ALU.add)\
                .then_inc(s_idx, 1)
            pool.wait_ge(s_init, 6)

            def split(b, s, raw_count, n_split, free_sem=None, free_count=0):
                pool.wait_ge(s_raw[s], raw_count)
                if free_sem is not None:
                    pool.wait_ge(free_sem, free_count)
                pool.tensor_tensor(wH[s][:, :], wraw[s][:, :], zero[:, :].broadcast_to([P, BW]), ALU.add)\
                    .then_inc(s_whi, 1)
                pool.wait_ge(s_whi, n_split)
                pool.tensor_tensor(wL[s][:, :], wraw[s][:, :], wH[s][:, :].bitcast(F32), ALU.subtract)\
                    .then_inc(s_split, 1)

            pools_c = [A["pool_kc"], A["pool_vc"]]

            def gather(u):
                kv, pr = divmod(u, 4)
                if u >= 4:
                    pool.wait_ge(s_xt, 4 * (u - 3))
                pool.indirect_dma_start(rawc[u % 4][:, :], None, pools_c[kv],
                                        bass.IndirectOffsetOnAxis(ap=idx[:, pr:pr + 1], axis=0))\
                    .then_inc(s_rc[u % 4], 16)

            pool.wait_ge(s_idx, 2)
            for u in range(4):
                gather(u)
            gather(4)
            split(1, 1, 16, 2)
            gather(5)
            gather(6)
            gather(7)
            split(2, 0, 32, 3, s_cmm, 4)
            pool.wait_ge(s_cmm, 8)
            pool.memset(uP[:, :, 0:TAPS - 1], 0.0).then_inc(s_init2, 1)
            split(3, 1, 32, 4, s_cmm, 8)
            pool.memset(XP[:, :, :, 64:130], 0.0).then_inc(s_init2, 1)
            pool.wait_ge(s_w2m, 8)
            pool.memset(kz[:, :, :, :], 0.0).then_inc(s_init2, 1)
            with pool.Fori(2, 4) as i:
                for s in range(2):
                    split(2 * i + s, s, 16 * i + 16, 2 * i + s + 1, s_grp, 4 * i + 2 * s - 6)
            pool.wait_ge(s_wg, 16)
            pool.tensor_copy(wgH[:, :], wg[:, :]).then_inc(s_wgs, 1)
            pool.wait_ge(s_wgs, 1)
            pool.tensor_tensor(wgL[:, :], wg[:, :], wgH[:, :].bitcast(F32), ALU.subtract).then_inc(s_wgs, 1)
            split(8, 0, 16 * 5, 9, s_grp, 10)
            split(9, 1, 16 * 5, 10, s_grp, 12)
            split(10, 0, 16 * 6, 11, s_grp, 14)

            pool.wait_ge(s_gmm, 1)
            pools_s = [A["pool_ks"], A["pool_vs"]]

            def dec_load(i):
                kv, b = divmod(i, NS)
                pool.indirect_dma_start(rks[i % 2][:, :], None, pools_s[kv],
                                        bass.IndirectOffsetOnAxis(ap=idx[:, 4 + b:5 + b], axis=0))\
                    .then_inc(s_dec[i % 2], 16)

            dec_load(0)
            dec_load(1)
            for i in range(2, 2 * NS):
                if i < NS + 2:
                    pool.wait_ge(s_kt, 3 * (i - 1))
                else:
                    pool.wait_ge(s_dpv, i - NS - 1)
                dec_load(i)
            split(13, 1, 16 * 7, 12, s_grp, 16)
            split(14, 0, 16 * 8, 13, s_grp, 18)
            split(15, 1, 16 * 8, 14, s_grp, 20)
            split(16, 0, 16 * 9, 15, s_grp, 22)
            split(17, 1, 16 * 9, 16, s_grp, 24)
            for k in range(KT):
                pool.wait_ge(s_scaled, k + 1)
                pool.tensor_tensor(xT[:, k, :], xT[:, k, :], mixT[:, k, :], ALU.add).then_inc(s_res, 1)
            pool.wait_ge(s_ahi, 1)
            pool.tensor_tensor(wL[0][:, :], wraw[0][:, :], wH[0][:, :].bitcast(F32), ALU.subtract).then_inc(s_split, 1)
            with pool.Fori(0, (N_BLOCKS - 19) // 2) as i:
                for e in range(2):
                    split(19, 1 - e, 16 * (10 + i + e), 17 + 2 * i + e, s_grp, 28 + 4 * i + 2 * e)
            for k in range(1, 6):
                pool.wait_ge(s_fsq, k + 1)
                if k >= 2:
                    pool.wait_ge(s_acc, k - 1)
                pool.tensor_tensor(rl0[:, :], rl0[:, :], (h20, h21)[k % 2][:, :], ALU.add).then_inc(s_acc, 1)
            pool.wait_ge(s_rinv, 4)
            pool.wait_ge(s_fg, KT)
            for j, (k, c) in enumerate(Y_POOL):
                pool.tensor_tensor(fs[:, k, c], fs[:, k, c], rb[:, c], ALU.mult).then_inc(s_ypm, 1)
                pool.wait_ge(s_ypm, j + 1)
                pool.tensor_tensor(xT[:, k, c], xT[:, k, c], fs[:, k, c], ALU.add).then_inc(s_yp, 1)

        @block.scalar
        def _(act):
            def square(norm, k, src):
                if k >= 3:
                    act.wait_ge(s_add, 6 * norm + k - 2)
                act.activation(sqb[k][:, :].rearrange("p (a b) -> p a b", a=2) if norm == 1 else sqb[k][:, :],
                               src, ACT.Square).then_inc(s_sq, 1)

            def root(norm, mean):
                act.wait_ge(s_st, norm + 1)
                act.activation(rb[:, :].rearrange("p (a b) -> p a b", a=2), mean[:, :, 0:HT], ACT.Sqrt,
                               bias=epsc[:, :]).then_inc(s_std, 1)

            n_warm = [0]

            def load_table(f):
                act.wait_ge(s_init, 6)
                if n_warm[0]:
                    act.wait_ge(s_warm, n_warm[0])
                act.activation(warm[:, :], epsc[:, :], f).then_inc(s_warm, 1)
                n_warm[0] += 1

            def x_evac(u, i):
                act.wait_ge(s_xt, 4 * u + i + 1)
                act.activation(XH[u % 2][:, 2 * i:2 * i + 2, 0:256],
                               PR[:, i % 2, :].rearrange("p (j n) -> p j n", j=2), ACT.Copy).then_inc(s_xh, 1)

            def norm_hi(ks):
                for k in ks:
                    act.wait_ge(s_nt, k + 1)
                    act.activation(actH[k], sq[k % 2][:, :], ACT.Copy).then_inc(s_nh, 1)

            def gelu(u):
                kv = u // 4
                act.wait_ge(s_cmm, u + 1)
                act.wait_ge(s_bias, kv + 1)
                if u >= 2:
                    act.wait_ge(s_w2m, u - 1)
                act.activation(hc[u % 2][:, 0:256], PA[:, u % 2, 0:256], ACT.Gelu_apprx_tanh,
                               bias=biasc[:, kv:kv + 1]).then_inc(s_gelu, 1)

            act.dma_start(pt_i[:, :], A["pt_rep"]).then_inc(s_pt, 16)
            act.dma_start(C(C_CI, 2), A["consts"][:, C_CI:C_CI + 2]).then_inc(s_pt, 16)
            load_table(ACT.Gelu_apprx_tanh)
            act.wait_ge(s_raw[0], 16)
            act.activation(wH[0][:, :], wraw[0][:, :], ACT.Copy).then_inc(s_whi, 1)
            act.wait_ge(s_vec, 32)
            for u in range(8):
                kv, pr = divmod(u, 4)
                if u >= 2:
                    act.wait_ge(s_cmm, u - 1)
                if pr == 0:
                    act.wait_ge(s_pei, 2)
                    act.activation(XH[u % 2][:, :, 256:258], vec[:, V_PE + 16 * kv:V_PE + 16 * kv + 16]
                                   .rearrange("p (a j) -> p j a", a=2), ACT.Copy).then_inc(s_pe, 1)
                for i in range(4):
                    x_evac(u, i)
                if 2 <= u < 4:
                    act.wait_ge(s_x, 16)
                    for k in range(4 * (u - 2), 4 * (u - 1)):
                        square(0, k, xT[:, k, :])
                if u == 4:
                    act.wait_ge(s_init, 6)
                    root(0, PB)
                if u >= 5:
                    norm_hi(NORM_AT[u])
                if u >= 1:
                    gelu(u - 1)
            gelu(7)
            def tok_evac(c):
                act.wait_ge(s_tok, c + 1)
                dst = vtok[:, (c - 3) // 2] if c in (3, 5) else ktok[:, TOKSLOT[c]]
                act.activation(dst[:, 0:QT, :], PS[:, 0, :].rearrange("p (t d) -> p t d", t=QT), ACT.Copy)\
                    .then_inc(s_tokA, 1)

            def store_tok(c):
                act.wait_ge(s_tokA, c + 1)
                act.wait_ge(s_tokD, c + 1)
                src = vtok[:, (c - 3) // 2] if c in (3, 5) else ktok[:, TOKSLOT[c]]
                act.dma_start(A["p_rows"][c].rearrange("(t p) d -> p t d", p=P), src[:, 0:QT, :])\
                    .then_inc(s_kcd if c < 2 else s_tokst, 16)
                dst = A["s_rows"][c] if c < 4 else A["s_win"][c - 4][:, WIN - 1, :]
                act.dma_start(dst, src[0:NS, QT, :]).then_inc(s_tokst, 16)

            def kz_copies(bi, kfi):
                act.wait_ge(s_rope, kfi + 1)
                for g in range(G):
                    h = slice(g * HD, (g + 1) * HD)
                    act.activation(kz[h, bi, g, :], kf[kfi % 2][h, 0:TP], ACT.Copy).then_inc(s_kzc, 1)
                act.activation(knew[:, bi, :], kf[kfi % 2][:, TP:T], ACT.Copy).then_inc(s_kzc, 1)

            def prompt_chunks():
                act.wait_ge(s_rope, 1)
                act.wait_ge(s_z, 2)
                act.wait_ge(s_swp, 1)
                for kv, own in enumerate((kf[0], zr[1])):
                    for jj in range(2):
                        h = slice(jj * HD, (jj + 1) * HD)
                        for g, src in ((jj, own[h, 0:TP]), (1 - jj, PR[h, kv, :])):
                            act.activation(XP[h, kv, :, g * 32:(g + 1) * 32],
                                           src.rearrange("p (c t j) -> p t c j", t=8, j=2)[:, :, :, jj], ACT.Copy)\
                                .then_inc(s_xp, 1)

            act.dma_start(wg[:, :], A["wgate"]).then_inc(s_wg, 16)
            for kv in range(2):
                act.dma_start(A["s_win"][kv][:, 0:WIN - 1, :], A["win_rows"][kv][:, 1:WIN, :]).then_inc(s_out, 16)
            act.wait_ge(s_init2, 3)
            for n in range(N_Z):
                if n < 8:
                    if n % 2 == 0:
                        act.wait_ge(s_grp, n + 1)
                        if n >= 2:
                            act.wait_ge(s_u, 3 * (n // 2))
                        act.activation(sg[:, :].rearrange("p (a b) -> p a b", a=2), PZ[0][:, :, 0:HT], ACT.Sigmoid)\
                            .then_inc(s_sig, 1)
                else:
                    z = n - 8
                    act.wait_ge(s_grp, n + 1)
                    if z >= 3:
                        if ROPE[z - 3]:
                            act.wait_ge(s_rot, sum(ROPE[:z - 2]))
                            act.wait_ge(s_t1, sum(ROPE[:z - 2]))
                        if z == 4:
                            act.wait_ge(s_xp, 8)
                        if z - 3 < 6 and not ROPE[z - 3]:
                            act.wait_ge(s_tok, z - 2)
                    act.activation(zr[z % 3][:, :].rearrange("p (a b) -> p a b", a=2), PZ[n % 2][:, :, 0:HT],
                                   ACT.Copy, scale=(HD ** -0.5 if z >= 6 else 1.0)).then_inc(s_z, 1)
                    if z == 2:
                        prompt_chunks()
                    if z == 4:
                        kz_copies(0, 1)
                    if z == 6:
                        kz_copies(1, 2)
                    if 2 <= z < 8:
                        tok_evac(z - 2)
                        store_tok(z - 2)
            act.wait_ge(s_gmm, 1)
            act.activation(gT[:, :].rearrange("p (a b) -> p a b", a=2), PA[0:24, :, 0:HT], ACT.Sigmoid)\
                .then_inc(s_gt, 1)
            for i in range(2):
                act.dma_start(rkw[i][:, :], A["win_k"][i]).then_inc(s_win[i], 16)
            act.wait_ge(s_u, 3 * CT)
            act.dma_start(A["pconv"], uP[:, :, TP:TP + TAPS - 1]).then_inc(s_out, 16)
            act.dma_start(A["sconv"], uS[:, :, :, 1:TAPS]).then_inc(s_out, 16)
            for kv in range(2):
                act.wait_ge(s_pcm, kv + 1)
                act.activation(hcp[:, kv, 0:64], PA[:, kv, 0:64], ACT.Gelu_apprx_tanh, bias=biasc[:, kv:kv + 1])\
                    .then_inc(s_gelu, 1)
            act.wait_ge(s_tokst, 16 * 10)
            act.wait_ge(s_kcd, 32)

            def window_load(i):
                kv, b = divmod(i, NS)
                if 2 <= i < NS + 2:
                    act.wait_ge(s_kt, 3 * (i - 1))
                elif i >= 2:
                    act.wait_ge(s_dpv, i - NS - 1)
                act.dma_start(rkw[i % 2][:, :], (A["win_k"], A["win_v"])[kv][b]).then_inc(s_win[i % 2], 16)

            def keys_evac(b):
                if b >= 2:
                    act.wait_ge(s_sc, b - 1)
                act.wait_ge(s_kt, 3 * b + 1)
                act.activation(KTb[b % 2][:, 0:512], PR[:, 0, :], ACT.Copy).then_inc(s_ktA, 1)
                act.wait_ge(s_kt, 3 * b + 3)
                act.activation(KTb[b % 2][:, 1024:1536], PS[:, 0, :], ACT.Copy).then_inc(s_ktA, 1)
                window_load(b + 2)

            act.wait_ge(s_dV, DV_CMAX)
            act.activation(Sc0[:, 0:63], PB[0:64, 1, 0:63], ACT.Exp, bias=dsm[:, 0:1], accum_out=dsm[:, 1:2])\
                .then_inc(s_dA, 1)
            for b in range(NS):
                keys_evac(b)
            act.wait_ge(s_sc, NS)
            act.activation(Sw[:, 0:WIN], PB[0:64, 0, :], ACT.Copy).then_inc(s_dA, 1)
            act.wait_ge(s_dV, DV_SMAX)
            act.activation(Ss[:, 0:PAST + 1], Ss[:, 0:PAST + 1], ACT.Exp, bias=dsm[:, 8:9], accum_out=dsm[:, 9:10])\
                .then_inc(s_dA, 1)
            act.wait_ge(s_dV, DV_WMAX)
            act.activation(Sw[:, 0:WIN + 1], Sw[:, 0:WIN + 1], ACT.Exp, bias=dsm[:, 4:5], accum_out=dsm[:, 5:6])\
                .then_inc(s_dA, 1)
            act.wait_ge(s_dP, DP_PTS)
            act.activation(PT[:, 0:512], PR[:, 0, :], ACT.Copy).then_inc(s_dA, 1)
            act.wait_ge(s_cV, 3)
            act.activation(Pc, Pc, ACT.Exp).then_inc(s_cX, 1)
            for i in range(NS + 2, NS + 5):
                window_load(i)
            for t in range(CT):
                act.wait_ge(s_tv, TV_XC + t)
                if t == 2:
                    window_load(NS + 5)
                if t >= 2:
                    act.wait_ge(s_tp, t)
                act.activation(sq[t % 2][:, :], yC[:, t, :], ACT.Square).then_inc(s_ta, 1)
            act.wait_ge(s_tp, 1 + CT)
            act.activation(rb[:, :].rearrange("p (a b) -> p a b", a=2), PB[:, :, 0:HT], ACT.Sqrt, bias=epsc[:, :])\
                .then_inc(s_ta, 1)
            window_load(NS + 6)
            act.wait_ge(s_cT, 1)
            act.activation(PcT[:, :, :].rearrange("p c (i q) -> p i c q", i=QT),
                           PR[:, :, :].rearrange("p a (i c q) -> p (a i) c q", i=2, c=2), ACT.Copy).then_inc(s_cE, 1)
            window_load(NS + 7)
            for t in range(CT):
                act.wait_ge(s_tv, TV_NRM + t)
                if t >= 2:
                    act.wait_ge(s_tv, TV_NRM + CT + t - 2)
                act.activation(sq[t % 2][:, :], yC[:, t, :], ACT.Silu, scale=vec[:, V_LG + t:V_LG + t + 1],
                               bias=vec[:, V_LB + t:V_LB + t + 1]).then_inc(s_ta, 1)
                act.wait_ge(s_ta, CT + 2 + 2 * t)
                act.activation(actH[t], sq[t % 2][:, :], ACT.Copy).then_inc(s_ta, 1)
            load_table(ACT.Exp)
            act.wait_ge(s_dpv, NS)
            act.activation(od[:, :].rearrange("p (a b) -> p a b", a=2), PA[0:8, :, :], ACT.Copy).then_inc(s_dA, 1)
            act.wait_ge(s_dP, DP_OT)
            for g in range(G):
                h = slice(g * HD, (g + 1) * HD)
                act.activation(oH[h, :, TP:T],
                               PS[h, 0, 0:64].rearrange("p (b g r) -> p g r b", b=NS, g=G)[:, g], ACT.Copy)\
                    .then_inc(s_dA, 1)
            for s in range(N_UNITS + LAG):
                if s >= LAG:
                    u = s - LAG
                    r, g, br, i = UNITS[u]
                    act.wait_ge(s_T, u + 1)
                    if u >= 2:
                        act.wait_ge(s_pv, u - 1)
                    act.activation(PTb[u % 2][:, 0:(i + 1) * P], PR[:, u % 2, 0:(i + 1) * P], ACT.Copy)\
                        .then_inc(s_ev, 1)
                if s < N_UNITS:
                    r, g, br, i = UNITS[s]
                    act.wait_ge(s_mx, s + 1)
                    if s >= 4:
                        act.wait_ge(s_T, s - 3)
                    act.activation(Pb[s % 4][:, 0:(i + 1) * P], PZ[s // 2 % 2][:, s % 2, 0:(i + 1) * P], ACT.Exp,
                                   bias=smx[:, s:s + 1], accum_out=sms[:, s:s + 1]).then_inc(s_ex, 1)
                if s >= 20 and s % 16 == 4 and s < N_UNITS:
                    rr = s // 16 - 1
                    act.wait_ge(s_pv, 16 * (rr + 1))
                    act.activation(actH[CT + rr][:, 0:TP], PS[:, rr % 2, :], ACT.Copy).then_inc(s_oh, 1)
            act.wait_ge(s_pv, N_UNITS)
            act.activation(actH[KT - 1][:, 0:TP], PS[:, 1, :], ACT.Copy).then_inc(s_oh, 1)
            load_table(ACT.Sqrt)
            for k in range(KT):
                act.wait_ge(s_grp, N_Z + k + 1)
                square(1, k, PZ[k % 2][:, :, 0:HT])
            root(1, PS)
            act.wait_ge(s_raw[0], 16 * 10)
            act.activation(wH[0][:, :], wraw[0][:, :], ACT.Copy).then_inc(s_ahi, 1)
            for k in range(KT):
                act.wait_ge(s_res, k + 1)
                act.activation(actH[k], xT[:, k, :], ACT.Copy, scale=vec[:, V_GPRE2 + k:V_GPRE2 + k + 1])\
                    .then_inc(s_nh, 1)
            for k in range(KT):
                square(2, k, xT[:, k, :])
            root(2, PS)
            for fh in range(2):
                def hidden(j, c, h_dst):
                    f = 16 * fh + 4 * j + c
                    act.wait_ge(s_evt, 8 + 8 * fh + f + 1)
                    if not isinstance(j, int) or fh or f >= 2:
                        act.wait_ge(s_hl, f - 1)
                    act.activation(h2[c % 2][:, :], rl[c % 2][:, :], ACT.Square).then_inc(s_h2, 1)
                    act.wait_ge(s_h2, f + 1)
                    act.activation(h_dst, h2[c % 2][:, :], ACT.Copy).then_inc(s_hh, 1)

                if fh == 0:
                    for c in range(4):
                        hidden(0, c, hH[:, c, :])
                with act.Fori(1 - fh, 4) as j:
                    for c in range(4):
                        hidden(j, c, hH[:, bass.ds(4 * j + c, 1), :].rearrange("p o t -> p (o t)"))
            act.wait_ge(s_hl, 32)
            fsq = [rl0, h21, h20, h21, h20, h21, sq[0], sq[1]]
            for k in range(KT):
                act.wait_ge(s_evt, 8 + 48 - 8 + k + 1)
                if 3 <= k < 6:
                    act.wait_ge(s_acc, k - 2)
                act.activation(fsq[k][:, :], fs[:, k, :], ACT.Square).then_inc(s_fsq, 1)
                act.activation(fs[:, k, :], fs[:, k, :], ACT.Copy, scale=vec[:, V_GPOST2 + k:V_GPOST2 + k + 1])\
                    .then_inc(s_fg, 1)
            root(3, PS)

        @block.vector
        def _(dve):
            def chain(ins, sm, n):
                ins.then_inc(sm, 1)
                dve.wait_ge(sm, n)

            def add_square(norm, k):
                dve.wait_ge(s_sq, KT * norm + k + 1)
                if 6 * norm + k >= 2:
                    dve.wait_ge(s_add, 6 * norm + k - 1)
                dve.tensor_tensor(sq[0][:, :], sq[0][:, :], sqb[k][:, :], ALU.add).then_inc(s_add, 1)

            def rinv(norm):
                dve.wait_ge(s_std, norm + 1)
                dve.reciprocal(rb[:, :], rb[:, :]).then_inc(s_rinv, 1)
                dve.wait_ge(s_rinv, norm + 1)

            def norm_lo(k):
                dve.wait_ge(s_nh, k + 1)
                dve.tensor_tensor(actL[k], sq[k % 2][:, :], actH[k].bitcast(F32), ALU.subtract).then_inc(s_nl, 1)

            dve.wait_ge(s_vec, 32)
            for i, X in enumerate((XH[0], XH[1], XL[0], XL[1])):
                ins = dve.memset(X[:, :, 256:XW].bitcast(U32), 0)
                ins.then_inc(s_pei if i < 2 else s_pel, 1)

            dve.wait_ge(s_whi, 1)
            dve.tensor_tensor(wL[0][:, :], wraw[0][:, :], wH[0][:, :].bitcast(F32), ALU.subtract).then_inc(s_split, 1)

            def cmp_out_evac(u):
                kv, pr = divmod(u, 4)
                dve.wait_ge(s_w2m, u + 1)
                dst = vcS[:, pr, :] if kv else kcS[:, pr * P:(pr + 1) * P]
                dve.tensor_copy(dst, PS[:, u % 2, 0:P]).then_inc(s_w2e, 1)

            for u in range(8):
                kv, pr = divmod(u, 4)
                if pr == 0:
                    dve.wait_ge(s_pel, 2)
                    dve.wait_ge(s_pe, kv + 1)
                    dve.tensor_tensor(XL[u % 2][:, :, 256:258], vec[:, V_PE + 16 * kv:V_PE + 16 * kv + 16]
                                      .rearrange("p (a j) -> p j a", a=2), XH[u % 2][:, :, 256:258].bitcast(F32),
                                      ALU.subtract).then_inc(s_pec, 1)
                for i in range(4):
                    c = slice(2 * i, 2 * i + 2)
                    dve.wait_ge(s_xh, 4 * u + i + 1)
                    dve.tensor_tensor(XL[u % 2][:, c, 0:256], PR[:, i % 2, :].rearrange("p (j n) -> p j n", j=2),
                                      XH[u % 2][:, c, 0:256].bitcast(F32), ALU.subtract).then_inc(s_xl, 1)
                if 2 <= u < 4:
                    for k in range(max(4 * (u - 2), 1), min(4 * (u - 1), KT - 1)):
                        add_square(0, k)
                if u == 4:
                    dve.wait_ge(s_std, 1)
                    dve.reciprocal(rb[:, 0:HT], rb[:, 0:HT]).then_inc(s_rh, 1)
                if u == 5:
                    dve.reciprocal(rb[:, HT:T], rb[:, HT:T]).then_inc(s_rinv, 1)
                    dve.wait_ge(s_rh, 1)
                    dve.wait_ge(s_rinv, 1)
                if u >= 5:
                    for k in NORM_AT[u]:
                        if k >= 2:
                            dve.wait_ge(s_nl, k - 1)
                        dve.scalar_tensor_tensor(out=sq[k % 2][:, :], in0=xT[:, k, :],
                                                 scalar=vec[:, V_GPRE + k:V_GPRE + k + 1], in1=rb[:, :],
                                                 op0=ALU.mult, op1=ALU.mult).then_inc(s_nt, 1)
                        if k >= 1:
                            norm_lo(k - 1)
                if pr == 1:
                    dve.wait_ge(s_cmm, u)
                    dve.tensor_tensor(biasc[:, kv:kv + 1], PA[:, (u - 1) % 2, 256:257],
                                      vec[:, V_B1 + kv:V_B1 + kv + 1], ALU.add).then_inc(s_bias, 1)
                if u >= 2:
                    cmp_out_evac(u - 2)
            norm_lo(KT - 1)
            cmp_out_evac(6)
            cmp_out_evac(7)
            dve.wait_ge(s_cst, 32)
            dve.tensor_copy(identb[:, :], ident[:, :]).then_inc(s_initd, 1)
            dve.tensor_copy(maskb[:, :], C(C_MASK, P)).then_inc(s_initd, 1)
            dve.wait_ge(s_init2, 3)
            dve.wait_ge(s_us, 16)

            taps_done = [0] * CT
            steps = [0]
            last = {}

            def conv(t, n):
                for _ in range(n):
                    k = taps_done[t]
                    if k == TAPS:
                        return
                    taps_done[t] += 1
                    w = vec[:, V_CW + t * TAPS + k:V_CW + t * TAPS + k + 1]
                    for hf in range(2):
                        c0 = hf * 256
                        src, dst = uP[:, t, k + c0:k + c0 + 256], yC[:, t, c0:c0 + 256]
                        if k == 0:
                            ins = dve.tensor_scalar(dst, src, w, vec[:, V_CB + t:V_CB + t + 1], ALU.mult, ALU.add)
                        else:
                            dve.wait_ge(s_tap, last[t, hf])
                            ins = dve.scalar_tensor_tensor(out=dst, in0=src, scalar=w, in1=dst, op0=ALU.mult,
                                                           op1=ALU.add)
                        ins.then_inc(s_tap, 1)
                        steps[0] += 1
                        last[t, hf] = steps[0]

            def conv_some(n):
                for _ in range(n):
                    left = [t for t in range(CT) if taps_done[t] < TAPS]
                    if left:
                        conv(left[0], 1)

            nrope = [0]

            def rope(z):
                j = nrope[0]
                nrope[0] += 1
                dve.wait_ge(s_z, z + 1)
                if j >= 1:
                    dve.wait_ge(s_rope, j)
                dve.tensor_tensor(t1[:, :], zr[z % 3][:, :], C(C_COS, T), ALU.mult).then_inc(s_t1, 1)
                dve.wait_ge(s_rot, j + 1)
                dve.tensor_tensor(t2[:, :].rearrange("p (a b) -> p a b", a=2), PR[:, :, 0:HT],
                                  C(C_SIN, T).rearrange("p (a b) -> p a b", a=2), ALU.mult).then_inc(s_rot2, 1)
                dve.wait_ge(s_t1, j + 1)
                dve.wait_ge(s_rot2, j + 1)
                if j < 3:
                    if j == 2:
                        dve.wait_ge(s_tok, 1)
                        dve.wait_ge(s_xp, 8)
                    dst = kf[j % 2][:, :]
                else:
                    dst = qT[:, j - 3, :]
                dve.tensor_tensor(dst, t1[:, :], t2[:, :], ALU.add).then_inc(s_rope, 1)

            def tok_evac_s(c):
                dve.wait_ge(s_tok, c + 1)
                dst = vtok[0:NS, (c - 3) // 2] if c in (3, 5) else ktok[0:NS, TOKSLOT[c]]
                dve.tensor_copy(dst[:, QT, :], PS[0:NS, 1, 0:P]).then_inc(s_tokD, 1)

            for n in range(N_Z + 2):
                if n < 8:
                    if n % 2 == 1:
                        t = n // 2
                        dve.wait_ge(s_grp, n + 1)
                        dve.wait_ge(s_sig, t + 1)
                        dve.tensor_tensor(uP[:, t, TAPS - 1:TAPS - 1 + HT], PB[:, 0, 0:HT], sg[:, 0:HT], ALU.mult)\
                            .then_inc(s_u, 1)
                        dve.tensor_tensor(uP[:, t, TAPS - 1 + HT:TAPS - 1 + TP], PB[:, 1, 0:TP - HT], sg[:, HT:TP],
                                          ALU.mult).then_inc(s_u, 1)
                        dve.tensor_tensor(uS[:, t, :, TAPS - 1], PB[:, 1, TP - HT:HT], sg[:, TP:T], ALU.mult)\
                            .then_inc(s_u, 1)
                        dve.wait_ge(s_u, 3 * (t + 1))
                        conv(t, 12)
                else:
                    z = n - 8
                    if 1 <= z <= 10 and ROPE[z - 1]:
                        rope(z - 1)
                    if 2 <= z < 8:
                        tok_evac_s(z - 2)
                    if z < 9:
                        conv(z // 3, 5)
            dve.wait_ge(s_gtt, 1)
            dve.tensor_copy(gtok[:, 0:QT, :], PS[:, 0, 0:96].rearrange("p (t j) -> p t j", t=QT)).then_inc(s_gtk, 1)
            dve.tensor_copy(gtok[0:NS, QT, :], PS[0:NS, 0, 96:120]).then_inc(s_gtk, 1)

            dve.wait_ge(s_rope, 7)
            dve.wait_ge(s_w2m, 9)
            for g in range(G):
                h = slice(g * HD, (g + 1) * HD)
                dve.tensor_copy(kcBD[h, g * 32:(g + 1) * 32], PS[h, 0, g * 32:(g + 1) * 32]).then_inc(s_w2e, 1)
            dve.wait_ge(s_w2m, 10)
            for rr in range(2):
                for g in range(G):
                    h = slice(rr * 64 + g * 32, rr * 64 + (g + 1) * 32)
                    dve.tensor_copy(vcBD[h, rr, g * HD:(g + 1) * HD], PS[h, 1, 0:HD]).then_inc(s_w2e, 1)
            dve.wait_ge(s_tokst, 16 * 10)
            dve.wait_ge(s_kcd, 32)

            def keys_evac(b):
                if b >= 2:
                    dve.wait_ge(s_sc, b - 1)
                dve.wait_ge(s_kt, 3 * b + 2)
                dve.tensor_copy(KTb[b % 2][:, 512:1024], PR[:, 1, :]).then_inc(s_ktD, 1)

            dve.memset(Qc[:, :], 0.0).then_inc(s_q, 1)
            dve.memset(Qpad[:, :], 0.0).then_inc(s_q, 1)
            dve.wait_ge(s_q, 2)
            for g in range(G):
                h = slice(g * HD, (g + 1) * HD)
                src = qT[h, :, TP:T]
                dve.tensor_copy(Qc[h, :].rearrange("p (b g r) -> p g r b", b=NS, g=G)[:, g], src).then_inc(s_q, 1)
                dve.tensor_copy(Qpad[h, :].rearrange("p (b s) -> p s b", b=NS)[:, g * R:(g + 1) * R, :], src)\
                    .then_inc(s_q, 1)
            nv = [0]

            def v(ins):
                ins.then_inc(s_dV, 1)
                nv[0] += 1
                dve.wait_ge(s_dV, nv[0])

            dve.wait_ge(s_scc, 2)
            v(dve.tensor_reduce(dsm[:, 0:1], PB[0:64, 1, 0:63], AX.X, ALU.max, negate=True))
            assert nv[0] == DV_CMAX
            v(dve.tensor_tensor(tg[:, :], PS[0:64, 1, 16:40], C(C_HM, 24, 0, 64), ALU.mult))
            v(dve.tensor_reduce(gB[:, 0:3], tg[:, :].rearrange("p (c h) -> p c h", c=3), AX.X, ALU.add))
            for bi, S_, col in ((0, Ss, PAST), (1, Sw, WIN)):
                v(dve.tensor_tensor(nw[:, bi, :], PS[0:64, 1, bi * 8:bi * 8 + 8], C(C_BM, 8, 0, 64), ALU.mult))
                v(dve.tensor_reduce(S_[:, col:col + 1], nw[:, bi, :], AX.X, ALU.add))
            keys_evac(0)
            dve.wait_ge(s_dA, 1)
            v(dve.tensor_scalar_max(dsm[:, 2:3], dsm[:, 1:2], 1e-30))
            v(dve.reciprocal(dsm[:, 3:4], dsm[:, 2:3]))
            v(dve.memset(Sc0[:, 63:64], 0.0))
            v(dve.tensor_scalar(Sc0[:, 0:63], Sc0[:, 0:63], dsm[:, 3:4], None, ALU.mult))
            assert nv[0] == DV_PN
            keys_evac(1)
            conv_some(4)
            dve.wait_ge(s_dP, DP_PN)
            v(dve.tensor_copy(pnT[:, :], PS[0:64, 1, 64:128]))
            keys_evac(2)
            conv_some(4)
            dve.wait_ge(s_dP, DP_IM1)
            v(dve.tensor_copy(im1[:, :], PS[0:64, 1, 128:144]))
            keys_evac(3)
            conv_some(4)
            dve.wait_ge(s_dP, DP_IM2)
            v(dve.tensor_copy(im2[:, :], PS[0:64, 1, 144:160]))
            v(dve.tensor_reduce(dsm[:, 12:13], im2[:, 1:15], AX.X, ALU.min))
            v(dve.tensor_scalar(tj[:, :], im2[:, 1:15], dsm[:, 12:13], None, ALU.is_le))
            v(dve.tensor_tensor(tj[:, :], tj[:, :], C(C_J, 14, 0, 64), ALU.mult))
            v(dve.tensor_reduce(dsm[:, 13:14], tj[:, :], AX.X, ALU.max))
            v(dve.memset(sb0[:, :], 0.0))
            v(dve.tensor_scalar(sb0[:, 1:15], C(C_J, 14, 0, 64), dsm[:, 13:14], NEG, ALU.is_equal, ALU.mult))
            assert nv[0] == DV_DROP
            for b in range(4, NS):
                keys_evac(b)
                conv_some(4)
            dve.wait_ge(s_sc, NS)
            bias4 = sb0[:, :].unsqueeze(1).unsqueeze(3).broadcast_to([64, 8, NBLK, 8])
            v(dve.tensor_tensor(Ss[:, 0:PAST].rearrange("p (r k c) -> p r k c", r=8, k=NBLK),
                                PA[0:64, :, :].rearrange("p a (r k c) -> p (a r) k c", r=4, k=NBLK), bias4, ALU.add))
            v(dve.tensor_reduce(dsm[:, 8:9], Ss[:, 0:PAST + 1], AX.X, ALU.max, negate=True))
            assert nv[0] == DV_SMAX
            dve.wait_ge(s_dA, 2)
            v(dve.tensor_reduce(dsm[:, 4:5], Sw[:, 0:WIN + 1], AX.X, ALU.max, negate=True))
            assert nv[0] == DV_WMAX
            for a_ in range(2):
                v(dve.tensor_scalar(Pd[:, a_, :], Sc0[:, :], gB[:, 0:1], C(C_PAR + a_, 1, 0, 64), ALU.mult, ALU.mult))
            for bi, S_, n_, o, na in ((0, Ss, PAST, 8, 3), (1, Sw, WIN, 4, 4)):
                dve.wait_ge(s_dA, na)
                v(dve.tensor_scalar_max(dsm[:, o + 2:o + 3], dsm[:, o + 1:o + 2], 1e-30))
                v(dve.reciprocal(dsm[:, o + 3:o + 4], dsm[:, o + 2:o + 3]))
                v(dve.tensor_scalar(S_[:, 0:n_ + 1], S_[:, 0:n_ + 1], dsm[:, o + 3:o + 4], gB[:, 1 + bi:2 + bi],
                                    ALU.mult, ALU.mult))
                v(dve.tensor_scalar(nw[:, bi, :], C(C_BM, 8, 0, 64), S_[:, n_:n_ + 1], None, ALU.mult))
                assert nv[0] == (DV_P if bi else DV_PS)
            dve.wait_ge(s_dP, DP_PT)
            v(dve.tensor_copy(PT[:, 512:832], PR[:, 1, 0:320]))
            v(dve.tensor_copy(PTn[:, :], PS[0:8, 0, 0:128]))
            conv_some(TAPS * CT)
            for t in range(CT):
                w = vec[:, V_CW + t * TAPS:V_CW + (t + 1) * TAPS].unsqueeze(1).broadcast_to([P, NS, TAPS])
                dve.tensor_tensor(ctmp[:, t], uS[:, t, :, :], w, ALU.mult).then_inc(s_ys, 1)
            dve.wait_ge(s_ys, CT)
            dve.tensor_reduce(yC[:, :, TP:T], ctmp[:, :, :, :], AX.X, ALU.add).then_inc(s_ys, 1)
            dve.wait_ge(s_ys, CT + 1)
            dve.tensor_tensor(yC[:, :, TP:T], yC[:, :, TP:T],
                              vec[:, V_CB:V_CB + CT].unsqueeze(2).broadcast_to([P, CT, NS]), ALU.add).then_inc(s_ys, 1)
            tv = [0]

            def tvi(ins, wait=True):
                ins.then_inc(s_tv, 1)
                tv[0] += 1
                if wait:
                    dve.wait_ge(s_tv, tv[0])

            dve.wait_ge(s_tap, 2 * TAPS * CT)
            dve.wait_ge(s_ys, CT + 2)
            tvi(dve.tensor_tensor(ysm[:, :], yC[:, 0, :], yC[:, 1, :], ALU.add))
            tvi(dve.tensor_tensor(ysm[:, :], ysm[:, :], yC[:, 2, :], ALU.add))
            tvi(dve.tensor_tensor(ysm[:, :], ysm[:, :], yC[:, 3, :], ALU.add))
            assert tv[0] == TV_SUM
            nc_ = [0]

            def cv(ins):
                ins.then_inc(s_cV, 1)
                nc_[0] += 1
                dve.wait_ge(s_cV, nc_[0])

            p4 = Pc.rearrange("p (i h n) -> p i h n", i=QT, h=NH)
            p3 = Pc.rearrange("p (h n) -> p h n", n=32)
            vis, visb = (C(c, 128).rearrange("p (i n) -> p i n", i=QT).unsqueeze(2).broadcast_to([P, QT, NH, 32])
                         for c in (C_VIS, C_VISB))
            cmx = smc[:, :, :].rearrange("p i h -> p (i h)")
            csum, cinv = smx[:, 0:32], sms[:, 0:32]
            dve.wait_ge(s_cS, 1)
            cv(dve.tensor_tensor(p4, PR[:, :, :].rearrange("p a (i h n) -> p (a i) h n", i=2, h=NH), visb, ALU.add))
            cv(dve.tensor_reduce(cmx, p3, AX.X, ALU.max))
            cv(dve.tensor_tensor(p3, p3, cmx.unsqueeze(2).broadcast_to([P, 32, 32]), ALU.subtract))
            dve.wait_ge(s_tp, 1)
            for t in range(CT):
                y3 = yC[:, t, :].rearrange("p (a b) -> p a b", a=2)
                tvi(dve.tensor_tensor(y3, y3, PB[:, :, 0:HT], ALU.subtract), wait=False)
            assert tv[0] == TV_XC - 1 + CT
            dve.wait_ge(s_cX, 1)
            cv(dve.tensor_tensor(p4, p4, vis, ALU.mult))
            cv(dve.tensor_reduce(csum, p3, AX.X, ALU.add))
            cv(dve.tensor_scalar_max(csum, csum, 1e-30))
            cv(dve.reciprocal(cinv, csum))
            for g in range(G):
                cinv_g = cinv.rearrange("p (i r g) -> p i r g", i=QT, r=R)[:, :, :, g]
                cv(dve.tensor_tensor(cinv_g, cinv_g, gtok[:, 0:QT, g * R:(g + 1) * R], ALU.mult))
            cv(dve.tensor_tensor(p3, p3, cinv.unsqueeze(2).broadcast_to([P, 32, 32]), ALU.mult))
            assert nc_[0] == PC_DONE
            dve.wait_ge(s_ta, CT + 1)
            tvi(dve.reciprocal(rb[:, :], rb[:, :]))
            for t in range(CT):
                tvi(dve.tensor_tensor(yC[:, t, :], yC[:, t, :], rb[:, :], ALU.mult), wait=False)
            assert tv[0] == TV_NRM - 1 + CT
            for t in range(CT):
                dve.wait_ge(s_ta, CT + 1 + 2 * (t + 1))
                tvi(dve.tensor_tensor(actL[t], sq[t % 2][:, :], actH[t].bitcast(F32), ALU.subtract), wait=False)
            dve.wait_ge(s_dA, 8)
            for g in range(G):
                h = slice(g * HD, (g + 1) * HD)
                v(dve.tensor_tensor(oL[h, :, TP:T],
                                    PS[h, 0, 0:64].rearrange("p (b g r) -> p g r b", b=NS, g=G)[:, g],
                                    oH[h, :, TP:T].bitcast(F32), ALU.subtract))
            for s in range(N_UNITS + 1):
                if s < N_UNITS:
                    r, g, br, i = UNITS[s]
                    dve.wait_ge(s_S, s + 1)
                    dve.tensor_reduce(smx[:, s:s + 1], PZ[s // 2 % 2][:, s % 2, 0:(i + 1) * P], AX.X, ALU.max,
                                      negate=True).then_inc(s_mx, 1)
                if s >= 1:
                    u = s - 1
                    r, g, br, i = UNITS[u]
                    dve.wait_ge(s_ex, u + 1)
                    dve.tensor_scalar_max(sms[:, u:u + 1], sms[:, u:u + 1], 1e-30).then_inc(s_sm, 1)
                    dve.wait_ge(s_sm, 2 * u + 1)
                    dve.reciprocal(smr[:, u:u + 1], sms[:, u:u + 1]).then_inc(s_sm, 1)
                    dve.wait_ge(s_sm, 2 * u + 2)
                    gc = 8 * (1 + br) + g * R + r
                    dve.tensor_scalar(Pb[u % 4][:, 0:(i + 1) * P], Pb[u % 4][:, 0:(i + 1) * P], smr[:, u:u + 1],
                                      gtok[:, i, gc:gc + 1], ALU.mult, ALU.mult).then_inc(s_pn, 1)
                if s >= 20 and s % 16 == 4 and s < N_UNITS:
                    rr = s // 16 - 1
                    dve.wait_ge(s_oh, rr + 1)
                    dve.tensor_tensor(actL[CT + rr][:, 0:TP], PS[:, rr % 2, :], actH[CT + rr][:, 0:TP].bitcast(F32),
                                      ALU.subtract).then_inc(s_ol, 1)
            dve.wait_ge(s_oh, R)
            dve.tensor_tensor(actL[KT - 1][:, 0:TP], PS[:, 1, :], actH[KT - 1][:, 0:TP].bitcast(F32), ALU.subtract)\
                .then_inc(s_ol, 1)
            for k in range(KT):
                dve.wait_ge(s_grp, N_Z + k + 1)
                dve.wait_ge(s_sq, KT + k + 1)
                if 1 <= k < KT - 1:
                    add_square(1, k)
                dve.tensor_scalar(mixT[:, k, :].rearrange("p (a b) -> p a b", a=2), PZ[k % 2][:, :, 0:HT],
                                  vec[:, V_GPOST + k:V_GPOST + k + 1], None, ALU.mult).then_inc(s_evt, 1)
            dve.wait_ge(s_evt, KT)
            rinv(1)
            for j in range(KT + 2):
                if j < KT:
                    dve.tensor_tensor(mixT[:, j, :], mixT[:, j, :], rb[:, :], ALU.mult).then_inc(s_scaled, 1)
                k = j - 2
                if k >= 0:
                    dve.wait_ge(s_nh, KT + k + 1)
                    dve.scalar_tensor_tensor(out=actL[k], in0=xT[:, k, :], scalar=vec[:, V_GPRE2 + k:V_GPRE2 + k + 1],
                                             in1=actH[k].bitcast(F32), op0=ALU.mult, op1=ALU.subtract)\
                        .then_inc(s_nl, 1)
            dve.wait_ge(s_out, 16 * 4)
            dve.wait_ge(s_nl, 2 * KT)
            GB = 26
            for fh in range(2):
                def relu(j, c):
                    dve.wait_ge(s_grp, GB + 32 * fh + 4 * j + c + 1)
                    dve.tensor_scalar(rl[c % 2][:, :].rearrange("p (a b) -> p a b", a=2), PZ[c % 2][:, :, 0:HT],
                                      0.0, None, ALU.max).then_inc(s_evt, 1)

                def hidden_lo(j, c, hi, lo):
                    dve.wait_ge(s_hh, 16 * fh + 4 * j + c + 1)
                    dve.tensor_tensor(lo, h2[c % 2][:, :], hi.bitcast(F32), ALU.subtract).then_inc(s_hl, 1)

                if fh == 0:
                    relu(0, 0)
                    relu(0, 1)
                    for k in range(1, KT - 1):
                        add_square(2, k)
                    for c in range(4):
                        if c >= 2:
                            relu(0, c)
                        hidden_lo(0, c, hH[:, c, :], hL[:, c, :])
                with dve.Fori(1 - fh, 4) as j:
                    for c in range(4):
                        relu(j, c)
                        hidden_lo(j, c, *(h_[:, bass.ds(4 * j + c, 1), :].rearrange("p o t -> p (o t)")
                                          for h_ in (hH, hL)))
                if fh == 0:
                    dve.wait_ge(s_std, 3)
                    dve.tensor_tensor(r2[:, :], rb[:, :], rb[:, :], ALU.mult).then_inc(s_r, 1)
                    dve.wait_ge(s_r, 1)
                    dve.reciprocal(r2[:, :], r2[:, :]).then_inc(s_rinv, 1)
                    dve.wait_ge(s_rinv, 3)
                with dve.Fori(0, 4) as mp:
                    dve.wait_ge(s_evt, 24 * fh + 24)
                    for c in range(2):
                        dve.wait_ge(s_grp, GB + 32 * fh + 16 + 4 * mp + 2 + c + 1)
                        f3 = fs[:, bass.ds(2 * mp + c, 1), :].rearrange("p o (a b) -> p (o a) b", a=2)
                        if fh == 0:
                            dve.tensor_copy(f3, PZ[c % 2][:, :, 0:HT]).then_inc(s_evt, 1)
                        else:
                            dve.tensor_tensor(f3, f3, PZ[c % 2][:, :, 0:HT], ALU.add).then_inc(s_r, 1)
                            dve.wait_ge(s_r, 2 * mp + c + 2)
                            dve.tensor_tensor(f3, f3, r2[:, :].rearrange("p (a b) -> p a b", a=2), ALU.mult)\
                                .then_inc(s_evt, 1)
            dve.wait_ge(s_evt, 8 + 48)
            rinv(3)
            dve.wait_ge(s_fg, KT)
            for j in range(len(Y_DVE) + 1):
                if j < len(Y_DVE):
                    k, c = Y_DVE[j]
                    dve.tensor_tensor(fs[:, k, c], fs[:, k, c], rb[:, c], ALU.mult).then_inc(s_ym, 1)
                if j >= 1:
                    k, c = Y_DVE[j - 1]
                    dve.wait_ge(s_ym, j)
                    dve.tensor_tensor(xT[:, k, c], xT[:, k, c], fs[:, k, c], ALU.add).then_inc(s_yd, 1)

        @block.tensor
        def _(pe):
            def feed_mean(norm, dst):
                for i, (sm, n, src) in enumerate(((s_add, 6 * norm + 6, sq[0]), (s_sq, KT * (norm + 1), sq[1]))):
                    pe.wait_ge(sm, n)
                    for hf in range(2):
                        mm = pe.matmul(dst[:, hf, 0:HT], ones[:, 0, :], src[:, hf * HT:(hf + 1) * HT],
                                       start=(i == 0), stop=(i == 1))
                mm.then_inc(s_st, 1)

            def group(s, c, pz, src_h, src_l, k0=0, first=True, last=True, nk=KT):
                for hf in range(2):
                    cols = slice(hf * HT, (hf + 1) * HT)
                    for k in range(nk):
                        w = slice(k * 2 * P + c * P, k * 2 * P + (c + 1) * P)
                        for i, (W_, X_) in enumerate(((wH, src_h), (wH, src_l), (wL, src_h))):
                            mm = pe.matmul(pz[:, hf, 0:HT], W_[s][:, w], X_[k0 + k][:, cols],
                                           start=(first and k == 0 and i == 0),
                                           stop=(last and k == nk - 1 and i == 2))
                mm.then_inc(s_grp, 1)

            def first_groups(s):
                for k in range(KT):
                    pe.wait_ge(s_nl, KT + k + 1)
                    for c in range(2):
                        w = slice(k * 2 * P + c * P, k * 2 * P + (c + 1) * P)
                        for i, (W_, X_) in enumerate(((wH, actH), (wH, actL), (wL, actH))):
                            for hf in range(2):
                                mm = pe.matmul(PZ[c][:, hf, 0:HT], W_[s][:, w], X_[k][:, hf * HT:(hf + 1) * HT],
                                               start=(k == 0 and i == 0), stop=(k == KT - 1 and i == 2))
                        if k == KT - 1:
                            mm.then_inc(s_grp, 1)

            def turn(u, i):
                f = 4 * u + i
                if i == 0:
                    pe.wait_ge(s_rc[u % 4], 16 * (u // 4 + 1))
                if f >= 2:
                    pe.wait_ge(s_xl, f - 1)
                raw = rawc[u % 4][:, :].rearrange("p (g n) -> p g n", g=G)
                for jj in range(2):
                    for g in range(G):
                        jp = 2 * i + jj
                        mm = pe.transpose(PR[:, f % 2, (jj * 2 + g) * P:(jj * 2 + g + 1) * P],
                                          raw[:, g, jp * P:(jp + 1) * P], ident[:, :])
                mm.then_inc(s_xt, 1)

            def cmp_mm(u, feed=None):
                kv, pr = divmod(u, 4)
                N = 258 if pr == 0 else 256
                s = B_CK + kv
                pe.wait_ge(s_split, s + 1)
                if pr == 0:
                    pe.wait_ge(s_pec, kv + 1)
                if u >= 2:
                    pe.wait_ge(s_gelu, u - 1)
                for t in range(16):
                    if t == 9 and feed is not None:
                        feed()
                    if t % 4 == 2 and u < 7:
                        turn(u + 1, t // 4)
                    if t < 8 and t % 2 == 0:
                        pe.wait_ge(s_xl, 4 * u + t // 2 + 1)
                    w = slice(t * P, (t + 1) * P)
                    sh = t // 8
                    for i, (W_, X_) in enumerate(((wH, XH), (wH, XL), (wL, XH))):
                        mm = pe.matmul(PA[:, u % 2, 0:N], W_[s][:, w], X_[u % 2][:, t % 8, sh:sh + N],
                                       start=(t == 0 and i == 0), stop=(t == 15 and i == 2))
                mm.then_inc(s_cmm, 1)

            def cmp_out(u):
                pe.wait_ge(s_gelu, u + 1)
                if u == 0:
                    pe.wait_ge(s_misc, 48)
                if u >= 2:
                    pe.wait_ge(s_w2e, u - 1)
                h = hc[u % 2]
                for g in range(G):
                    if u < 4:
                        mm = pe.matmul(PS[g * HD:(g + 1) * HD, u % 2, 0:P], w2[:, 0, :], h[:, g * P:(g + 1) * P],
                                       start=True, stop=True)
                    else:
                        mm = pe.matmul(PS[:, u % 2, g * HD:(g + 1) * HD], h[:, g * P:(g + 1) * P], w2[:, 1, :],
                                       start=True, stop=True)
                mm.then_inc(s_w2m, 1)

            pe.wait_ge(s_vec, 32)
            for i in range(4):
                turn(0, i)
            for u in range(9):
                def feed():
                    pe.wait_ge(s_init, 6)
                    feed_mean(0, PB)

                if u >= 1:
                    cmp_mm(u - 1, feed if u == 4 else None)
                if u >= 2:
                    cmp_out(u - 2)

            def rot(z, j):
                pe.wait_ge(s_z, z + 1)
                if j == 0:
                    pe.wait_ge(s_cst, 32)
                else:
                    pe.wait_ge(s_rot2, j)
                if j == 1:
                    pe.wait_ge(s_xp, 8)
                for hf in range(2):
                    mm = pe.matmul(PR[:, hf, 0:HT], C(C_PERM, P), zr[z % 3][:, hf * HT:(hf + 1) * HT],
                                   start=True, stop=True)
                mm.then_inc(s_rot, 1)

            def turn_tok(c):
                if ROPE[c]:
                    j = sum(ROPE[:c])
                    pe.wait_ge(s_rope, j + 1)
                    src = kf[j % 2]
                else:
                    pe.wait_ge(s_z, c + 1)
                    src = zr[c % 3]
                if c >= 1:
                    pe.wait_ge(s_tokA, c)
                    pe.wait_ge(s_tokD, c)
                for t in range(QT):
                    pe.transpose(PS[:, 0, t * P:(t + 1) * P], src[:, t * P:(t + 1) * P], ident[:, :])
                pe.transpose(PS[0:NS, 1, 0:P], src[:, TP:T], ident[:, :]).then_inc(s_tok, 1)

            pe.wait_ge(s_nl, KT)
            for n in range(N_Z):
                b, c = B_IN + n // 2, n % 2
                pe.wait_ge(s_split, SPLITS(b))
                if n == 0:
                    pe.wait_ge(s_gelu, 8)
                if 2 <= n < 10:
                    if n % 2 == 0:
                        pe.wait_ge(s_sig, (n - 2) // 2 + 1)
                    else:
                        pe.wait_ge(s_u, 3 * ((n - 2) // 2 + 1))
                elif n >= 10:
                    pe.wait_ge(s_z, n - 2 - 8 + 1)
                group(b % 2, c, PZ[n % 2], actH, actL)
                if n == 0:
                    cmp_out(7)
                z = n - 8
                if z >= 1 and ROPE[z - 1]:
                    rot(z - 1, sum(ROPE[:z - 1]))
                if z == 2:
                    pe.wait_ge(s_rope, 1)
                    pe.wait_ge(s_z, 2)
                    for kv, src in enumerate((kf[0], zr[1])):
                        mm = pe.matmul(PR[:, kv, :], swap[:, :], src[:, 0:TP], start=True, stop=True)
                    mm.then_inc(s_swp, 1)
                if 2 <= z < 8:
                    turn_tok(z - 2)
            pe.wait_ge(s_wgs, 2)
            pe.wait_ge(s_z, 9)
            for hf in range(2):
                for k in range(KT):
                    for i, (W_, X_) in enumerate(((wgH, actH), (wgH, actL), (wgL, actH))):
                        mm = pe.matmul(PA[0:24, hf, 0:HT], W_[:, k * 24:(k + 1) * 24],
                                       X_[k][:, hf * HT:(hf + 1) * HT],
                                       start=(k == 0 and i == 0), stop=(k == KT - 1 and i == 2))
            mm.then_inc(s_gmm, 1)
            rot(9, 6)
            pe.wait_ge(s_gt, 1)
            pe.wait_ge(s_tokA, 6)
            pe.wait_ge(s_tokD, 6)
            for t in range(QT):
                pe.transpose(PS[:, 0, t * 24:(t + 1) * 24], gT[:, t * P:(t + 1) * P], ident[0:24, 0:24])
            pe.transpose(PS[0:NS, 0, 96:120], gT[:, TP:T], ident[0:24, 0:24]).then_inc(s_gtt, 1)

            pe.wait_ge(s_rope, 7)
            for kv in range(2):
                s = (B_PK + kv) % 2
                pe.wait_ge(s_raw[s], 16 * ((B_PK + kv) // 2 + 1))
                pe.wait_ge(s_xp, 8)
                for t in range(16):
                    sh = t // 8
                    mm = pe.matmul(PA[:, kv, 0:P], wraw[s][:, t * P:(t + 1) * P], XP[:, kv, t % 8, sh:sh + P],
                                   start=(t == 0), stop=(t == 15))
                mm.then_inc(s_pcm, 1)
            pe.wait_ge(s_gtk, 2)
            pe.wait_ge(s_gelu, 9)
            for g in range(G):
                mm = pe.matmul(PS[g * HD:(g + 1) * HD, 0, g * 32:(g + 1) * 32], w2[:, 0, :],
                               hcp[:, 0, g * 32:(g + 1) * 32], start=True, stop=True)
            mm.then_inc(s_w2m, 1)
            pe.wait_ge(s_gelu, 10)
            for rr in range(2):
                mm = pe.matmul(PS[rr * 64:(rr + 1) * 64, 1, 0:HD], hcp[:, 1, 0:64], w2[:, 1, :],
                               start=True, stop=True)
            mm.then_inc(s_w2m, 1)
            def turn_keys(b):
                pe.wait_ge(s_dec[b % 2], 16 * (b // 2 + 1))
                pe.wait_ge(s_win[b % 2], 16 * (b // 2 + 1))
                for q in range(2):
                    if b >= 1:
                        pe.wait_ge(s_ktA if q == 0 else s_ktD, 2 * b - 1 if q == 0 else b)
                    for r in range(4):
                        mm = pe.transpose(PR[:, q, r * P:(r + 1) * P], rks[b % 2][:, (4 * q + r) * P:(4 * q + r + 1) * P],
                                          ident[:, :])
                    mm.then_inc(s_kt, 1)
                if b >= 1:
                    pe.wait_ge(s_ktA, 2 * b)
                for r in range(4):
                    mm = pe.transpose(PS[:, 0, r * P:(r + 1) * P], rkw[b % 2][:, r * P:(r + 1) * P], ident[:, :])
                mm.then_inc(s_kt, 1)

            def key_scores(b):
                pe.wait_ge(s_ktA, 2 * b + 2)
                pe.wait_ge(s_ktD, b + 1)
                q = Qpad[:, b * 64:(b + 1) * 64]
                f, l = b == 0, b == NS - 1
                pe.matmul(PA[0:64, 0, :], q, KTb[b % 2][:, 0:512], start=f, stop=l)
                pe.matmul(PA[0:64, 1, :], q, KTb[b % 2][:, 512:1024], start=f, stop=l)
                pe.matmul(PB[0:64, 0, :], q, KTb[b % 2][:, 1024:1536], start=f, stop=l).then_inc(s_sc, 1)

            pe.wait_ge(s_q, 6)
            pe.wait_ge(s_w2e, 14)
            for b in range(NS):
                mm = pe.matmul(PB[0:64, 1, 0:64], Qpad[:, b * 64:(b + 1) * 64], kcS[:, b * 64:(b + 1) * 64],
                               start=(b == 0), stop=(b == NS - 1))
            mm.then_inc(s_scc, 1)
            pe.wait_ge(s_kzc, 6)
            for bi in range(2):
                pe.matmul(PS[0:64, 1, bi * 8:bi * 8 + 8], Qc[:, :], knew[:, bi, :], start=True, stop=True)
            pe.matmul(PS[0:64, 1, 16:40], C(C_EB, 64, 0, 8), gtok[0:8, QT, :], start=True, stop=True)\
                .then_inc(s_scc, 1)
            for b in range(NS + 1):
                if b < NS:
                    turn_keys(b)
                if b >= 1:
                    key_scores(b - 1)
                if b == 1:
                    pe.wait_ge(s_dV, DV_PN)
                    pe.transpose(PS[0:64, 1, 64:128], Sc0[:, :], ident[0:64, 0:64]).then_inc(s_dP, 1)
                if b == 2:
                    pe.wait_ge(s_dV, DV_PN + 1)
                    pe.matmul(PS[0:64, 1, 128:144], pnT[:, :], C(C_OV, 16, 0, 64), start=True, stop=True)\
                        .then_inc(s_dP, 1)
                if b == 3:
                    pe.wait_ge(s_dV, DV_PN + 2)
                    pe.matmul(PS[0:64, 1, 144:160], C(C_RS, 64, 0, 64), im1[:, :], start=True, stop=True)\
                        .then_inc(s_dP, 1)
            pe.wait_ge(s_dV, DV_PS)
            for r in range(8):
                mm = pe.transpose(PR[:, 0, r * 64:(r + 1) * 64], Ss[:, r * P:(r + 1) * P], ident[0:64, 0:64])
            mm.then_inc(s_dP, 1)
            pe.wait_ge(s_dV, DV_P)
            for r in range(4):
                pe.transpose(PR[:, 1, r * 64:(r + 1) * 64], Sw[:, r * P:(r + 1) * P], ident[0:64, 0:64])
            pe.transpose(PR[:, 1, 256:320], Pd[:, :, :].rearrange("p a n -> p (a n)"), ident[0:64, 0:64])
            for bi in range(2):
                mm = pe.transpose(PS[0:8, 0, bi * 64:(bi + 1) * 64], nw[:, bi, :], ident[0:64, 0:64])
            mm.then_inc(s_dP, 1)
            pe.wait_ge(s_dA, 5)
            pe.wait_ge(s_dV, DV_P + 2)
            for i in range(QT):
                for r in range(R):
                    mm = pe.matmul(PR[:, i // 2, (i % 2) * 256 + r * 64:(i % 2) * 256 + (r + 1) * 64],
                                   qT[:, r, i * P:(i + 1) * P], kcBD[:, :], start=True, stop=True)
            mm.then_inc(s_cS, 1)
            for b in range(NS):
                i = NS + b
                pe.wait_ge(s_dec[i % 2], 16 * (i // 2 + 1))
                pe.wait_ge(s_win[i % 2], 16 * (i // 2 + 1))
                o = PA[0:8, b // 4, (b % 4) * P:(b % 4 + 1) * P]
                for r in range(8):
                    pe.matmul(o, PT[:, r * 64 + b * 8:r * 64 + b * 8 + 8], rks[i % 2][:, r * P:(r + 1) * P],
                              start=(r == 0), stop=False)
                for r in range(4):
                    pe.matmul(o, PT[:, 512 + r * 64 + b * 8:512 + r * 64 + b * 8 + 8],
                              rkw[i % 2][:, r * P:(r + 1) * P], start=False, stop=False)
                pe.matmul(o, PT[:, 768 + b * 8:768 + b * 8 + 8], vcS[:, b // 2, :], start=False, stop=False)
                for bi in range(2):
                    mm = pe.matmul(o, PTn[0:8, bi * 64 + b * 8:bi * 64 + b * 8 + 8], vtok[0:8, bi, QT, :],
                                   start=False, stop=(bi == 1))
                mm.then_inc(s_dpv, 1)
                if b == 2:
                    pe.wait_ge(s_tv, TV_SUM)
                    for hf in range(2):
                        mm = pe.matmul(PB[:, hf, 0:HT], ones[:, 1, :], ysm[:, hf * HT:(hf + 1) * HT],
                                       start=True, stop=True)
                    mm.then_inc(s_tp, 1)
                if b == 4:
                    pe.wait_ge(s_tv, TV_XC - 1 + CT)
                    for t in range(CT):
                        pe.wait_ge(s_ta, t + 1)
                        for hf in range(2):
                            mm = pe.matmul(PB[:, hf, 0:HT], ones[:, 1, :], sq[t % 2][:, hf * HT:(hf + 1) * HT],
                                           start=(t == 0), stop=(t == CT - 1))
                        mm.then_inc(s_tp, 1)
                if b == 5:
                    pe.wait_ge(s_cV, PC_DONE)
                    for i in range(QT):
                        for rp in range(2):
                            c = (i % 2) * 256 + rp * P
                            mm = pe.transpose(PR[:, i // 2, c:c + P], Pc[:, i * 256 + rp * P:i * 256 + (rp + 1) * P],
                                              ident[:, :])
                    mm.then_inc(s_cT, 1)
            pe.wait_ge(s_dA, 6)
            for b in range(NS):
                mm = pe.transpose(PS[:, 0, b * 8:(b + 1) * 8], od[:, b * P:(b + 1) * P], ident[0:8, 0:8])
            mm.then_inc(s_dP, 1)
            pe.wait_ge(s_cE, 1)
            pe.wait_ge(s_ta, CT + 1)
            pe.wait_ge(s_initd, 2)
            pe.wait_ge(s_dV, DV_P + 4)
            for s in range(N_UNITS + LAG + 1):
                if s < N_UNITS:
                    r, g, br, i = UNITS[s]
                    n = (i + 1) * P
                    if s >= 4:
                        pe.wait_ge(s_ex, s - 3)
                    dst = PZ[s // 2 % 2][:, s % 2, 0:n]
                    pe.matmul(dst, qT[:, r, i * P:(i + 1) * P], kz[:, br, g, 0:n], start=True, stop=True)
                    pe.matmul(dst[:, i * P:n], identb[:, :], maskb[:, :], start=False, stop=True,
                              skip_group_check=True).then_inc(s_S, 1)
                if LAG <= s < N_UNITS + LAG:
                    u = s - LAG
                    r, g, br, i = UNITS[u]
                    pe.wait_ge(s_pn, u + 1)
                    if u >= 2:
                        pe.wait_ge(s_ev, u - 1)
                    for j in range(i + 1):
                        mm = pe.transpose(PR[:, u % 2, j * P:(j + 1) * P], Pb[u % 4][:, j * P:(j + 1) * P], ident[:, :])
                    mm.then_inc(s_T, 1)
                if s > LAG:
                    u = s - LAG - 1
                    r, g, br, i = UNITS[u]
                    if u % 16 == 0:
                        if r >= 2:
                            pe.wait_ge(s_ol, r - 1)
                        pe.matmul(PS[:, r % 2, :], vcBD[:, r % 2, :], PcT[:, r // 2, :], start=True, stop=False,
                                  skip_group_check=True)
                    pe.wait_ge(s_ev, u + 1)
                    for j in range(i + 1):
                        mm = pe.matmul(PS[g * HD:(g + 1) * HD, r % 2, i * P:(i + 1) * P],
                                       vtok[:, br, j, g * HD:(g + 1) * HD], PTb[u % 2][:, j * P:(j + 1) * P],
                                       start=False, stop=(j == i), skip_group_check=True)
                    mm.then_inc(s_pv, 1)
            pe.wait_ge(s_tv, TV_NRM - 1 + 2 * CT)
            pe.wait_ge(s_ol, R)
            pe.wait_ge(s_ex, N_UNITS)
            for k in range(KT):
                b = B_OUT + k // 2
                pe.wait_ge(s_split, SPLITS(b))
                if k >= 2:
                    pe.wait_ge(s_evt, k - 1)
                group(b % 2, k % 2, PZ[k % 2], actH, actL)
            feed_mean(1, PS)
            pe.wait_ge(s_evt, KT)
            hHk, hLk = ([h_[:, k, :] for k in range(16)] for h_ in (hH, hL))
            for fh in range(2):
                for q in range(2):
                    pe.wait_ge(s_split, SPLITS(B_FFN) - 1 + 16 * fh + q + 1)
                    if fh == 0 and q == 0:
                        first_groups(B_FFN % 2)
                    else:
                        for c in range(2):
                            pe.wait_ge(s_evt, 24 * fh + 2 * q + c + 7)
                            group((B_FFN + q) % 2, c, PZ[c], actH, actL)
                            if fh == 0 and c == 0:
                                feed_mean(2, PS)
                with pe.Fori(1, 4) as j:
                    for q in range(2):
                        pe.wait_ge(s_split, SPLITS(B_FFN) - 1 + 16 * fh + 2 * j + q + 1)
                        for c in range(2):
                            pe.wait_ge(s_evt, 24 * fh + 4 * j + 2 * q + c + 7)
                            group((B_FFN + q) % 2, c, PZ[c], actH, actL)
                with pe.Fori(0, 4) as mp:
                    for q in range(2):
                        s = (B_FFN + q) % 2
                        pe.wait_ge(s_split, SPLITS(B_FFN) - 1 + 16 * fh + 8 + 2 * mp + q + 1)
                        pe.wait_ge(s_hl, 16 * fh + 8 * q + 8)
                        for c in range(2):
                            if q == 0:
                                pe.wait_ge(s_evt, 24 * fh + 16 + 2 * mp + c + 7)
                            group(s, c, PZ[c], hHk, hLk, q * KT, q == 0, q == 1)
            pe.wait_ge(s_std, 3)
            for i, (sm, n, src) in enumerate(((s_acc, 5, rl0), (s_fsq, 7, sq[0]), (s_fsq, 8, sq[1]))):
                pe.wait_ge(sm, n)
                for hf in range(2):
                    mm = pe.matmul(PS[:, hf, 0:HT], ones[:, 0, :], src[:, hf * HT:(hf + 1) * HT],
                                   start=(i == 0), stop=(i == 2))
            mm.then_inc(s_st, 1)


def kernel(**inputs):
    import concourse.bacc as bacc
    from concourse.bass_utils import run_bass_kernel_spmd

    x = {n: np.asarray(v) for n, v in inputs.items()}
    f32 = np.float32

    def tiles(w):
        return w.reshape(-1, P, w.shape[-1]).transpose(1, 0, 2)

    def fm(v):
        return v.reshape(-1, P).T

    def chunks(n):
        return x[n].reshape(-1, STRIDE, G, HD).transpose(0, 2, 1, 3).reshape(-1, STRIDE * P)

    w_in, w_out, w_up, w_down = (x[n][0] for n in ("w_in", "w_out", "w_up", "w_down"))
    blocks = []
    w1s = [x[n][0].reshape(STRIDE, 2, HD, 2 * HD).transpose(1, 2, 0, 3).reshape(P, BW)
           for n in ("cmp_k_w1", "cmp_v_w1")]
    for t in range(CT):
        blocks.append(np.concatenate([w_in[:, CH + P * t:CH + P * (t + 1)], w_in[:, P * t:P * (t + 1)]], 1))
    c1 = 2 * CH + NH * HD
    for t in range(3):
        blocks.append(w_in[:, c1 + 2 * P * t:c1 + 2 * P * (t + 1)])
    q_w = w_in[:, 2 * CH:c1].reshape(D, G, R, HD).transpose(0, 2, 1, 3).reshape(D, NH * HD)
    blocks += [q_w[:, 0:2 * P], q_w[:, 2 * P:]]
    blocks = w1s + [tiles(b).reshape(P, BW) for b in blocks] + w1s
    att = w_out[CH:].reshape(G, R, HD, D).transpose(1, 0, 2, 3).reshape(NH * HD, D)
    w_o = np.concatenate([w_out[:CH], att], 0)
    blocks += [tiles(w_o[:, 2 * P * m:2 * P * (m + 1)]).reshape(P, BW) for m in range(4)]
    for fh in range(2):
        for b in range(8):
            c = fh * 2048 + 2 * P * b
            blocks.append(tiles(w_up[:, c:c + 2 * P]).reshape(P, BW))
        for mp in range(4):
            for q in range(2):
                r = fh * 2048 + q * 1024
                blocks.append(tiles(w_down[r:r + 1024, 2 * P * mp:2 * P * (mp + 1)]).reshape(P, BW))
    wblk = np.stack(blocks)

    pe_ = [x[n][0].reshape(STRIDE, 2, HD).transpose(1, 2, 0).reshape(P, STRIDE) for n in ("cmp_k_pe", "cmp_v_pe")]
    vecs = np.concatenate(
        [fm(x["g_pre_mix"][0]), fm(x["conv_b"][0]), fm(x["conv_ln_g"][0]), fm(x["conv_ln_b"][0]),
         fm(x["g_post_mix"][0]), fm(x["g_pre_ffn"][0]), fm(x["g_post_ffn"][0]),
         x["cmp_k_b1"][0][:, None], x["cmp_v_b1"][0][:, None],
         x["conv_w"][0].reshape(TAPS, CT, P).transpose(2, 1, 0).reshape(P, CT * TAPS)] + pe_, 1)
    wgate = tiles(w_in[:, c1 + 6 * P:]).reshape(P, KT * 24)

    p = np.arange(P)
    pos = np.concatenate([np.arange(TP), np.full(NS, PAST)]).astype(f32)
    inv = np.power(f32(500000.0), -np.arange(8, dtype=f32) * f32(2.0) / f32(16)).astype(f32)
    ang = (pos[None, :] * inv[:, None]).astype(f32)
    cos, sin, perm = np.ones((P, T), f32), np.zeros((P, T), f32), np.zeros((P, P), f32)
    for g in range(G):
        for d in range(16):
            cos[g * HD + d], sin[g * HD + d] = np.cos(ang[d % 8]), np.sin(ang[d % 8])
        for d in range(8):
            perm[g * HD + d + 8, g * HD + d] = -1
            perm[g * HD + d, g * HD + d + 8] = 1
    mask = np.where(p[None, :] <= p[:, None], 0, NEG).astype(f32)
    qpos = (np.arange(QT)[None, :] * P + p[:, None])[:, :, None]
    n32 = np.arange(NCH_P)[None, None, :]
    vis = ((STRIDE * n32 + 31 <= qpos) & (n32 < NCH_P - 1)).reshape(P, QT * NCH_P)
    r64 = np.arange(64)
    i_, j_ = np.arange(NCH_S)[:, None], np.arange(NBLK)[None, :]
    ov = np.maximum(np.minimum(i_ * 16 + 32, (j_ + 1) * 64) - np.maximum(i_ * 16, j_ * 64), 0) // 16 * (i_ < 63)

    def rows(m):
        return np.concatenate([m, np.zeros((P - m.shape[0], m.shape[1]))], 0).astype(f32)

    same = (r64[:, None] // 4 == r64[None, :] // 4)
    consts = np.concatenate(
        [np.eye(P), perm, cos, sin, mask, vis, np.where(vis, 0, NEG),
         rows(r64[:, None] % 8 == np.arange(24)[None, :] % 8), rows(r64[:, None] // 8 == np.arange(8)[None, :]),
         rows(same), rows(np.arange(8)[:, None] == r64[None, :] // 8), rows(ov),
         rows(np.tile(np.arange(1, 15), (64, 1))),
         np.stack([p % 8, p % 16, p // 8 % 2 == 0, p // 8 % 2 == 1], 1)], 1).astype(f32)
    assert consts.shape == (P, N_C) and vecs.shape == (P, N_VEC)

    xs = np.concatenate([x["x_prompt"][0], x["x_sample"][:, 0]], 0)
    us0 = np.concatenate([x["cache_conv"][0], np.zeros((NS, 1, CH), f32)], 1)
    us0 = us0.reshape(NS, TAPS, CT, P).transpose(3, 2, 0, 1)
    pt = x["page_table"]
    pt_rep = np.stack([pt[2 * pr + p // 64, (p % 64) // 8] for pr in range(4)]
                      + [pt[b, p // STRIDE] for b in range(NS)], 1)
    ins = {"wblk": wblk, "wgate": wgate, "vecs": vecs, "consts": consts, "x_fm": tiles(xs.T), "us0": us0,
           "w2": np.stack([x["cmp_k_w2"][0], x["cmp_v_w2"][0]], 1), "pt_rep": pt_rep,
           "pool_kc": chunks("cache_k_cmp"), "pool_vc": chunks("cache_v_cmp"),
           "pool_ks": x["cache_k_sel"].reshape(-1, 1024), "pool_vs": x["cache_v_sel"].reshape(-1, 1024),
           "cwk": x["cache_k_win"].reshape(NS, WIN, P), "cwv": x["cache_v_win"].reshape(NS, WIN, P)}
    outs = {"y_fm": (P, KT, T), "pconv": (P, CT, TAPS - 1), "sconv": (P, CT, NS, TAPS - 1)}
    for c in range(6):
        outs[f"p_rows{c}"] = (TP, P)
    for c in range(4):
        outs[f"s_rows{c}"] = (NS, P)
    for kv in range(2):
        outs[f"s_win{kv}"] = (NS, WIN, P)

    nc = bacc.Bacc("TRN2", target_bir_lowering=False, num_devices=1)
    arrays, A = {}, {}
    for name, v in ins.items():
        v = np.ascontiguousarray(v)
        arrays[name + "_dram"] = v
        A[name] = nc.dram_tensor(name + "_dram", v.shape, mybir.dt.from_np(v.dtype), kind="ExternalInput").ap()
    for name, shape in outs.items():
        A[name] = nc.dram_tensor(name + "_dram", shape, F32, kind="ExternalOutput").ap()
    for base, n in (("p_rows", 6), ("s_rows", 4), ("s_win", 2)):
        A[base] = [A[f"{base}{i}"] for i in range(n)]
    A["win_rows"] = [A["cwk"], A["cwv"]]
    A["win_k"], A["win_v"] = (A[n].rearrange("b (p r) d -> b p (r d)", r=4) for n in ("cwk", "cwv"))
    hymba_step(nc, A)
    res = run_bass_kernel_spmd(nc, [arrays], core_ids=[0]).results[0]
    res = {name: res[name + "_dram"] for name in outs}

    y = res["y_fm"].transpose(2, 1, 0).reshape(T, D)
    p_new = [res[f"p_rows{c}"].reshape(1, 1, TP, G, HD) for c in range(6)]
    s_new = [res[f"s_rows{c}"].reshape(1, NS, 1, G, HD) for c in range(4)]
    s_win = [res[f"s_win{kv}"].reshape(1, NS, WIN, G, HD) for kv in range(2)]
    pconv = res["pconv"].transpose(2, 1, 0).reshape(1, 1, TAPS - 1, CH)
    sconv = res["sconv"].transpose(2, 3, 1, 0).reshape(1, NS, TAPS - 1, CH)
    return (y[None, :TP], y[TP:, None], *p_new, pconv, *s_new, *s_win, sconv)
```
